# Optimizing a Trainium2 kernel written in Bass

```python
import math
import jax
import jax.numpy as jnp
from jax import lax
import numpy as np

D_MODEL = 1024
BATCH = 1
SEQ = 128
DEPTH = 4
DEC_BATCH = 1
DEC_SEQ = 128
PAST_LEN = 128

GRID_W = 64
N_MIXERS = 4
N_HYENA = (DEPTH + 3) // 4
N_GLA = (DEPTH + 2) // 4
N_FNET = (DEPTH + 1) // 4
N_POOL = DEPTH // 4

HY_ORDER = 2
HY_BANDS = 8
HY_EMB = 1 + 2 * HY_BANDS
HY_FILTER_HIDDEN = 64
HY_FAST_DECAY = 0.3
HY_SLOW_DECAY = 1.5
HY_DECAY_TARGET = 1e-2

GLA_HEADS = 4
GLA_DK = D_MODEL // 2 // GLA_HEADS
GLA_DV = D_MODEL // GLA_HEADS
GLA_GATE_RANK = 16
GLA_GATE_NORMALIZER = 16.0
GLA_CHUNK = 64

FNET_GROUPS = 4
POOL_WINDOWS = (2, 4, 8, 16)
POOL_GROUP = D_MODEL // len(POOL_WINDOWS)

MOE_GROUPS = 4
MOE_PER_GROUP = 4
MOE_EXPERTS = MOE_GROUPS * MOE_PER_GROUP
MOE_HIDDEN = D_MODEL // 2
NORM_EPS = 1e-6

kernel_name = 'hybrid_diffusion_trunk_step'

def rmsnorm(x, g):
    xf = x.astype(jnp.float32)
    y = xf * lax.rsqrt(jnp.mean(xf * xf, axis=-1, keepdims=True) + NORM_EPS)
    return (y * g.astype(jnp.float32)).astype(x.dtype)

def short_conv3(u, w, b):
    up = jnp.pad(u, ((0, 0), (1, 1), (0, 0)))
    return up[:, :-2] * w[0] + up[:, 1:-1] * w[1] + up[:, 2:] * w[2] + b

def hyena_filters(L, w1, b1, freq, w2, b2, w3):
    pos = jnp.arange(L, dtype=jnp.float32)
    bands = jnp.linspace(1e-4, HY_BANDS - 1, HY_BANDS, dtype=jnp.float32)
    ang = (2.0 * math.pi * pos / L)[:, None] * bands[None, :]
    z = jnp.concatenate([(pos / L)[:, None], jnp.cos(ang), -jnp.sin(ang)], axis=-1)
    f = jnp.sin(freq * (z @ w1 + b1))
    f = jnp.sin(freq * (f @ w2 + b2))
    f = (f @ w3).astype(jnp.float32).reshape(L, 2, HY_ORDER, D_MODEL)
    t_lin = jnp.linspace(0.0, 1.0, L, dtype=jnp.float32)[:, None]
    max_decay = math.log(HY_DECAY_TARGET) / HY_FAST_DECAY
    min_decay = math.log(HY_DECAY_TARGET) / HY_SLOW_DECAY
    deltas = jnp.linspace(min_decay, max_decay, D_MODEL, dtype=jnp.float32)
    window = jnp.exp(-t_lin * jnp.abs(deltas)[None, :])
    f = f * window[:, None, None, :]
    return f[:, 0], f[:, 1]

def two_sided_filter(kf, kb):
    return jnp.concatenate([kf, jnp.zeros_like(kf[:1]), kb[:0:-1]], axis=0)

def fft_long_conv(z, kf_hat, skip):
    L = z.shape[1]
    zh = jnp.fft.rfft(z, n=2 * L, axis=1)
    y = jnp.fft.irfft(zh * kf_hat[None], n=2 * L, axis=1)[:, :L]
    return y + z * skip

def hyena_mixer(h, w_in, b_in, conv_w, conv_b, f_w1, f_b1, f_freq, f_w2, f_b2, f_w3, skip, w_out, b_out):
    L = h.shape[1]
    u = short_conv3(h @ w_in + b_in, conv_w, conv_b).astype(jnp.float32)
    v, x1, x2 = jnp.split(u, 3, axis=-1)
    kf, kb = hyena_filters(L, f_w1, f_b1, f_freq, f_w2, f_b2, f_w3)
    k_hat = jnp.fft.rfft(two_sided_filter(kf, kb), axis=0)
    z = x1 * fft_long_conv(v, k_hat[:, 0], skip[0])
    z = x2 * fft_long_conv(z, k_hat[:, 1], skip[1])
    return z.astype(h.dtype) @ w_out + b_out

def gla_chunked(q, k, v, gk, s0):
    B, L, H, DK = q.shape
    DV = v.shape[-1]
    n = L // GLA_CHUNK

    def chunks(a):
        return a.reshape(B, n, GLA_CHUNK, H, a.shape[-1]).transpose(0, 3, 1, 2, 4)

    q, k, v, gk = chunks(q), chunks(k), chunks(v), chunks(gk)
    b = jnp.cumsum(gk, axis=3)
    b_last = b[:, :, :, -1:]
    qe = q * jnp.exp(b)
    ke = k * jnp.exp(-b)
    kd = k * jnp.exp(b_last - b)
    lower = jnp.tril(jnp.ones((GLA_CHUNK, GLA_CHUNK), dtype=bool))
    scores = jnp.where(lower, jnp.einsum('bhncd,bhnsd->bhncs', qe, ke), 0.0)
    o_intra = jnp.einsum('bhncs,bhnse->bhnce', scores, v)
    upd = jnp.einsum('bhncd,bhnce->nbhde', kd, v)
    dec = jnp.exp(b_last[:, :, :, 0]).transpose(2, 0, 1, 3)

    def step(s, inp):
        d, u = inp
        return d[..., None] * s + u, s

    s_final, s_prev = lax.scan(step, s0.astype(jnp.float32), (dec, upd))
    o_inter = jnp.einsum('bhncd,nbhde->bhnce', qe, s_prev)
    o = (o_intra + o_inter).transpose(0, 2, 3, 1, 4).reshape(B, L, H, DV)
    return o, s_final

def gla_mixer(h, s0, w_q, w_k, w_v, w_g, w_gk1, w_gk2, b_gk, norm_g, w_o):
    B, L, _ = h.shape
    f32 = jnp.float32
    q = (h @ w_q).astype(f32).reshape(B, L, GLA_HEADS, GLA_DK) * GLA_DK ** -0.5
    k = (h @ w_k).astype(f32).reshape(B, L, GLA_HEADS, GLA_DK)
    v = (h @ w_v).astype(f32).reshape(B, L, GLA_HEADS, GLA_DV)
    g = jax.nn.silu((h @ w_g).astype(f32)).reshape(B, L, GLA_HEADS, GLA_DV)
    gk_f = jax.nn.log_sigmoid(((h @ w_gk1[0]) @ w_gk2[0] + b_gk[0]).astype(f32)) / GLA_GATE_NORMALIZER
    gk_b = jax.nn.log_sigmoid(((h @ w_gk1[1]) @ w_gk2[1] + b_gk[1]).astype(f32)) / GLA_GATE_NORMALIZER
    gk_f = gk_f.reshape(B, L, GLA_HEADS, GLA_DK)
    gk_b = gk_b.reshape(B, L, GLA_HEADS, GLA_DK)
    o_f, s_f = gla_chunked(q, k, v, gk_f, s0[:, 0])
    o_b, s_b = gla_chunked(q[:, ::-1], k[:, ::-1], v[:, ::-1], gk_b[:, ::-1], s0[:, 1])
    o = o_f + o_b[:, ::-1]
    o = rmsnorm(o, norm_g) * g
    y = o.reshape(B, L, GLA_HEADS * GLA_DV).astype(h.dtype) @ w_o
    return y, jnp.stack([s_f, s_b], axis=1)

def fnet_mixer(h, w_out, b_out):
    B, L, D = h.shape
    hg = h.astype(jnp.float32).reshape(B, L, FNET_GROUPS, D // FNET_GROUPS)
    mixed = jnp.fft.fftn(hg, axes=(1, 3), norm='ortho').real
    return mixed.reshape(B, L, D).astype(h.dtype) @ w_out + b_out

def window_mean(x, axis, k):
    L = x.shape[axis]
    lo = k // 2
    hi = k - lo - 1
    pad = [(0, 0)] * x.ndim
    pad[axis] = (1, 0)
    cs = jnp.pad(jnp.cumsum(x, axis=axis), pad)
    t = jnp.arange(L)
    end = jnp.minimum(t + hi + 1, L)
    start = jnp.maximum(t - lo, 0)
    s = jnp.take(cs, end, axis=axis) - jnp.take(cs, start, axis=axis)
    shape = [1] * x.ndim
    shape[axis] = L
    return s / (end - start).astype(x.dtype).reshape(shape)

def pool_mixer(h, grid_rows, w, b, scale):
    B, L, D = h.shape
    hf = h.astype(jnp.float32)
    means = []
    for gi, k in enumerate(POOL_WINDOWS):
        hg = hf[..., gi * POOL_GROUP:(gi + 1) * POOL_GROUP]
        if grid_rows is None:
            m = window_mean(hg, 1, k)
        else:
            g2 = hg.reshape(B, grid_rows, GRID_W, POOL_GROUP)
            m = window_mean(window_mean(g2, 1, k), 2, k).reshape(B, L, POOL_GROUP)
        means.append(m)
    d = jnp.stack(means, axis=2) - hf.reshape(B, L, len(POOL_WINDOWS), POOL_GROUP)
    y = jnp.einsum('blgc,gce->blge', d, w).reshape(B, L, D) + b
    return (y * scale).astype(h.dtype)

def hier_moe(h, w_rg, w_re, w1, w3, w2):
    B, L, D = h.shape
    xt = h.reshape(B * L, D)
    pg = jax.nn.softmax((xt @ w_rg).astype(jnp.float32), axis=-1)
    p_grp, g_idx = lax.top_k(pg, 1)
    le = (xt @ w_re).astype(jnp.float32).reshape(-1, MOE_GROUPS, MOE_PER_GROUP)
    le = jnp.take_along_axis(le, g_idx[:, :, None], axis=1)[:, 0]
    pe_top, e_idx = lax.top_k(jax.nn.softmax(le, axis=-1), 2)
    pe_top = pe_top / jnp.sum(pe_top, axis=-1, keepdims=True)
    expert = g_idx * MOE_PER_GROUP + e_idx
    weight = p_grp * pe_top
    combine = jnp.sum(jax.nn.one_hot(expert, MOE_EXPERTS, dtype=jnp.float32) * weight[..., None], axis=1)
    hid = jax.nn.silu(jnp.einsum('nd,xdf->nxf', xt, w1)) * jnp.einsum('nd,xdf->nxf', xt, w3)
    y = jnp.einsum('nxf,xfd->nd', hid * combine[..., None].astype(hid.dtype), w2)
    return y.reshape(B, L, D)

def trunk(x, cond, grid_rows, gla_s0, prm):
    states = []
    for i in range(DEPTH):
        mod = (jax.nn.silu(cond) @ prm['w_ada'][i] + prm['b_ada'][i])[:, None, :]
        sh1, sc1, g1, sh2, sc2, g2 = jnp.split(mod, 6, axis=-1)
        h = rmsnorm(x, prm['norm_g'][i, 0]) * (1.0 + sc1) + sh1
        kind, j = i % N_MIXERS, i // N_MIXERS
        if kind == 0:
            y = hyena_mixer(h, prm['hy_w_in'][j], prm['hy_b_in'][j], prm['hy_conv_w'][j], prm['hy_conv_b'][j],
                            prm['hy_f_w1'][j], prm['hy_f_b1'][j], prm['hy_f_freq'][j], prm['hy_f_w2'][j],
                            prm['hy_f_b2'][j], prm['hy_f_w3'][j], prm['hy_skip'][j], prm['hy_w_out'][j],
                            prm['hy_b_out'][j])
        elif kind == 1:
            if gla_s0 is None:
                s0 = jnp.zeros((x.shape[0], 2, GLA_HEADS, GLA_DK, GLA_DV), jnp.float32)
            else:
                s0 = gla_s0[:, j]
            y, s_fin = gla_mixer(h, s0, prm['gla_w_q'][j], prm['gla_w_k'][j], prm['gla_w_v'][j], prm['gla_w_g'][j],
                                 prm['gla_w_gk1'][j], prm['gla_w_gk2'][j], prm['gla_b_gk'][j],
                                 prm['gla_norm_g'][j], prm['gla_w_o'][j])
            if gla_s0 is None:
                states.append(s_fin)
        elif kind == 2:
            y = fnet_mixer(h, prm['fn_w_out'][j], prm['fn_b_out'][j])
        else:
            y = pool_mixer(h, grid_rows, prm['pool_w'][j], prm['pool_b'][j], prm['pool_scale'][j])
        x = x + g1 * y
        h = rmsnorm(x, prm['norm_g'][i, 1]) * (1.0 + sc2) + sh2
        x = x + g2 * hier_moe(h, prm['moe_w_rg'][i], prm['moe_w_re'][i], prm['moe_w1'][i],
                              prm['moe_w3'][i], prm['moe_w2'][i])
    return rmsnorm(x, prm['final_g']), states

def setup_inputs(seed: int = 0) -> dict:
    key = jax.random.key(seed)
    ks = iter(jax.random.split(key, 64))

    def nrm(shape, scale):
        return jax.random.normal(next(ks), shape, jnp.float32) * scale

    D = D_MODEL
    return {
        'x_prompt': nrm((BATCH, SEQ, D), 1.0),
        'x_sample': nrm((DEC_BATCH, DEC_SEQ, D), 1.0),
        'state_gla': nrm((DEC_BATCH, N_GLA, 2, GLA_HEADS, GLA_DK, GLA_DV), 1.0),
        'c': nrm((DEC_BATCH, D), 1.0),
        'c_ctx': nrm((D,), 0.5),
        'w_ada': nrm((DEPTH, D, 6 * D), 0.5 * D ** -0.5),
        'b_ada': nrm((DEPTH, 6 * D), 0.02),
        'norm_g': 1.0 + nrm((DEPTH, 2, D), 0.02),
        'hy_w_in': nrm((N_HYENA, D, 3 * D), D ** -0.5),
        'hy_b_in': nrm((N_HYENA, 3 * D), 0.02),
        'hy_conv_w': nrm((N_HYENA, 3, 3 * D), 0.5),
        'hy_conv_b': nrm((N_HYENA, 3 * D), 0.02),
        'hy_f_w1': nrm((N_HYENA, HY_EMB, HY_FILTER_HIDDEN), HY_EMB ** -0.5),
        'hy_f_b1': nrm((N_HYENA, HY_FILTER_HIDDEN), 0.02),
        'hy_f_freq': 1.0 + nrm((N_HYENA, HY_FILTER_HIDDEN), 0.02),
        'hy_f_w2': nrm((N_HYENA, HY_FILTER_HIDDEN, HY_FILTER_HIDDEN), HY_FILTER_HIDDEN ** -0.5),
        'hy_f_b2': nrm((N_HYENA, HY_FILTER_HIDDEN), 0.02),
        'hy_f_w3': nrm((N_HYENA, HY_FILTER_HIDDEN, 2 * HY_ORDER * D), 0.005),
        'hy_skip': nrm((N_HYENA, HY_ORDER, D), 0.5),
        'hy_w_out': nrm((N_HYENA, D, D), D ** -0.5),
        'hy_b_out': nrm((N_HYENA, D), 0.02),
        'gla_w_q': nrm((N_GLA, D, GLA_HEADS * GLA_DK), D ** -0.5),
        'gla_w_k': nrm((N_GLA, D, GLA_HEADS * GLA_DK), D ** -0.5),
        'gla_w_v': nrm((N_GLA, D, GLA_HEADS * GLA_DV), D ** -0.5),
        'gla_w_g': nrm((N_GLA, D, GLA_HEADS * GLA_DV), D ** -0.5),
        'gla_w_gk1': nrm((N_GLA, 2, D, GLA_GATE_RANK), D ** -0.5),
        'gla_w_gk2': nrm((N_GLA, 2, GLA_GATE_RANK, GLA_HEADS * GLA_DK), GLA_GATE_RANK ** -0.5),
        'gla_b_gk': nrm((N_GLA, 2, GLA_HEADS * GLA_DK), 0.02),
        'gla_norm_g': 1.0 + nrm((N_GLA, GLA_DV), 0.02),
        'gla_w_o': nrm((N_GLA, GLA_HEADS * GLA_DV, D), (GLA_HEADS * GLA_DV) ** -0.5),
        'fn_w_out': nrm((N_FNET, D, D), D ** -0.5),
        'fn_b_out': nrm((N_FNET, D), 0.02),
        'pool_w': nrm((N_POOL, len(POOL_WINDOWS), POOL_GROUP, POOL_GROUP), POOL_GROUP ** -0.5),
        'pool_b': nrm((N_POOL, D), 0.02),
        'pool_scale': 0.5 + nrm((N_POOL, D), 0.05),
        'moe_w_rg': nrm((DEPTH, D, MOE_GROUPS), D ** -0.5),
        'moe_w_re': nrm((DEPTH, D, MOE_EXPERTS), D ** -0.5),
        'moe_w1': nrm((DEPTH, MOE_EXPERTS, D, MOE_HIDDEN), D ** -0.5),
        'moe_w3': nrm((DEPTH, MOE_EXPERTS, D, MOE_HIDDEN), D ** -0.5),
        'moe_w2': nrm((DEPTH, MOE_EXPERTS, MOE_HIDDEN, D), MOE_HIDDEN ** -0.5),
        'final_g': 1.0 + nrm((D,), 0.02),
    }

def reference(x_prompt, x_sample, state_gla, c, c_ctx, w_ada, b_ada, norm_g,
              hy_w_in, hy_b_in, hy_conv_w, hy_conv_b, hy_f_w1, hy_f_b1, hy_f_freq, hy_f_w2, hy_f_b2,
              hy_f_w3, hy_skip, hy_w_out, hy_b_out,
              gla_w_q, gla_w_k, gla_w_v, gla_w_g, gla_w_gk1, gla_w_gk2, gla_b_gk, gla_norm_g, gla_w_o,
              fn_w_out, fn_b_out, pool_w, pool_b, pool_scale,
              moe_w_rg, moe_w_re, moe_w1, moe_w3, moe_w2, final_g):
    prm = {
        'w_ada': w_ada, 'b_ada': b_ada, 'norm_g': norm_g,
        'hy_w_in': hy_w_in, 'hy_b_in': hy_b_in, 'hy_conv_w': hy_conv_w, 'hy_conv_b': hy_conv_b,
        'hy_f_w1': hy_f_w1, 'hy_f_b1': hy_f_b1, 'hy_f_freq': hy_f_freq, 'hy_f_w2': hy_f_w2,
        'hy_f_b2': hy_f_b2, 'hy_f_w3': hy_f_w3, 'hy_skip': hy_skip, 'hy_w_out': hy_w_out, 'hy_b_out': hy_b_out,
        'gla_w_q': gla_w_q, 'gla_w_k': gla_w_k, 'gla_w_v': gla_w_v, 'gla_w_g': gla_w_g,
        'gla_w_gk1': gla_w_gk1, 'gla_w_gk2': gla_w_gk2, 'gla_b_gk': gla_b_gk, 'gla_norm_g': gla_norm_g,
        'gla_w_o': gla_w_o, 'fn_w_out': fn_w_out, 'fn_b_out': fn_b_out,
        'pool_w': pool_w, 'pool_b': pool_b, 'pool_scale': pool_scale,
        'moe_w_rg': moe_w_rg, 'moe_w_re': moe_w_re, 'moe_w1': moe_w1, 'moe_w3': moe_w3, 'moe_w2': moe_w2,
        'final_g': final_g,
    }
    y_prompt, ctx_states = trunk(x_prompt, c_ctx[None, :], None, None, prm)
    new_state_gla = jnp.stack(ctx_states, axis=1)
    rows = x_sample.shape[1] // GRID_W
    y_sample, _ = trunk(x_sample, c, rows, state_gla, prm)
    return (y_prompt, y_sample, new_state_gla)


_drawn_inputs = setup_inputs


def setup_inputs(seed=0):
    import zlib

    import numpy as np

    out = dict(_drawn_inputs(seed))
    spreads = {}
    factors = {'state_gla': 3.137,
     'hy_b_in': 8.0,
     'hy_conv_b': 8.0,
     'hy_f_w1': 2.944,
     'hy_f_b1': 8.0,
     'hy_f_freq': 8.0,
     'hy_f_w2': 2.924,
     'hy_f_b2': 8.0,
     'hy_f_w3': 3.222,
     'hy_b_out': 4.303,
     'gla_b_gk': 7.006,
     'gla_norm_g': 8.0,
     'fn_b_out': 7.054,
     'pool_b': 8.0,
     'pool_scale': 3.889}
    for name, (base, spread) in spreads.items():
        noise = np.random.default_rng([zlib.crc32(name.encode()), seed]).standard_normal(out[name].shape)
        drawn = base * np.exp(spread * noise) if base else spread * noise
        out[name] = jnp.asarray(drawn.astype(out[name].dtype))
    for name, factor in factors.items():
        out[name] = (out[name] * factor).astype(out[name].dtype)
    return out
```

```python
import math
from contextlib import ExitStack

import numpy as np
import concourse.bass as bass
from concourse import mybir

F32 = mybir.dt.float32
BF16 = mybir.dt.bfloat16
I32 = mybir.dt.int32
U32 = mybir.dt.uint32
ALU = mybir.AluOpType
ACT = mybir.ActivationFunctionType
AX = mybir.AxisListType

D = 1024
L = 128
G = 2
NT = G * L
P = 128
KD = D // P
LAYERS = 4
GRID_W = 64
EPS = 1e-6
HY_BANDS, HY_HID, HY_ORDER = 8, 64, 2
HY_EMB = 1 + 2 * HY_BANDS
HEADS, DK, DV, CH = 4, 128, 256, 64
WINDOWS = (2, 4, 8, 16)
EXPERTS, EGROUPS, FF = 16, 4, 512
SLOTS = 64
PAIRS = EXPERTS // 2
RING = 6
PIECE = 4096

VEC = {}


def vec_layout():
    tiles = [[("norm_g", 64), ("final_g", 8), ("c", 8), ("c_ctx", 8), ("hy_skip", 16), ("hy_b_out", 8),
              ("fn_b_out", 8), ("pool_b", 8)],
             [("b_ada01", 96), ("hy_b_in", 24), ("pool_scale", 8)],
             [("b_ada23", 96), ("hy_conv_b", 24), ("gla_b_gk", 8)],
             [("hy_conv_w", 72), ("gla_norm_g", 2), ("hy_f_b1", 1), ("hy_f_freq", 1), ("hy_f_b2", 1)]]
    return [(name, t, sum(n for _, n in tile[:i]), n) for t, tile in enumerate(tiles)
            for i, (name, n) in enumerate(tile)]


VEC = {name: t * P + r for name, t, r, _ in vec_layout()}


def constants():
    n = np.arange(L)
    f = np.arange(P)
    ang = 2 * np.pi * np.outer(n, f) / (2 * L)
    cos, sin = np.cos(ang), np.sin(ang)
    nyq = (-1.0) ** n
    fwd_re = cos.copy()
    fwd_im = -sin.copy()
    fwd_im[:, 0] = nyq
    kf_im = -sin
    kb_re = cos.copy()
    kb_re[0] = 0
    kb_im = sin.copy()
    kf_d = cos.copy()
    kf_d[:, 0] = nyq
    kb_d = kf_d.copy()
    kb_d[0] = 0
    inv_re = 2 * cos.T / (2 * L)
    inv_re[0] /= 2
    inv_im = -2 * sin.T / (2 * L)
    inv_im[0] = nyq / (2 * L)
    dft = np.concatenate([fwd_re, fwd_im, kf_im, kb_re, kb_im, kf_d, kb_d, inv_re, inv_im], axis=1)

    bands = np.linspace(1e-4, HY_BANDS - 1, HY_BANDS)
    a = (2 * np.pi * n / L)[:, None] * bands[None]
    pos = np.concatenate([(n / L)[:, None], np.cos(a), -np.sin(a)], axis=-1).T
    deltas = np.linspace(math.log(1e-2) / 1.5, math.log(1e-2) / 0.3, D)
    window = np.exp(-np.linspace(0, 1, L)[:, None] * np.abs(deltas)[None])

    c = D // 4
    ch = 2 * np.pi * np.outer(np.arange(c), np.arange(c)) / c
    cs = np.concatenate([np.cos(ch), np.sin(ch)], axis=1).reshape(2, P, 2 * c).transpose(1, 0, 2).reshape(P, -1)
    tok = 2 * np.pi * np.outer(n, n) / L
    fnet = np.concatenate([cs, np.cos(tok) / math.sqrt(L * c), -np.sin(tok) / math.sqrt(L * c)], axis=1)

    def mean(length, k):
        m = np.zeros((length, length))
        for t in range(length):
            lo, hi = max(t - k // 2, 0), min(t + k - k // 2, length)
            m[t, lo:hi] = 1.0 / (hi - lo)
        return m

    pool = []
    for g in range(G):
        for k in WINDOWS:
            m = mean(L, k) if g == 0 else np.kron(mean(L // GRID_W, k), mean(GRID_W, k))
            pool.append((m - np.eye(L)).T)
    pool = np.concatenate(pool, axis=1)

    base = np.concatenate([np.eye(P), np.triu(np.ones((P, P)), 1), np.tile(np.arange(SLOTS), (P, 1)),
                           np.tile(np.arange(4, 0, -1), (P, 1))], axis=1)
    s, t = np.arange(P)[:, None] % CH, np.arange(P)[None]
    same = (np.arange(P)[:, None] // CH) == (t // CH)
    mask = np.concatenate([same & (s <= t % CH), same & (s >= t % CH)], axis=1).astype(np.uint32)
    out = {"base": base, "dft": dft, "pos": pos, "window": window, "fnet": fnet, "pool": pool}
    return {k: v.astype(np.float32) for k, v in out.items()} | {"mask": mask}


def piece_stream(layers):
    ada = lambda i, q: [("ada", i, q, j) for j in range(4)]
    lay = [ada(0, 0) + [("w_in", c) for c in range(6)] + ada(0, 1) + ada(0, 2) + [("w_out", h) for h in range(2)],
           [("wq", 0), ("wk", 0), ("wv", 0), ("wv", 1), ("wg", 0), ("wg", 1)] + ada(1, 1) + ada(1, 2)
           + [("wo", 0), ("wo", 1)],
           ada(2, 1) + ada(2, 2) + [("fn", 0), ("fn", 1)],
           [("pool", 0)] + ada(3, 1) + ada(3, 2)]
    used, out, at = [0] * RING, [], 0
    for i in range(layers):
        for what in lay[i] + (ada(i + 1, 0) if i + 1 < layers else []):
            slot = at % RING
            out.append((what, slot, used[slot]))
            used[slot] += 1
            at += 1
        at = 0
        out.append((("moe", i), list(used), None))
        used = [u + PAIRS for u in used]
    return out


def build(nc, a, layers=LAYERS):
    stream = piece_stream(layers)
    where = {what: (slot, nth) for what, slot, nth in stream if what[0] != "moe"}
    moe_uses = {what[1]: slots for what, slots, _ in stream if what[0] == "moe"}

    ctx = ExitStack()
    sems = {}

    def s(name):
        if name not in sems:
            sems[name] = ctx.enter_context(nc.semaphore(name))
        return sems[name]

    def sb(name, shape, dt=F32):
        return ctx.enter_context(nc.sbuf_tensor(name, shape, dt))

    with ctx:
        ring = [sb(f"ring{i}", [P, PIECE]) for i in range(RING)]
        xT = sb("xT", [P, KD, G, L])
        hT = sb("hT", [P, KD, G, L])
        arena = sb("arena", [P, 20480])
        cm = sb("cm", [P, 1280])
        base = sb("base", [P, 324])
        ident, upper, iota, tie = base[:, 0:128], base[:, 128:256], base[:, 256:320], base[:, 320:324]
        ones = sb("ones", [P, P])
        zeros = sb("zeros", [P, P], BF16)
        vec = sb("vec", [P, 4 * P])
        mod = sb("mod", [P, 2, 48, G])
        scale = sb("scale", [P, 2, 2, KD, G])
        condT = sb("condT", [P, KD, 32])
        rstd = sb("rstd", [P, G, L])
        rows = sb("rows", [P, 512])
        small = sb("small", [P, 4])
        eps, one = small[:, 0:1], small[:, 1:2]
        rw = sb("rw", [P, KD, 20])
        mask = sb("mask", [P, 2, P], U32)
        over = sb("over", [1, 2], I32)
        bank = [ctx.enter_context(nc.psum_tensor(f"bank{i}", [P, 512], F32)) for i in range(8)]

        def ar(lo, *dims):
            n = int(np.prod(dims))
            v = arena[:, lo:lo + n]
            if len(dims) == 1:
                return v
            names = "abcd"[:len(dims)]
            return v.rearrange(f"p ({' '.join(names)}) -> p {' '.join(names)}",
                               **dict(zip(names, dims)))

        def vcol(name, lo, n=1):
            return vec[:, VEC[name] + lo:VEC[name] + lo + n]

        def piece(slot, *dims):
            names = "abc"[:len(dims)]
            return ring[slot][:, 0:int(np.prod(dims))].rearrange(
                f"p ({' '.join(names)}) -> p {' '.join(names)}", **dict(zip(names, dims)))

        def b_ada(i, lo, n):
            return vcol("b_ada01" if i < 2 else "b_ada23", 48 * (i % 2) + lo, n)

        def half(m):
            return bank[m // 2][:, (m % 2) * NT:(m % 2) * NT + NT]

        xin = ar(15360, G, D)
        vrows = ar(17408, 4, P)
        w3f = ar(6144, 4096)
        kfb = ar(10240, 2, HY_ORDER, D)
        win = ar(14336, D)
        spec = ar(0, 3, HY_ORDER, D)
        uT = ar(6144, 24, G, L)
        zt = ar(12288, G, D)
        prod = ar(14336, D)
        ysp = ar(15360, 2, D)
        up = ar(17408, 4, G, L + 2)
        vskip = ar(17408, D)
        prod2 = ar(18448, D)
        fsmall = ar(18448, 8, P)
        htok = ar(0, G, D)
        xg = ar(2048, KD, P)
        sil = ar(3072, FF)
        hid = ar(3584, FF)
        hidT = ar(4096, 4, P)
        yv = ar(4608, D)
        sel = ar(5632, G, 2, SLOTS)
        selw = ar(5888, G, 2, SLOTS)
        selT = ar(6144, NT)
        comb = ar(6400, G, EXPERTS)
        memb = ar(6432, G, EXPERTS)
        rank = ar(6464, G, EXPERTS)
        lraw = ar(6496, NT)
        lg = ar(6752, G, 20)
        rt = ar(6800, 1024)
        yb = ar(14336, 4, NT)

        fnp = ar(8192, G, 4, 512)
        fnm = ar(12288, KD, G, L)
        plr = ar(8192, G, 4, 256)
        qT, kT = ar(0, HEADS, G, L), ar(1024, HEADS, G, L)
        vrow = ar(2048, G, D)
        gT = ar(4096, KD, NT)
        gx, gt = ar(6144, 1024), ar(7168, 1024)
        e1, e2 = ar(8192, 1024), ar(9216, 1024)
        qe, ke, kdT = ar(10240, HEADS, G, L), ar(11264, HEADS, G, L), ar(12288, HEADS, G, L)
        reset = ar(10240, 1024)
        kdr = ar(13312, G, HEADS, P)
        sc = ar(14336, G, HEADS, P)
        s0 = ar(15360, 2, HEADS, DV)
        s1c, s1l, s2 = ar(17408, HEADS, DV), ar(18432, HEADS, DV), ar(19456, HEADS, DV)
        oT, osq, ors = ar(8192, KD, G, L), ar(10240, KD, NT), ar(6144, HEADS, NT)
        wg1 = cm[:, 0:256].rearrange("p (k r) -> p k r", k=KD)
        gk1 = cm[:, 0:NT]
        wg2 = cm[:, 256:1280].rearrange("p (d n) -> p d n", d=2)

        def psum_tok(b, n):
            return bank[b][:, 0:n * P].rearrange("p (a b) -> p a b", a=n)

        def rtv(lo, *dims):
            n = int(np.prod(dims))
            v = rt[:, lo:lo + n]
            if len(dims) == 1:
                return v
            names = "abcd"[:len(dims)]
            return v.rearrange(f"p ({' '.join(names)}) -> p {' '.join(names)}", **dict(zip(names, dims)))

        r_gd, r_ge = rtv(0, G, 4), rtv(8, G, 4)
        r_dd, r_de = rtv(16, G), rtv(18, G)
        r_gm, r_key, r_km, r_og = rtv(20, G), rtv(24, G, 4), rtv(32, G), rtv(40, G, 4)
        r_x4 = rtv(48, G, 4, 4)
        r_le, r_m1, r_o1, r_o2 = rtv(80, G, 4), rtv(88, G), rtv(96, G, 4), rtv(104, G, 4)
        r_le2, r_m2, r_sg, r_w1, r_w2 = rtv(112, G, 4), rtv(120, G), rtv(122, G), rtv(124, G), rtv(126, G)
        r_wt, r_mt, r_rk = rtv(128, G, 4), rtv(136, G, 4), rtv(144, G, EXPERTS)
        r_mx, r_rd = rtv(176, 1), rtv(177, 4)
        route_exp = [(r_ge, r_gd), (r_de, r_dd)]

        block = ctx.enter_context(nc.Block())

        def freed(what):
            k = what[0]
            if k == "ada":
                return "ada_mm", 3 * what[1] + what[2] + 1
            if k == "w_in":
                return "win_mm", 4 * what[1] + 4
            if k in ("w_out", "wo", "fn"):
                return "res_mm", KD * {"w_out": 0, "wo": 1, "fn": 2}[k] + 4 * what[1] + 4
            if k == "pool":
                return "pool_hw", 4
            return "gla_proj", {"wq": 2, "wk": 4, "wv": 6 + 2 * what[1], "wg": 12 + 4 * what[1]}[k]

        def source(what):
            k = what[0]
            if k == "ada":
                c = 4 * what[2] + what[3]
                return a["w_ada"][what[1]][:, 512 * c:512 * c + 512].rearrange("(k p) n -> p k n", p=P), KD
            if k == "w_in":
                return a["hy_w_in"][0][:, 512 * what[1]:512 * what[1] + 512].rearrange("(k p) n -> p k n", p=P), KD
            if k == "pool":
                return a["pool_w"][0].rearrange("g (k p) e -> p (g k) e", p=P), KD
            name = {"w_out": "hy_w_out", "wo": "gla_w_o", "fn": "fn_w_out", "wq": "gla_w_q", "wk": "gla_w_k",
                    "wv": "gla_w_v", "wg": "gla_w_g"}[k]
            return a[name][0][:, 512 * what[1]:512 * what[1] + 512].rearrange("(k p) n -> p k n", p=P), KD

        expert_dram = [a["moe_w1"].rearrange("l x (k p) n -> (l x) p k n", p=P),
                       a["moe_w3"].rearrange("l x (k p) n -> (l x) p k n", p=P),
                       a["moe_w2"].rearrange("l x (k p) n -> (l x) p k n", p=P)]
        USED = ["h1_mm", "h3_mm", "y_mm"]

        def used_up(pre, kind, pairs):
            return s(pre + USED[kind]), pairs * (2 if kind == 2 else 1)

        def expert_load(sp, kind, e, first_expert, full):
            slot = 2 * kind + e
            dst = piece(slot, KD, FF) if kind < 2 else piece(slot, 4, D)
            src = expert_dram[kind][bass.ds(first_expert + e, 1)].rearrange("o p k n -> p (o k) n")
            sp.dma_start(dst, src).then_inc(s(f"{full}{slot}"), 16)

        def needed_rounds(eng, i):
            eng.wait_ge(s("rounds_known"), i + 1)
            return eng.value_load(over[0:1, 0:1], min_val=1, max_val=NT // SLOTS)

        def fb_count(eng, name):
            reg = eng.alloc_register(name)
            eng.reg_mov(reg, 0)
            return reg

        def further_rounds(eng, i, rounds, reg, one_round):
            with eng.If(rounds - 1):
                with eng.Fori(1, rounds) as _:
                    b = eng.snap(reg, min_val=0, max_val=8 * 3 * LAYERS)
                    one_round(b)
                    eng.reg_add(reg, reg, PAIRS)

        @block.sync
        def _(sp):
            reg = fb_count(sp, "sp_extra_pairs")
            last = [None] * RING
            extra = None

            def slot_free(slot):
                if last[slot]:
                    name, value = last[slot]
                    sp.wait_ge(s(name), value)
                    if name in USED:
                        sp.wait_ge(s("fb_" + name), extra * (2 if name == "y_mm" else 1))

            for what, slot, nth in stream:
                if what[0] != "moe":
                    slot_free(slot)
                    src, n = source(what)
                    sp.dma_start(piece(slot, n, 512) if what[0] != "pool" else piece(slot, n, 256), src) \
                        .then_inc(s(f"full{slot}"), 16)
                    last[slot] = freed(what)
                    continue
                i = what[1]
                for kind in range(3):
                    for e in range(2):
                        slot_free(2 * kind + e)
                        expert_load(sp, kind, e, EXPERTS * i, "full")
                with sp.Fori(1, PAIRS) as p:
                    for kind in range(3):
                        sem, v = used_up("", kind, 1)
                        sp.wait_ge(sem, (PAIRS * i + p) * v)
                        for e in range(2):
                            expert_load(sp, kind, e, EXPERTS * i + p * 2, "full")
                rounds = needed_rounds(sp, i)

                def one_round(b):
                    for kind in range(3):
                        sem, v = used_up("", kind, 1)
                        sp.wait_ge(sem, PAIRS * (i + 1) * v)
                    with sp.Fori(0, PAIRS) as p:
                        for kind in range(3):
                            sem, v = used_up("fb_", kind, 1)
                            sp.wait_ge(sem, (b + p) * v)
                            for e in range(2):
                                expert_load(sp, kind, e, EXPERTS * i + p * 2, "fb_full")

                further_rounds(sp, i, rounds, reg, one_round)
                for kind in range(3):
                    last[2 * kind] = last[2 * kind + 1] = (USED[kind], PAIRS * (i + 1) * (2 if kind == 2 else 1))
                extra = sp.snap(reg, min_val=0, max_val=8 * 3 * LAYERS)
            for g, name in enumerate(("y_prompt", "y_sample")):
                sp.wait_ge(s("out_rows"), g + 1)
                sp.dma_start(a[name][0], xin[:, g, :]).then_inc(s("stored"), 16)
            if layers > 1:
                sp.wait_ge(s("state_stored"), 32)
            sp.wait_ge(s("stored"), 32)

        mm = nc.tensor.matmul
        tr = nc.tensor.transpose

        def pe_gla(pe, arrived, ada, norm, project, residual):
            norm(2)
            pe.wait_ge(s("h_ready"), KD * 3)
            pe.wait_ge(s("cm1_loaded"), 16 * 4)
            for k in range(KD):
                last = mm(bank[4][0:32, 0:NT], wg1[:, k, :], hT[:, k].rearrange("p g t -> p (g t)"),
                          start=k == 0, stop=k == KD - 1)
            last.then_inc(s("gk1_mm"), 1)
            for w, name in enumerate(("wq", "wk")):
                slot = arrived((name, 0))
                for h in range(HEADS):
                    w8 = piece(slot, KD, 512)
                    for k in range(KD):
                        last = mm(half(4 * w + h), w8[:, k, h * P:h * P + P], hT[:, k].rearrange("p g t -> p (g t)"),
                                  start=k == 0, stop=k == KD - 1)
                    if h % 2:
                        last.then_inc(s("gla_proj"), 1)
                if w == 0:
                    gates(pe, 0)
            for h in range(2):
                slot = arrived(("wv", h))
                for g in range(G):
                    b = (2 * h + g) % 4
                    pe.wait_ge(s("qk_ready"), 1 + b)
                    for k in range(KD):
                        last = mm(bank[b][:], hT[:, k, g], piece(slot, KD, 512)[:, k, :], start=k == 0, stop=k == KD - 1)
                    last.then_inc(s("gla_proj"), 1)
            for m in range(KD):
                if m % 4 == 0:
                    slot = arrived(("wg", m // 4))
                pe.wait_ge(s("v_ready"), m + 1) if m < 4 else pe.wait_ge(s("g_ready"), m - 3)
                project(bank[m % 4][:, 0:NT], slot, m % 4, "gla_proj")
            ada(1, 1)
            pe.wait_ge(s("g_ready"), 8)
            for m in range(4):
                mm(bank[m][:], zeros[:], zeros[:, 0:1].broadcast_to([P, 512]), start=True, stop=False, skip_group_check=True)
            for d in range(2):
                if d == 1:
                    gates(pe, 1)
                    ada(1, 2)
                pe.wait_ge(s("qke_ready"), 2 * d + 2)
                for g in range(G):
                    for h in range(HEADS):
                        last = mm(bank[4 + g][:, h * P:h * P + P], ke[:, h, g], qe[:, h, g])
                    last.then_inc(s("scores_mm"), 1)
                pe.wait_ge(s("kd_ready"), d + 1)
                for g in range(G):
                    if g or d:
                        pe.wait_ge(s("kdr_ready"), 2 * d + g)
                    for h in range(HEADS):
                        last = tr(bank[6][:, h * P:h * P + P], kdT[:, h, g], ident)
                    last.then_inc(s("kd_tr"), 1)
                for g in range(G):
                    pe.wait_ge(s("sc_ready"), 2 * d + g + 1)
                    for m in range(KD):
                        mm(half(m)[:, g * L:g * L + L], vrow[:, g, m * P:m * P + P], sc[:, g, m // 2, :],
                           start=False, stop=False, skip_group_check=True)
                pe.wait_ge(s("kdr_ready"), 2 * d + 2)
                for n, (g, c) in enumerate(((1, d), (0, d), (0, 1 - d))):
                    pe.wait_ge(s("sc_ready"), 2 * d + 2) if n == 0 else pe.wait_ge(s("upd_read"), 3 * d + n)
                    for h in range(HEADS):
                        last = mm(bank[4 + h // 2][:, (h % 2) * DV:(h % 2) * DV + DV],
                                  kdr[c * CH:c * CH + CH, g, h, :], vrow[c * CH:c * CH + CH, g, h * DV:h * DV + DV])
                    last.then_inc(s("upd_mm"), 1)
                pe.wait_ge(s("s0_loaded"), 32)
                pe.wait_ge(s("upd_read"), 3 * d + 2)
                for g, c, st in ((1, d, s0[:, d]), (1, 1 - d, s1l), (0, 1 - d, s1c)):
                    for m in range(KD):
                        last = mm(half(m)[:, g * L + c * CH:g * L + c * CH + CH],
                                  st[:, m // 2, (m % 2) * P:(m % 2) * P + P], qe[:, m // 2, g, c * CH:c * CH + CH],
                                  start=False, stop=False, skip_group_check=True)
                last.then_inc(s("o_mm"), 1)
            pe.wait_ge(s("osq_ready"), 4)
            pe.wait_ge(s("upd_read"), 6)
            for h in range(HEADS):
                dst = bank[4 + h // 2][:, (h % 2) * NT:(h % 2) * NT + NT]
                for t in range(2):
                    last = mm(dst, ones[:], osq[:, 2 * h + t], start=t == 0, stop=t == 1)
            last.then_inc(s("osum_mm"), 1)
            pe.wait_ge(s("o_ready"), 1)
            residual(1, "wo", rhs=oT)

        def gates(pe, d):
            if d == 0:
                pe.wait_ge(s("gk1_ready"), 1)
            else:
                pe.wait_ge(s("upd_read"), 3)
            for h in range(HEADS):
                last = mm(bank[4 + h // 2][:, (h % 2) * NT:(h % 2) * NT + NT], wg2[0:32, d, h * P:h * P + P],
                          gk1[0:32, :])
            last.then_inc(s("gate_mm"), 1)

        @block.tensor
        def _(pe):
            reg = fb_count(pe, "pe_extra_pairs")

            def arrived(what):
                slot, nth = where[what]
                pe.wait_ge(s(f"full{slot}"), 16 * (nth + 1))
                return slot

            def ada(i, q):
                n = 3 * i + q
                if n:
                    pe.wait_ge(s("mod_ready"), n)
                slots = [arrived(("ada", i, q, j)) for j in range(4)]
                for k in range(KD):
                    for j in range(4):
                        last = mm(bank[7][32 * j:32 * j + 32, :], condT[:, k, :], piece(slots[j], KD, 512)[:, k, :],
                                  start=k == 0, stop=k == KD - 1)
                last.then_inc(s("ada_mm"), 1)
                pe.wait_ge(s("ada_rows"), n + 1)
                for t in range(4):
                    last = tr(bank[7][:, t * P:t * P + P], rows[:, t * P:t * P + P], ident)
                last.then_inc(s("ada_tr"), 1)

            def norm(n):
                for h in range(2):
                    pe.wait_ge(s("squares"), 2 * n + h + 1)
                    for k in range(4 * h, 4 * h + 4):
                        last = mm(bank[6][:, 0:NT], ones[:], hT[:, k].rearrange("p g t -> p (g t)"),
                                  start=k == 0, stop=k == KD - 1)
                last.then_inc(s("square_sum"), 1)

            def project(dst, slot, t, done, rhs=None):
                w = piece(slot, KD, 512)
                for k in range(KD):
                    last = mm(dst, w[:, k, t * P:t * P + P],
                              (hT[:, k] if rhs is None else rhs[:, k]).rearrange("p g t -> p (g t)"),
                              start=k == 0, stop=k == KD - 1)
                last.then_inc(s(done), 1)

            def residual(i, name, rhs=None):
                for m in range(KD):
                    if m % 4 == 0:
                        slot = arrived((name, m // 4))
                    if m >= 4:
                        pe.wait_ge(s("y_biased"), KD * i + m - 3)
                    project(bank[m % 4][:, 0:NT], slot, m % 4, "res_mm", rhs)

            def moe_round(pre, b, i):
                ringsem = pre + "full"
                nbase = moe_uses[i] if pre == "" else None

                def filled(slot, p):
                    if pre == "":
                        pe.wait_ge(s(f"full{slot}"), (p + (nbase[slot] + 1)) * 16)
                    else:
                        pe.wait_ge(s(f"fb_full{slot}"), (b + p + 1) * 16)

                def gather(p1):
                    for k in range(KD):
                        for g in range(G):
                            last = mm(bank[6 + k // 4][:, (k % 4) * P:(k % 4) * P + P], htok[:, g, k * P:k * P + P],
                                      sel[:, g].rearrange("p e n -> p (e n)"), start=g == 0, stop=g == G - 1)
                    last.then_inc(s(pre + "gathered"), 1)

                def pair(p, more):
                    n = b + p
                    pe.wait_ge(s(pre + "xg_ready"), n * 2 + 2)
                    pe.wait_ge(s(pre + "hidT_ready"), n)
                    for kind, done in ((0, "h1_mm"), (1, "h3_mm")):
                        if kind == 1:
                            pe.wait_ge(s(pre + "selT_ready"), n)
                        filled(2 * kind, p)
                        filled(2 * kind + 1, p)
                        for k in range(KD):
                            for e in range(2):
                                last = mm(bank[4 + kind][SLOTS * e:SLOTS * e + SLOTS, :],
                                          xg[:, k, SLOTS * e:SLOTS * e + SLOTS],
                                          piece(2 * kind + e, KD, FF)[:, k, :], start=k == 0, stop=k == KD - 1)
                        last.then_inc(s(pre + done), 1)
                    if more:
                        pe.wait_ge(s(pre + "sel_ready"), n + 2)
                        pe.wait_ge(s(pre + "yv_lo"), n)
                        pe.wait_ge(s(pre + "yv_hi"), n)
                        gather(None)
                    pe.wait_ge(s(pre + "hid_ready"), n + 1)
                    for f in range(4):
                        last = tr(bank[4][:, f * P:f * P + P], hid[:, f * P:f * P + P], ident)
                    last.then_inc(s(pre + "hidT_mm"), 1)
                    pe.wait_ge(s(pre + "selw_ready"), n + 1)
                    for g in range(G):
                        last = tr(bank[5][:, g * P:g * P + P], selw[:, g].rearrange("p e n -> p (e n)"), ident)
                    last.then_inc(s(pre + "selT_mm"), 1)
                    pe.wait_ge(s(pre + "hidT_ready"), n + 1)
                    if more:
                        pe.wait_ge(s(pre + "xg_ready"), n * 2 + 4)
                    filled(4, p)
                    filled(5, p)
                    for h in range(2):
                        for f in range(4):
                            for e in range(2):
                                last = mm(bank[6 + h][SLOTS * e:SLOTS * e + SLOTS, :],
                                          hidT[:, f, SLOTS * e:SLOTS * e + SLOTS],
                                          piece(4 + e, 4, D)[:, f, h * 512:h * 512 + 512], start=f == 0, stop=f == 3)
                        last.then_inc(s(pre + "y_mm"), 1)
                    pe.wait_ge(s(pre + "selT_ready"), n + 1)
                    for m in range(KD):
                        if m % 4 == 0:
                            pe.wait_ge(s(pre + ("yv_hi" if m else "yv_lo")), n + 1)
                        last = mm(half(m), yv[:, m * P:m * P + P], selT[:], start=False, stop=False,
                                  skip_group_check=True)
                    last.then_inc(s(pre + "scattered"), 1)

                for m in range(4):
                    mm(bank[m][:], zeros[:], zeros[:, 0:1].broadcast_to([P, 512]), start=True, stop=False, skip_group_check=True)
                pe.wait_ge(s(pre + "sel_ready"), b + 1)
                gather(None)
                with pe.Fori(0, PAIRS - 1) as p:
                    pair(p, True)
                pair(PAIRS - 1, False)

            def moe(i):
                norm(2 * i + 1)
                pe.wait_ge(s("h_ready"), KD * (2 * i + 2))
                pe.wait_ge(s("rw_loaded"), 32 * (i + 1))
                for k in range(KD):
                    last = mm(bank[4][0:20, 0:NT], rw[:, k, :], hT[:, k].rearrange("p g t -> p (g t)"),
                              start=k == 0, stop=k == KD - 1)
                last.then_inc(s("logits_mm"), 1)
                for g in range(G):
                    for k in range(KD):
                        last = tr(bank[2 * g + k // 4][:, (k % 4) * P:(k % 4) * P + P], hT[:, k, g], ident)
                    if g == 0:
                        last.then_inc(s("htok_tr"), 1)
                        pe.wait_ge(s("logits"), i + 1)
                        for gg in range(G):
                            lt = tr(bank[5][:, gg * 32:gg * 32 + 20], lraw[0:20, gg * P:gg * P + P], ident[0:20, 0:20])
                        lt.then_inc(s("logits_tr"), 1)
                last.then_inc(s("htok_tr"), 1)
                pe.wait_ge(s("members"), i + 1)
                mb = [memb[:, g, :] for g in range(G)]
                mm(bank[4][:, 0:16], upper, mb[0], start=True, stop=True)
                mm(bank[4][:, 16:32], upper, mb[1], start=True, stop=False)
                mm(bank[4][:, 16:32], ones[:], mb[0], start=False, stop=True)
                mm(bank[4][:, 32:48], ones[:], mb[0], start=True, stop=False)
                mm(bank[4][:, 32:48], ones[:], mb[1], start=False, stop=True).then_inc(s("ranks_mm"), 1)
                rounds = needed_rounds(pe, i)
                pe.wait_ge(s("htok_ready"), 2 * (i + 1))
                moe_round("", PAIRS * i, i)

                def one_round(b):
                    pe.wait_ge(s("x_ready"), 2 * i + 3)
                    pe.wait_ge(s("fb_rounds_added"), b // PAIRS)
                    moe_round("fb_", b, i)

                further_rounds(pe, i, rounds, reg, one_round)

            pe.wait_ge(s("base_loaded"), 16)
            pe.wait_ge(s("vrows_loaded"), 16 * len(vec_layout()))
            for t in range(4):
                last = tr(bank[4][:, t * P:t * P + P], vrows[:, t, :], ident)
            last.then_inc(s("vec_tr"), 1)
            pe.wait_ge(s("x_loaded"), 32)
            for k in range(KD):
                for g in range(G):
                    last = tr(half(k)[:, g * L:g * L + L], xin[:, g, k * P:k * P + P], ident)
                if k % 2:
                    last.then_inc(s("x_tr"), 1)

            dft = [cm[:, n * P:n * P + P] for n in range(9)]
            FRE, FIM, KFI, KBR, KBI, KFD, KBD, IRE, IIM = dft
            pe.wait_ge(s("filter_loaded"), 16 * 4)
            mm(bank[5][0:HY_HID, 0:L], fsmall[0:HY_EMB, 1, 0:HY_HID], fsmall[0:HY_EMB, 0, :]).then_inc(s("f_mm"), 1)
            pe.wait_ge(s("f_sin"), 1)
            mm(bank[5][0:HY_HID, 0:L], fsmall[0:HY_HID, 2, 0:HY_HID], fsmall[0:HY_HID, 4, :]).then_inc(s("f_mm"), 1)
            pe.wait_ge(s("f_sin"), 2)
            pe.wait_ge(s("w3_loaded"), 32)
            for c in range(8):
                if c >= 2:
                    pe.wait_ge(s("kfb_ready"), c - 1)
                mm(bank[4 + c % 2][:], fsmall[0:HY_HID, 5, :], w3f[0:HY_HID, c * 512:c * 512 + 512]) \
                    .then_inc(s("f3_mm"), 1)
            pe.wait_ge(s("kfb_ready"), 8)
            pe.wait_ge(s("x_copied"), 4)
            for w, (mf, mb_) in enumerate(((FRE, KBR), (KFI, KBI), (KFD, KBD))):
                for o in range(HY_ORDER):
                    for h in range(2):
                        c = (w * HY_ORDER + o) * 2 + h
                        if c >= 4:
                            pe.wait_ge(s("spec_ready"), c - 3)
                        mm(bank[c % 4][:], mf, kfb[:, 0, o, h * 512:h * 512 + 512], start=True, stop=False)
                        mm(bank[c % 4][:], mb_, kfb[:, 1, o, h * 512:h * 512 + 512], start=False, stop=True) \
                            .then_inc(s("spec_mm"), 1)

            pe.wait_ge(s("cond_ready"), 3)
            ada(0, 0)
            norm(0)
            pe.wait_ge(s("h_ready"), KD)
            pe.wait_ge(s("spec_ready"), 12)
            for m in range(24):
                if m % 4 == 0:
                    slot = arrived(("w_in", m // 4))
                if m >= 4:
                    pe.wait_ge(s("up_ready"), m - 3)
                project(bank[m % 4][:, 0:NT], slot, m % 4, "win_mm")
            ada(0, 1)
            for o in range(HY_ORDER):
                for g in range(G):
                    n = 2 * o + g
                    if o == 0:
                        pe.wait_ge(s("conv_ready"), 8)
                        if g == 0:
                            pe.wait_ge(s("up_ready"), 24)
                        else:
                            pe.wait_ge(s("z_ready"), 1)
                    else:
                        pe.wait_ge(s("z_ready"), 2 + g)
                    for k in range(KD):
                        last = tr(bank[4 + k // 4][:, (k % 4) * P:(k % 4) * P + P], uT[:, k, g], ident)
                    last.then_inc(s("zt_tr"), 1)
                    pe.wait_ge(s("zt_ready"), 2 * n + 2)
                    if n:
                        pe.wait_ge(s("prods"), 4 * n)
                    for w, f in enumerate((FRE, FIM)):
                        for h in range(2):
                            last = mm(bank[2 * w + h][:], f, zt[:, g, h * 512:h * 512 + 512])
                    last.then_inc(s("zf_mm"), 1)
                    if n == 1:
                        ada(0, 2)
                    pe.wait_ge(s("yspec"), 2 * n + 2)
                    for k in range(KD):
                        dst = bank[4 + k // 4][:, (k % 4) * P:(k % 4) * P + P]
                        mm(dst, ysp[:, 0, k * P:k * P + P], IRE, start=True, stop=False)
                        last = mm(dst, ysp[:, 1, k * P:k * P + P], IIM, start=False, stop=True)
                    last.then_inc(s("zi_mm"), 1)
            pe.wait_ge(s("z_ready"), 4)
            residual(0, "w_out", rhs=uT)
            if layers > 1:
                ada(1, 0)
            moe(0)

            if layers > 1:
                pe_gla(pe, arrived, ada, norm, project, residual)
                if layers > 2:
                    ada(2, 0)
                moe(1)

            if layers > 2:
                norm(4)
                ada(2, 1)
                pe.wait_ge(s("h_ready"), KD * 5)
                pe.wait_ge(s("cm2_loaded"), 16)
                cg, cl, sl = cm[:, 0:1024].rearrange("p (k n) -> p k n", k=2), cm[:, 1024:1152], cm[:, 1152:1280]
                for g in range(G):
                    for r in range(4):
                        n = 4 * g + r
                        if n >= 4:
                            pe.wait_ge(s("fn_rows"), n - 3)
                        for k in range(2):
                            last = mm(bank[n % 4][:], hT[:, 2 * r + k, g], cg[:, k, :], start=k == 0, stop=k == 1)
                        last.then_inc(s("fn_ch_mm"), 1)
                ada(2, 2)
                pe.wait_ge(s("fn_rows"), 8)
                for m in range(KD):
                    for g in range(G):
                        dst = half(m)[:, g * L:g * L + L]
                        rws = fnp[:, g, m // 2]
                        mm(dst, rws[:, (m % 2) * P:(m % 2) * P + P], cl, start=True, stop=False)
                        last = mm(dst, rws[:, 256 + (m % 2) * P:256 + (m % 2) * P + P], sl, start=False, stop=True)
                    if m % 2:
                        last.then_inc(s("fn_tok_mm"), 1)
                pe.wait_ge(s("fn_mixed"), 4)
                residual(2, "fn", rhs=fnm)
                if layers > 3:
                    ada(3, 0)
                moe(2)

            if layers > 3:
                norm(6)
                slot = arrived(("pool", 0))
                pe.wait_ge(s("h_ready"), KD * 7)
                pe.wait_ge(s("cm3_loaded"), 16)
                pw = piece(slot, KD, 256)
                for g in range(G):
                    for r in range(4):
                        n = 4 * g + r
                        dst = bank[n // 2][:, (n % 2) * 256:(n % 2) * 256 + 256]
                        for k in range(2):
                            last = mm(dst, hT[:, 2 * r + k, g], pw[:, 2 * r + k, :], start=k == 0, stop=k == 1)
                        if r % 2:
                            last.then_inc(s("pool_hw"), 1)
                ada(3, 1)
                pe.wait_ge(s("pool_rows"), 4)
                for m in range(KD):
                    for g in range(G):
                        last = mm(half(m)[:, g * L:g * L + L], plr[:, g, m // 2, (m % 2) * P:(m % 2) * P + P],
                                  cm[:, (4 * g + m // 2) * P:(4 * g + m // 2) * P + P])
                    last.then_inc(s("res_mm"), 1)
                ada(3, 2)
                moe(3)

            norm(2 * layers)
            for g in range(G):
                pe.wait_ge(s("final_ready"), g + 1)
                for k in range(KD):
                    last = tr(bank[2 * g + k // 4][:, (k % 4) * P:(k % 4) * P + P], hT[:, k, g], ident)
                last.then_inc(s("out_tr"), 1)

        @block.scalar
        def _(act):
            reg = fb_count(act, "act_extra_pairs")
            act_fn = nc.scalar.activation
            chained = [0]

            def chain(ins):
                chained[0] += 1
                ins.then_inc(s("act_chain"), 1)
                act.wait_ge(s("act_chain"), chained[0])

            act.dma_start(base[:], a["c_base"]).then_inc(s("base_loaded"), 16)
            act.wait_ge(s("vrows_clear"), 1)
            for name, t, r, n in vec_layout():
                dst = vrows[r:r + n, t, :]
                if name in ("b_ada01", "b_ada23"):
                    i = 0 if name == "b_ada01" else 2
                    src = a["b_ada"][i:i + 2].rearrange("l (c p) -> (l c) p", p=P)
                elif name in ("hy_f_b1", "hy_f_freq", "hy_f_b2"):
                    src, dst = a[name], vrows[r:r + 1, t, 0:HY_HID]
                elif name == "norm_g":
                    src = a[name].rearrange("l w (c p) -> (l w c) p", p=P)
                elif name in ("final_g", "c_ctx"):
                    src = a[name].rearrange("(c p) -> c p", p=P)
                elif name in ("hy_skip", "hy_conv_w", "gla_b_gk"):
                    src = a[name][0].rearrange("w (c p) -> (w c) p", p=P)
                else:
                    src = a[name].rearrange("o (c p) -> (o c) p", p=P)
                act.dma_start(dst, src).then_inc(s("vrows_loaded"), 16)
            act.dma_start(xin[:, 0, :], a["x_prompt"][0]).then_inc(s("x_loaded"), 16)
            act.dma_start(xin[:, 1, :], a["x_sample"][0]).then_inc(s("x_loaded"), 16)

            def norm(n):
                act.wait_ge(s("x_ready"), n + 1)
                for h in range(2):
                    act_fn(hT[:, 4 * h:4 * h + 4], xT[:, 4 * h:4 * h + 4], ACT.Square).then_inc(s("squares"), 1)
                act.wait_ge(s("square_sum"), n + 1)
                chain(act_fn(rstd[:].rearrange("p g t -> p (g t)"), bank[6][:, 0:NT], ACT.Ln, bias=eps, scale=1.0 / D))
                act_fn(rstd[:], rstd[:], ACT.Exp, scale=-0.5).then_inc(s("rstd_ready"), 1)

            def shift(n):
                i, w = n // 2, n % 2
                for k in range(KD):
                    act.wait_ge(s("scaled"), KD * n + k + 1)
                    for g in range(G):
                        last = act_fn(hT[:, k, g], hT[:, k, g], ACT.Identity,
                                      bias=mod[:, i % 2, 24 * w + k, g:g + 1])
                    last.then_inc(s("h_ready"), 1)

            def residual(i, bias, src):
                for m in range(KD):
                    act.wait_ge(s("res_mm"), KD * i + m + 1 if i < 3 else KD * i + (m | 1) + 1)
                    if m >= 4:
                        act.wait_ge(s("y_added"), 7 * i + m - 3)
                    ins = dict(bias=vcol(bias, m)) if bias else {}
                    act_fn(yb[:, m % 4], src(m), ACT.Identity, **ins).then_inc(s("y_biased"), 1)

            quarter = lambda m: bank[m % 4][:, 0:NT]

            def evac(pre, n):
                act.wait_ge(s(pre + "gathered"), n + 1)
                for h in range(2):
                    act_fn(xg[:, 4 * h:4 * h + 4], psum_tok(6 + h, 4), ACT.Copy).then_inc(s(pre + "xg_ready"), 1)

            def moe_round(pre, b):
                def pair(p, more):
                    n = b + p
                    act.wait_ge(s(pre + "h1_mm"), n + 1)
                    act.wait_ge(s(pre + "hid_ready"), n)
                    act_fn(sil[:], bank[4][:], ACT.Silu).then_inc(s(pre + "sil_ready"), 1)
                    if more:
                        evac(pre, n + 1)
                    act.wait_ge(s(pre + "selT_mm"), n + 1)
                    act.wait_ge(s(pre + "scattered"), n)
                    act_fn(selT[:], bank[5][:, 0:NT], ACT.Copy).then_inc(s(pre + "selT_ready"), 1)
                    act.wait_ge(s(pre + "y_mm"), n * 2 + 1)
                    act_fn(yv[:, 0:512], bank[6][:], ACT.Copy).then_inc(s(pre + "yv_lo"), 1)

                evac(pre, b)
                with act.Fori(0, PAIRS - 1) as p:
                    pair(p, True)
                pair(PAIRS - 1, False)

            def moe(i):
                norm(2 * i + 1)
                shift(2 * i + 1)
                act.wait_ge(s("logits_mm"), i + 1)
                act_fn(lraw[0:20, :], bank[4][0:20, 0:NT], ACT.Copy).then_inc(s("logits"), 1)
                for g in range(G):
                    act.wait_ge(s("htok_tr"), 2 * i + g + 1)
                    for h in range(2):
                        last = act_fn(htok[:, g, h * 512:h * 512 + 512], bank[2 * g + h][:], ACT.Copy)
                    last.then_inc(s("htok_ready"), 1)
                    act.wait_ge(s("route_in"), 2 * i + g + 1)
                    act_fn(*route_exp[g], ACT.Exp).then_inc(s("route_exp"), 1)
                rounds = needed_rounds(act, i)
                moe_round("", PAIRS * i)

                def one_round(b):
                    act.wait_ge(s("x_ready"), 2 * i + 3)
                    act.wait_ge(s("fb_rounds_added"), b // PAIRS)
                    moe_round("fb_", b)
                    act.wait_ge(s("fb_rounds_added"), b // PAIRS + 1)

                further_rounds(act, i, rounds, reg, one_round)

            act.wait_ge(s("vec_ready"), 1)
            act.wait_ge(s("cond_ready"), 1)
            for g, name in enumerate(("c_ctx", "c")):
                act_fn(condT[:, :, g], vcol(name, 0, KD), ACT.Silu).then_inc(s("cond_ready"), 1)
            for n in range(2):
                act.wait_ge(s("f_arg"), n + 1)
                act_fn(fsmall[0:HY_HID, 4 + n, :], fsmall[0:HY_HID, 3, :], ACT.Sin).then_inc(s("f_sin"), 1)
            for c in range(12):
                act.wait_ge(s("spec_mm"), c + 1)
                act_fn(spec[:, c // 4, (c // 2) % 2, (c % 2) * 512:(c % 2) * 512 + 512], bank[c % 4][:], ACT.Copy) \
                    .then_inc(s("spec_ready"), 1)
            norm(0)
            shift(0)
            act.wait_ge(s("up_clear"), 1)
            for m in range(24):
                act.wait_ge(s("win_mm"), m + 1)
                if m >= 4:
                    act.wait_ge(s("conv_ready"), m - 3)
                act_fn(up[:, m % 4, :, 1:L + 1], bank[m % 4][:, 0:NT].rearrange("p (g t) -> p g t", g=G), ACT.Identity,
                       bias=vcol("hy_b_in", m)).then_inc(s("up_ready"), 1)
            for n in range(4):
                act.wait_ge(s("zt_tr"), n + 1)
                for h in range(2):
                    act_fn(zt[:, n % 2, h * 512:h * 512 + 512], bank[4 + h][:], ACT.Copy).then_inc(s("zt_ready"), 1)
            residual(0, "hy_b_out", quarter)
            moe(0)
            if layers > 1:
                norm(2)
                shift(2)
                for b in range(2):
                    act.wait_ge(s("gla_proj"), b + 1)
                    act_fn(qT[:, 2 * b:2 * b + 2], bank[b][:].rearrange("p (h g t) -> p h g t", h=2, g=G),
                           ACT.Copy, scale=DK ** -0.5).then_inc(s("qk_ready"), 1)

                def gate_chain(d):
                    act.wait_ge(s("gate_mm"), d + 1)
                    if d:
                        act.wait_ge(s("kd_ready"), 1)
                    for h in range(HEADS):
                        last = act_fn(gx[:, h * NT:h * NT + NT], bank[4 + h // 2][:, (h % 2) * NT:(h % 2) * NT + NT],
                                      ACT.Identity, bias=vcol("gla_b_gk", 4 * d + h))
                    chain(last)
                    chain(act_fn(gt[:], gx[:], ACT.Abs))
                    chain(act_fn(gt[:], gt[:], ACT.Exp, scale=-1.0))
                    act_fn(gt[:], gt[:], ACT.Ln, bias=one).then_inc(s("gate_ln"), 1)
                    act.wait_ge(s("gate_cum"), 2 * d + 1)
                    act_fn(e1[:], gt[:], ACT.Exp, scale=1.0 / 16).then_inc(s("gate_exp"), 1)
                    act_fn(e2[:], gt[:], ACT.Exp, scale=-1.0 / 16).then_inc(s("gate_exp"), 1)
                    act.wait_ge(s("gate_cum"), 2 * d + 2)
                    act_fn(gx[:], gx[:], ACT.Exp, scale=1.0 / 16).then_inc(s("gate_exp"), 1)

                for b in range(2, 4):
                    act.wait_ge(s("gla_proj"), b + 1)
                    act_fn(kT[:, 2 * b - 4:2 * b - 2], bank[b][:].rearrange("p (h g t) -> p h g t", h=2, g=G),
                           ACT.Copy).then_inc(s("qk_ready"), 1)
                gate_chain(0)
                for n in range(4):
                    act.wait_ge(s("gla_proj"), 5 + n)
                    act_fn(vrow[:, n % 2, (n // 2) * 512:(n // 2) * 512 + 512], bank[n][:], ACT.Copy) \
                        .then_inc(s("v_ready"), 1)
                for m in range(KD):
                    act.wait_ge(s("gla_proj"), 9 + m)
                    act_fn(gT[:, m], bank[m % 4][:, 0:NT], ACT.Silu).then_inc(s("g_ready"), 1)
                for d in range(2):
                    if d == 1:
                        act.wait_ge(s("o_mm"), 1)
                        gate_chain(1)
                    for g in range(G):
                        act.wait_ge(s("kd_tr"), 2 * d + g + 1)
                        act_fn(kdr[:, g], psum_tok(6, 4), ACT.Copy).then_inc(s("kdr_ready"), 1)
                act.wait_ge(s("o_mm"), 2)
                for b in range(4):
                    act_fn(osq[:, 2 * b:2 * b + 2], bank[b][:].rearrange("p (h t) -> p h t", h=2), ACT.Square) \
                        .then_inc(s("osq_ready"), 1)
                act.wait_ge(s("osum_mm"), 1)
                for b in range(2):
                    v = ors[:, 2 * b:2 * b + 2].rearrange("p h t -> p (h t)")
                    chain(act_fn(v, bank[4 + b][:], ACT.Ln, bias=eps, scale=1.0 / DV))
                    act_fn(v, v, ACT.Exp, scale=-0.5).then_inc(s("ors_ready"), 1)
                residual(1, None, quarter)
                moe(1)
            if layers > 2:
                norm(4)
                shift(4)
                for n in range(8):
                    act.wait_ge(s("fn_ch_mm"), n + 1)
                    act_fn(fnp[:, n // 4, n % 4], bank[n % 4][:], ACT.Copy).then_inc(s("fn_rows"), 1)
                for b in range(4):
                    act.wait_ge(s("fn_tok_mm"), b + 1)
                    act_fn(fnm[:, 2 * b:2 * b + 2], bank[b][:].rearrange("p (h g t) -> p h g t", h=2, g=G), ACT.Copy) \
                        .then_inc(s("fn_mixed"), 1)
                residual(2, "fn_b_out", quarter)
                moe(2)
            if layers > 3:
                norm(6)
                shift(6)
                for b in range(4):
                    act.wait_ge(s("pool_hw"), b + 1)
                    act_fn(plr[:, b // 2, 2 * (b % 2):2 * (b % 2) + 2], bank[b][:].rearrange("p (r n) -> p r n", r=2),
                           ACT.Copy).then_inc(s("pool_rows"), 1)
                residual(3, "pool_b", half)
                moe(3)
            norm(2 * layers)

        @block.vector
        def _(dve):
            reg = fb_count(dve, "dve_extra_pairs")
            v = nc.vector
            tt, ts, stt = v.tensor_tensor, v.tensor_scalar, v.scalar_tensor_tensor
            chained = [0]

            def chain(ins):
                chained[0] += 1
                ins.then_inc(s("dve_chain"), 1)
                dve.wait_ge(s("dve_chain"), chained[0])

            def ada(i, q):
                n = 3 * i + q
                dve.wait_ge(s("ada_mm"), n + 1)
                v.tensor_copy(rows[:], bank[7][:]).then_inc(s("ada_rows"), 1)
                dve.wait_ge(s("ada_tr"), n + 1)
                src = bank[7][:].rearrange("p (t j r) -> p j t r", t=4, j=4)[:, :, :, 0:G]
                dst = mod[:, i % 2, 16 * q:16 * q + 16].rearrange("p (j t) g -> p j t g", j=4)
                bia = b_ada(i, 16 * q, 16).rearrange("p (j t) -> p j t", j=4).unsqueeze(3).broadcast_to([P, 4, 4, G])
                tt(dst, src, bia, ALU.add).then_inc(s("mod_ready"), 1)
                dve.wait_ge(s("mod_ready"), n + 1)
                if q != 1:
                    w = q // 2
                    ng = vcol("norm_g", 16 * i + 8 * w, KD).unsqueeze(2).broadcast_to([P, KD, G])
                    chain(stt(scale[:, i % 2, w], mod[:, i % 2, 24 * w + 8:24 * w + 16], 1.0, ng, ALU.add, ALU.mult))

            def norm(n):
                i, w = n // 2, n % 2
                dve.wait_ge(s("rstd_ready"), n + 1)
                for k in range(KD):
                    for g in range(G):
                        last = stt(hT[:, k, g], xT[:, k, g], scale[:, i % 2, w, k, g:g + 1], rstd[:, g],
                                   ALU.mult, ALU.mult)
                    last.then_inc(s("scaled"), 1)

            def residual(i, gate):
                for m in range(KD):
                    dve.wait_ge(s("y_biased"), KD * i + m + 1)
                    for g in range(G):
                        last = stt(xT[:, m, g], yb[:, m % 4, g * L:g * L + L], gate(m, g), xT[:, m, g],
                                   ALU.mult, ALU.add)
                    last.then_inc(s("y_added" if m < KD - 1 else "x_ready"), 1)

            g1 = lambda i: lambda m, g: mod[:, i % 2, 16 + m, g:g + 1]

            def build_sel(pre, n, p):
                r = rank[:, :, bass.ds(p * 2, 2)].unsqueeze(3).broadcast_to([P, G, 2, SLOTS])
                io = iota.unsqueeze(1).unsqueeze(1).broadcast_to([P, G, 2, SLOTS])
                tt(sel[:], io, r, ALU.is_equal).then_inc(s(pre + "sel_ready"), 1)

            def moe_round(pre, b, i):
                def pair(p, more):
                    n = b + p
                    dve.wait_ge(s(pre + "sel_ready"), n + 1)
                    dve.wait_ge(s(pre + "selT_mm"), n)
                    c = comb[:, :, bass.ds(p * 2, 2)].unsqueeze(3).broadcast_to([P, G, 2, SLOTS])
                    tt(selw[:], sel[:], c, ALU.mult).then_inc(s(pre + "selw_ready"), 1)
                    if more:
                        dve.wait_ge(s(pre + "gathered"), n + 1)
                        dve.wait_ge(s(pre + "selw_ready"), n + 1)
                        build_sel(pre, n + 1, p + 1)
                    dve.wait_ge(s(pre + "sil_ready"), n + 1)
                    dve.wait_ge(s(pre + "h3_mm"), n + 1)
                    dve.wait_ge(s(pre + "hidT_mm"), n)
                    tt(hid[:], sil[:], bank[5][:], ALU.mult).then_inc(s(pre + "hid_ready"), 1)
                    dve.wait_ge(s(pre + "hidT_mm"), n + 1)
                    dve.wait_ge(s(pre + "y_mm"), n * 2)
                    v.tensor_copy(hidT[:], psum_tok(4, 4)).then_inc(s(pre + "hidT_ready"), 1)
                    dve.wait_ge(s(pre + "y_mm"), n * 2 + 2)
                    dve.wait_ge(s(pre + "scattered"), n)
                    v.tensor_copy(yv[:, 512:1024], bank[7][:]).then_inc(s(pre + "yv_hi"), 1)

                build_sel(pre, b, 0)
                with dve.Fori(0, PAIRS - 1) as p:
                    pair(p, True)
                pair(PAIRS - 1, False)
                dve.wait_ge(s(pre + "scattered"), b + PAIRS)
                for m in range(KD):
                    for g in range(G):
                        last = stt(xT[:, m, g], half(m)[:, g * L:g * L + L], mod[:, i % 2, 40 + m, g:g + 1],
                                   xT[:, m, g], ALU.mult, ALU.add)
                last.then_inc(s("x_ready" if pre == "" else "fb_rounds_added"), 1)

            def first_best(out, vals, m):
                chain(tt(r_key, vals, m.unsqueeze(2).broadcast_to([P, G, 4]), ALU.is_equal))
                chain(tt(r_key, r_key, tie.unsqueeze(1).broadcast_to([P, G, 4]), ALU.mult))
                chain(v.reduce_max(r_km, r_key, AX.X))
                chain(tt(out, r_key, r_km.unsqueeze(2).broadcast_to([P, G, 4]), ALU.is_equal))

            def moe(i):
                norm(2 * i + 1)
                dve.wait_ge(s("logits_tr"), i + 1)
                chain(v.tensor_copy(lg[:], bank[5][:, 0:64].rearrange("p (g n) -> p g n", g=G)[:, :, 0:20]))
                b4 = lambda x: x.unsqueeze(2).broadcast_to([P, G, 4])
                chain(v.reduce_max(r_gm, lg[:, :, 0:4], AX.X))
                tt(r_gd, lg[:, :, 0:4], b4(r_gm), ALU.subtract).then_inc(s("route_in"), 1)
                first_best(r_og, lg[:, :, 0:4], r_gm)
                ex = lg[:, :, 4:20].rearrange("p g (q e) -> p g e q", q=4)
                chain(tt(r_x4, ex, r_og.unsqueeze(2).broadcast_to([P, G, 4, 4]), ALU.mult))
                chain(v.reduce_sum(r_le, r_x4, AX.X))
                chain(v.reduce_max(r_m1, r_le, AX.X))
                first_best(r_o1, r_le, r_m1)
                chain(stt(r_le2, r_o1, -1e30, r_le, ALU.mult, ALU.add))
                chain(v.reduce_max(r_m2, r_le2, AX.X))
                tt(r_dd, r_m2, r_m1, ALU.subtract).then_inc(s("route_in"), 1)
                first_best(r_o2, r_le2, r_m2)
                chain(tt(r_mt, r_o1, r_o2, ALU.add))
                tt(memb.rearrange("p g (q e) -> p g q e", q=4), r_og.unsqueeze(3).broadcast_to([P, G, 4, 4]),
                   r_mt.unsqueeze(2).broadcast_to([P, G, 4, 4]), ALU.mult).then_inc(s("members"), 1)
                dve.wait_ge(s("route_exp"), 2 * i + 1)
                chain(v.reduce_sum(r_sg, r_ge, AX.X))
                dve.wait_ge(s("route_exp"), 2 * i + 2)
                chain(stt(r_w2, r_de, 1.0, r_sg, ALU.add, ALU.mult))
                chain(v.reciprocal(r_w1, r_w2))
                chain(tt(r_w2, r_w1, r_de, ALU.mult))
                chain(tt(r_wt, r_o1, b4(r_w1), ALU.mult))
                chain(tt(r_key, r_o2, b4(r_w2), ALU.mult))
                chain(tt(r_wt, r_wt, r_key, ALU.add))
                chain(tt(comb.rearrange("p g (q e) -> p g q e", q=4), r_og.unsqueeze(3).broadcast_to([P, G, 4, 4]),
                         r_wt.unsqueeze(2).broadcast_to([P, G, 4, 4]), ALU.mult))
                dve.wait_ge(s("ranks_mm"), i + 1)
                chain(stt(r_rk, bank[4][:, 0:32].rearrange("p (g e) -> p g e", g=G), 1.0, memb, ALU.add, ALU.mult))
                chain(ts(rank[:], r_rk, -1.0, None, ALU.add))
                chain(v.reduce_max(r_mx, bank[4][:, 32:48], AX.X))
                for j in range(3):
                    chain(ts(r_rd[:, j:j + 1], r_mx, float(SLOTS * (j + 1)), None, ALU.is_gt))
                chain(ts(r_rd[:, 3:4], r_rd[:, 0:1], 1.0, r_rd[:, 1:2], ALU.add, ALU.add))
                tt(over[0:1, 0:1], r_rd[0:1, 3:4], r_rd[0:1, 2:3], ALU.add).then_inc(s("rounds_known"), 1)
                rounds = needed_rounds(dve, i)
                moe_round("", PAIRS * i, i)

                def one_round(b):
                    dve.wait_ge(s("x_ready"), 2 * i + 3)
                    dve.wait_ge(s("fb_rounds_added"), b // PAIRS)
                    ts(rank[:], rank[:], -float(SLOTS), None, ALU.add).then_inc(s("fb_rank"), 1)
                    dve.wait_ge(s("fb_rank"), b // PAIRS + 1)
                    moe_round("fb_", b, i)
                    dve.wait_ge(s("fb_rounds_added"), b // PAIRS + 1)

                further_rounds(dve, i, rounds, reg, one_round)

            v.memset(vrows[:], 0.0).then_inc(s("vrows_clear"), 1)
            v.memset(ones[:], 1.0)
            v.memset(zeros[:], 0.0)
            v.memset(eps, EPS)
            v.memset(one, 1.0)
            v.memset(condT[:], 0.0).then_inc(s("cond_ready"), 1)
            dve.wait_ge(s("vec_tr"), 1)
            v.tensor_copy(vec[:], bank[4][:]).then_inc(s("vec_ready"), 1)
            for b in range(4):
                dve.wait_ge(s("x_tr"), b + 1)
                v.tensor_copy(xT[:, 2 * b:2 * b + 2], bank[b][:].rearrange("p (k g t) -> p k g t", k=2, g=G)) \
                    .then_inc(s("x_copied"), 1)
            dve.wait_ge(s("vec_ready"), 1)
            H = HY_HID
            big = 1.5 * 2 ** 23
            twopi = 2 * math.pi
            c1 = 6.28125
            c2 = float(np.float32(twopi - c1))
            c2 = math.floor(c2 * 2 ** 20) / 2 ** 20
            c3 = twopi - c1 - c2
            for n, bias in enumerate(("hy_f_b1", "hy_f_b2")):
                dve.wait_ge(s("f_mm"), n + 1)
                arg, turns = fsmall[0:H, 3, :], fsmall[0:H, 6, :]
                if n:
                    dve.wait_ge(s("f_sin"), 1)
                chain(ts(arg, bank[5][0:H, 0:L], vcol(bias, 0)[0:H], vcol("hy_f_freq", 0)[0:H], ALU.add, ALU.mult))
                chain(ts(turns, arg, 1.0 / twopi, big, ALU.mult, ALU.add))
                chain(ts(turns, turns, -big, None, ALU.add))
                chain(stt(arg, turns, -c1, arg, ALU.mult, ALU.add))
                chain(stt(arg, turns, -c2, arg, ALU.mult, ALU.add))
                chain(stt(arg, turns, -c3, arg, ALU.mult, ALU.add))
                pi = 3.1415925
                ts(arg, arg, pi, -pi, ALU.min, ALU.max).then_inc(s("f_arg"), 1)
            for c in range(8):
                dve.wait_ge(s("f3_mm"), c + 1)
                if c == 0:
                    dve.wait_ge(s("window_loaded"), 16)
                h = c % 2
                tt(kfb[:, c // 4, (c // 2) % 2, h * 512:h * 512 + 512], bank[4 + c % 2][:],
                   win[:, h * 512:h * 512 + 512], ALU.mult).then_inc(s("kfb_ready"), 1)
            ada(0, 0)
            v.tensor_copy(small[:, 2:3], small[:, 0:1]).then_inc(s("x_ready"), 1)
            norm(0)
            dve.wait_ge(s("x_tr"), 4)
            dve.wait_ge(s("vec_tr"), 1)
            v.memset(up[:, :, :, 0:1], 0.0)
            v.memset(up[:, :, :, L + 1:L + 2], 0.0).then_inc(s("up_clear"), 1)
            for m in range(24):
                dve.wait_ge(s("up_ready"), m + 1)
                if m == 0:
                    dve.wait_ge(s("spec_ready"), 12)
                u, src = uT[:, m], up[:, m % 4]
                w = lambda t: vcol("hy_conv_w", 24 * t + m)
                chain(ts(u, src[:, :, 0:L], w(0), vcol("hy_conv_b", m), ALU.mult, ALU.add))
                chain(stt(u, src[:, :, 1:L + 1], w(1), u, ALU.mult, ALU.add))
                stt(u, src[:, :, 2:L + 2], w(2), u, ALU.mult, ALU.add).then_inc(s("conv_ready"), 1)
            ada(0, 1)
            for o in range(HY_ORDER):
                for g in range(G):
                    n = 2 * o + g
                    dve.wait_ge(s("zf_mm"), n + 1)
                    zre = [bank[0][:], bank[1][:]]
                    zim = [bank[2][:], bank[3][:]]
                    for w, (first, second, ka, kb) in enumerate(((zre, zim, 0, 1), (zre, zim, 1, 2))):
                        if n or w:
                            dve.wait_ge(s("yspec"), 2 * n + w)
                        for dst, z, kk in ((prod, first, ka), (prod2, second, kb)):
                            for h in range(2):
                                last = tt(dst[:, h * 512:h * 512 + 512], z[h], spec[:, kk, o, h * 512:h * 512 + 512],
                                          ALU.mult)
                            last.then_inc(s("prods"), 1)
                    if n == 1:
                        ada(0, 2)
                    dve.wait_ge(s("zi_mm"), n + 1)
                    dve.wait_ge(s("skip_ready"), n + 1)
                    for h in range(2):
                        sk = vskip.rearrange("p (k t) -> p k t", k=KD)[:, 4 * h:4 * h + 4]
                        chain(tt(sk, sk, psum_tok(4 + h, 4), ALU.add))
                        last = tt(uT[:, 4 * h:4 * h + 4, g], sk, uT[:, 8 * (o + 1) + 4 * h:8 * (o + 1) + 4 * h + 4, g],
                                  ALU.mult)
                    last.then_inc(s("z_ready"), 1)
            residual(0, g1(0))
            if layers > 1:
                ada(1, 0)
            moe(0)
            if layers > 1:
                norm(2)
                dve.wait_ge(s("gk1_mm"), 1)
                v.tensor_copy(gk1[0:32, :], bank[4][0:32, 0:NT]).then_inc(s("gk1_ready"), 1)

                def gate_chain(d):
                    if d:
                        dve.wait_ge(s("o_mm"), 1)
                    v.memset(reset[:], 1.0).then_inc(s("reset"), 1)
                    dve.wait_ge(s("reset"), 2 * d + 1)
                    e = reset.rearrange("p (n t) -> p n t", t=CH)
                    v.memset(e[:, :, 0:1] if d == 0 else e[:, :, CH - 1:CH], 0.0).then_inc(s("reset"), 1)
                    dve.wait_ge(s("gate_ln"), d + 1)
                    chain(stt(gx[:], gx[:], 0.0, gt[:], ALU.min, ALU.subtract))
                    dve.wait_ge(s("reset"), 2 * d + 2)
                    if d == 0:
                        v.tensor_tensor_scan(gt[:], reset[:], gx[:], 0.0, ALU.mult, ALU.add).then_inc(s("gate_cum"), 1)
                    else:
                        v.tensor_tensor_scan(gt[:, ::-1], reset[:, ::-1], gx[:, ::-1], 0.0, ALU.mult, ALU.add) \
                            .then_inc(s("gate_cum"), 1)
                    dve.wait_ge(s("gate_cum"), 2 * d + 1)
                    b16 = gt.rearrange("p (n t) -> p n t", t=CH)
                    bl = b16[:, :, CH - 1:CH] if d == 0 else b16[:, :, 0:1]
                    tt(gx.rearrange("p (n t) -> p n t", t=CH), bl.broadcast_to([P, 16, CH]), b16, ALU.subtract) \
                        .then_inc(s("gate_cum"), 1)
                    dve.wait_ge(s("gate_exp"), 3 * d + 2)
                    dve.wait_ge(s("qk_ready"), 4)
                    fl = lambda x: x.rearrange("p h g t -> p (h g t)")
                    tt(fl(qe), fl(qT), e1[:], ALU.mult).then_inc(s("qke_ready"), 1)
                    tt(fl(ke), fl(kT), e2[:], ALU.mult).then_inc(s("qke_ready"), 1)
                    dve.wait_ge(s("gate_exp"), 3 * d + 3)
                    tt(fl(kdT), fl(kT), gx[:], ALU.mult).then_inc(s("kd_ready"), 1)

                gate_chain(0)
                v.memset(sc[:], 0.0).then_inc(s("sc_clear"), 1)
                ada(1, 1)
                for d in range(2):
                    if d == 1:
                        dve.wait_ge(s("o_mm"), 1)
                        gate_chain(1)
                        v.memset(sc[:], 0.0).then_inc(s("sc_clear"), 1)
                        ada(1, 2)
                    dve.wait_ge(s("sc_clear"), d + 1)
                    dve.wait_ge(s("mask_loaded"), 16)
                    for g in range(G):
                        dve.wait_ge(s("scores_mm"), 2 * d + g + 1)
                        v.copy_predicated(sc[:, g], mask[:, d, :].unsqueeze(1).broadcast_to([P, HEADS, P]),
                                          psum_tok(4 + g, 4)).then_inc(s("sc_ready"), 1)
                    e4 = e1.rearrange("p (h g t) -> p h g t", h=HEADS, g=G)
                    dec = lambda h, g, c: e4[:, h, g, c * CH + CH - 1:c * CH + CH] if d == 0 else \
                        e4[:, h, g, c * CH:c * CH + 1]
                    pu = lambda h: bank[4 + h // 2][:, (h % 2) * DV:(h % 2) * DV + DV]
                    dve.wait_ge(s("s0_loaded"), 32)
                    if d == 1:
                        dve.wait_ge(s("state_stored"), 16)
                    dve.wait_ge(s("upd_mm"), 3 * d + 1)
                    for h in range(HEADS):
                        last = stt(s1l[:, h], s0[:, d, h], dec(h, 1, d), pu(h), ALU.mult, ALU.add)
                    last.then_inc(s("upd_read"), 1)
                    dve.wait_ge(s("upd_mm"), 3 * d + 2)
                    for b in range(2):
                        last = v.tensor_copy(s1c[:, 2 * b:2 * b + 2], bank[4 + b][:].rearrange("p (h n) -> p h n", h=2))
                    last.then_inc(s("upd_read"), 1)
                    dve.wait_ge(s("upd_read"), 3 * d + 2)
                    dve.wait_ge(s("upd_mm"), 3 * d + 3)
                    for h in range(HEADS):
                        last = stt(s2[:, h], s1c[:, h], dec(h, 0, 1 - d), pu(h), ALU.mult, ALU.add)
                    last.then_inc(s("upd_read"), 1)
                dve.wait_ge(s("o_mm"), 2)
                dve.wait_ge(s("upd_read"), 6)
                for b in range(4):
                    dve.wait_ge(s("osq_ready"), b + 1)
                    chain(v.tensor_copy(oT[:, 2 * b:2 * b + 2], bank[b][:].rearrange("p (h g t) -> p h g t", h=2, g=G)))
                for b in range(2):
                    dve.wait_ge(s("ors_ready"), b + 1)
                    for m in range(4 * b, 4 * b + 4):
                        o = oT[:, m].rearrange("p g t -> p (g t)")
                        last = stt(o, o, vcol("gla_norm_g", m % 2), ors[:, m // 2], ALU.mult, ALU.mult)
                    chain(last)
                tt(oT.rearrange("p k g t -> p k (g t)"), oT.rearrange("p k g t -> p k (g t)"), gT, ALU.mult) \
                    .then_inc(s("o_ready"), 1)
                residual(1, g1(1))
                if layers > 2:
                    ada(2, 0)
                moe(1)
            if layers > 2:
                norm(4)
                ada(2, 1)
                ada(2, 2)
                residual(2, g1(2))
                if layers > 3:
                    ada(3, 0)
                moe(2)
            if layers > 3:
                norm(6)
                ada(3, 1)
                gs = rtv(200, KD, G)
                chain(tt(gs, mod[:, 1, 16:24], vcol("pool_scale", 0, KD).unsqueeze(2).broadcast_to([P, KD, G]), ALU.mult))
                residual(3, lambda m, g: gs[:, m, g:g + 1])
                ada(3, 2)
                moe(3)
            dve.wait_ge(s("rstd_ready"), 2 * layers + 1)
            for g in range(G):
                for k in range(KD):
                    last = stt(hT[:, k, g], xT[:, k, g], vcol("final_g", k), rstd[:, g], ALU.mult, ALU.mult)
                last.then_inc(s("final_ready"), 1)
            for g in range(G):
                dve.wait_ge(s("out_tr"), g + 1)
                for h in range(2):
                    last = v.tensor_copy(xin[:, g, h * 512:h * 512 + 512], bank[2 * g + h][:])
                last.then_inc(s("out_rows"), 1)

        @block.gpsimd
        def _(pool):
            v = nc.gpsimd
            pool.dma_start(cm[:, 0:1152], a["c_dft"]).then_inc(s("filter_loaded"), 16)
            pool.dma_start(fsmall[0:HY_EMB, 0, :], a["c_pos"]).then_inc(s("filter_loaded"), 16)
            pool.dma_start(fsmall[0:HY_EMB, 1, 0:HY_HID], a["hy_f_w1"][0]).then_inc(s("filter_loaded"), 16)
            pool.dma_start(fsmall[0:HY_HID, 2, 0:HY_HID], a["hy_f_w2"][0]).then_inc(s("filter_loaded"), 16)
            for h in range(2):
                pool.dma_start(w3f[0:HY_HID, 2048 * h:2048 * h + 2048], a["hy_f_w3"][0][:, 2048 * h:2048 * h + 2048]) \
                    .then_inc(s("w3_loaded"), 16)
            pool.dma_start(win[:], a["c_window"]).then_inc(s("window_loaded"), 16)
            pool.dma_start(mask[:].rearrange("p d t -> p (d t)"), a["c_mask"]).then_inc(s("mask_loaded"), 16)

            def load_router(i):
                pool.dma_start(rw[:, :, 0:4], a["moe_w_rg"][i].rearrange("(k p) n -> p k n", p=P)) \
                    .then_inc(s("rw_loaded"), 16)
                pool.dma_start(rw[:, :, 4:20], a["moe_w_re"][i].rearrange("(k p) n -> p k n", p=P)) \
                    .then_inc(s("rw_loaded"), 16)

            load_router(0)
            pool.wait_ge(s("conv_ready"), 24)
            for o in range(HY_ORDER):
                for g in range(G):
                    n = 2 * o + g
                    if n:
                        pool.wait_ge(s("z_ready"), n if n < 3 else 3)
                    if o == 1:
                        pool.wait_ge(s("z_ready"), 1 + g)
                    for k in range(KD):
                        last = v.tensor_scalar(vskip[:, k * P:k * P + P], uT[:, k, g], vcol("hy_skip", 8 * o + k), None,
                                               ALU.mult)
                    last.then_inc(s("skip_ready"), 1)
                    for w, op in enumerate((ALU.subtract, ALU.add)):
                        pool.wait_ge(s("prods"), 4 * n + 2 * w + 2)
                        if n:
                            pool.wait_ge(s("zi_mm"), n)
                        v.tensor_tensor(ysp[:, w], prod[:], prod2[:], op).then_inc(s("yspec"), 1)
            if layers > 1:
                pool.wait_ge(s("x_ready"), 2)
                v.memset(wg2[0:32], 0.0).then_inc(s("wg2_clear"), 1)
                pool.wait_ge(s("wg2_clear"), 1)
                for d in range(2):
                    pool.dma_start(wg1[:, :, 16 * d:16 * d + 16], a["gla_w_gk1"][0, d].rearrange("(k p) r -> p k r", p=P)) \
                        .then_inc(s("cm1_loaded"), 16)
                    pool.dma_start(wg2[16 * d:16 * d + 16, d, :], a["gla_w_gk2"][0, d]).then_inc(s("cm1_loaded"), 16)
                    pool.dma_start(s0[:, d], a["state_gla"][0, 0, d].rearrange("h k v -> k h v")) \
                        .then_inc(s("s0_loaded"), 16)
                pool.wait_ge(s("logits_mm"), 1)
                load_router(1)
                for d in range(2):
                    pool.wait_ge(s("upd_read"), 3 * d + 3)
                    pool.dma_start(a["new_state"][0, 0, d].rearrange("h k v -> k h v"), s2[:]) \
                        .then_inc(s("state_stored"), 16)
            if layers > 2:
                pool.wait_ge(s("x_ready"), 4)
                pool.dma_start(cm[:], a["c_fnet"]).then_inc(s("cm2_loaded"), 16)
                pool.wait_ge(s("logits_mm"), 2)
                load_router(2)
            if layers > 3:
                pool.wait_ge(s("x_ready"), 6)
                pool.dma_start(cm[:, 0:1024], a["c_pool"]).then_inc(s("cm3_loaded"), 16)
                pool.wait_ge(s("logits_mm"), 3)
                load_router(3)


INPUTS = ['x_prompt', 'x_sample', 'state_gla', 'c', 'c_ctx', 'w_ada', 'b_ada', 'norm_g',
          'hy_w_in', 'hy_b_in', 'hy_conv_w', 'hy_conv_b', 'hy_f_w1', 'hy_f_b1', 'hy_f_freq', 'hy_f_w2', 'hy_f_b2',
          'hy_f_w3', 'hy_skip', 'hy_w_out', 'hy_b_out',
          'gla_w_q', 'gla_w_k', 'gla_w_v', 'gla_w_g', 'gla_w_gk1', 'gla_w_gk2', 'gla_b_gk', 'gla_norm_g', 'gla_w_o',
          'fn_w_out', 'fn_b_out', 'pool_w', 'pool_b', 'pool_scale',
          'moe_w_rg', 'moe_w_re', 'moe_w1', 'moe_w3', 'moe_w2', 'final_g']


def declare(nc, arrays):
    aps = {n: nc.dram_tensor(f"in_{n}", x.shape, mybir.dt.from_np(x.dtype), kind="ExternalInput").ap()
           for n, x in arrays.items()}
    for n, shape in (("y_prompt", (1, L, D)), ("y_sample", (1, L, D)), ("new_state", (1, 1, 2, HEADS, DK, DV))):
        aps[n] = nc.dram_tensor(f"out_{n}", shape, F32, kind="ExternalOutput").ap()
    return aps


def kernel(**inputs):
    import concourse.bacc as bacc
    from concourse.bass_utils import run_bass_kernel_spmd

    nc = bacc.Bacc("TRN2", target_bir_lowering=False, num_devices=1)
    arrays = {n: np.ascontiguousarray(inputs[n]) for n in INPUTS}
    arrays.update({f"c_{n}": x for n, x in constants().items()})
    build(nc, declare(nc, arrays))
    r = run_bass_kernel_spmd(nc, [{f"in_{n}": x for n, x in arrays.items()}], core_ids=[0])
    got = r.results[0]
    return got["out_y_prompt"], got["out_y_sample"], got["out_new_state"]
```

```python
import math
from contextlib import ExitStack

import numpy as np
import concourse.bass as bass
from concourse import mybir

F32 = mybir.dt.float32
BF16 = mybir.dt.bfloat16
I32 = mybir.dt.int32
U8 = mybir.dt.uint8
ALU = mybir.AluOpType
ACT = mybir.ActivationFunctionType
AX = mybir.AxisListType

D = 1024
L = 128
G = 2
NT = G * L
P = 128
KD = D // P
LAYERS = 4
GRID_W = 64
EPS = 1e-6
HY_BANDS, HY_HID, HY_ORDER = 8, 64, 2
HY_EMB = 1 + 2 * HY_BANDS
HEADS, DK, DV, CH = 4, 128, 256, 64
WINDOWS = (2, 4, 8, 16)
EXPERTS, EGROUPS, FF = 16, 4, 512
SLOTS = 64
PAIRS = EXPERTS // 2
RING = 6
PIECE = 4096

VEC = {}


def vec_layout():
    tiles = [[("norm_g", 64), ("final_g", 8), ("c", 8), ("c_ctx", 8), ("hy_skip", 16), ("hy_b_out", 8),
              ("fn_b_out", 8), ("pool_b", 8)],
             [("b_ada01", 96), ("hy_b_in", 24), ("pool_scale", 8)],
             [("b_ada23", 96), ("hy_conv_b", 24), ("gla_b_gk", 8)],
             [("hy_conv_w", 72), ("gla_norm_g", 2), ("hy_f_b1", 1), ("hy_f_freq", 1), ("hy_f_b2", 1)]]
    return [(name, t, sum(n for _, n in tile[:i]), n) for t, tile in enumerate(tiles)
            for i, (name, n) in enumerate(tile)]


VEC = {name: t * P + r for name, t, r, _ in vec_layout()}
VECS = max(t * P + r + n for _, t, r, n in vec_layout())


def constants():
    n = np.arange(L)
    f = np.arange(P)
    ang = 2 * np.pi * np.outer(n, f) / (2 * L)
    cos, sin = np.cos(ang), np.sin(ang)
    nyq = (-1.0) ** n
    fwd_re = cos.copy()
    fwd_im = -sin.copy()
    fwd_im[:, 0] = nyq
    kf_im = -sin
    kb_re = cos.copy()
    kb_re[0] = 0
    kb_im = sin.copy()
    kf_d = cos.copy()
    kf_d[:, 0] = nyq
    kb_d = kf_d.copy()
    kb_d[0] = 0
    inv_re = 2 * cos.T / (2 * L)
    inv_re[0] /= 2
    inv_im = -2 * sin.T / (2 * L)
    inv_im[0] = nyq / (2 * L)
    dft = np.concatenate([fwd_re, fwd_im, kf_im, kb_re, kb_im, kf_d, kb_d, inv_re, inv_im], axis=1)

    bands = np.linspace(1e-4, HY_BANDS - 1, HY_BANDS)
    a = (2 * np.pi * n / L)[:, None] * bands[None]
    pos = np.concatenate([(n / L)[:, None], np.cos(a), -np.sin(a)], axis=-1).T
    deltas = np.linspace(math.log(1e-2) / 1.5, math.log(1e-2) / 0.3, D)
    window = np.exp(-np.linspace(0, 1, L)[:, None] * np.abs(deltas)[None])

    c = D // 4
    ch = 2 * np.pi * np.outer(np.arange(c), np.arange(c)) / c
    cs = np.concatenate([np.cos(ch), np.sin(ch)], axis=1).reshape(2, P, 2 * c).transpose(1, 0, 2).reshape(P, -1)
    tok = 2 * np.pi * np.outer(n, n) / L
    fnet = np.concatenate([cs, np.cos(tok) / math.sqrt(L * c), -np.sin(tok) / math.sqrt(L * c)], axis=1)

    def mean(length, k):
        m = np.zeros((length, length))
        for t in range(length):
            lo, hi = max(t - k // 2, 0), min(t + k - k // 2, length)
            m[t, lo:hi] = 1.0 / (hi - lo)
        return m

    pool = []
    for g in range(G):
        for k in WINDOWS:
            m = mean(L, k) if g == 0 else np.kron(mean(L // GRID_W, k), mean(GRID_W, k))
            pool.append((m - np.eye(L)).T)
    pool = np.concatenate(pool, axis=1)

    base = np.concatenate([np.eye(P), np.tile(np.arange(SLOTS), (P, 1)),
                           np.tile(np.arange(4, 0, -1), (P, 1))], axis=1)
    s, t = np.arange(P)[:, None] % CH, np.arange(P)[None]
    same = (np.arange(P)[:, None] // CH) == (t // CH)
    mask = np.concatenate([same & (s <= t % CH), same & (s >= t % CH)], axis=1)
    out = {"base": base, "upper": np.triu(np.ones((P, P)), 1), "dft": dft, "pos": pos, "window": window, "fnet": fnet, "pool": pool, "mask": mask}
    return {k: v.astype(np.float32) for k, v in out.items()}


ADA_AT = {"start": [0], "w_in1": [1], "w_in3": [2], "w_in5": [3], "conv0": [4], "conv1": [5], "conv2": [6],
          "queries": [7], "values": [8], "between": [9], "heads": [10], "fnet": [11]}


def adas_until(point, layers):
    points = list(ADA_AT)
    return sum(n < 3 * layers for at in points[:points.index(point) + 1] for n in ADA_AT[at])


def piece_stream(layers):
    ada = lambda at: [("ada", n // 3, n % 3, j) for n in ADA_AT[at] if n < 3 * layers for j in range(4)]
    halves = lambda name: [(name, 0), (name, 1)]
    lay = [ada("start") + sum([[("w_in", c), ("w_in", c + 1)] + ada(f"w_in{c + 1}") for c in (0, 2, 4)], [])
           + ada("conv0") + ada("conv1") + ada("conv2") + halves("w_out"),
           [("wq", 0)] + ada("queries") + [("wk", 0)] + halves("wv") + ada("values") + halves("wg")
           + ada("between") + ada("heads") + halves("wo"),
           ada("fnet") + halves("fn"),
           [("pool", 0)]]
    used, out, at = [0] * RING, [], 0
    for i in range(layers):
        for what in lay[i]:
            slot = at % RING
            out.append((what, slot, used[slot]))
            used[slot] += 1
            at += 1
        slots = [(at + n) % RING for n in range(RING)]
        out.append((("moe", i), slots, [used[x] for x in slots]))
        used = [u + PAIRS for u in used]
    return out


def build(nc, a, layers=LAYERS):
    stream = piece_stream(layers)
    where = {what: (slot, nth) for what, slot, nth in stream if what[0] != "moe"}
    moe_slots = {what[1]: slots for what, slots, _ in stream if what[0] == "moe"}
    moe_uses = {what[1]: nth for what, _, nth in stream if what[0] == "moe"}

    ctx = ExitStack()
    sems = {}

    def s(name):
        if name not in sems:
            sems[name] = ctx.enter_context(nc.semaphore(name))
        return sems[name]

    def sb(name, shape, dt=F32):
        return ctx.enter_context(nc.sbuf_tensor(name, shape, dt))

    with ctx:
        ring = [sb(f"ring{i}", [P, PIECE]) for i in range(RING)]
        xT = sb("xT", [P, KD, G, L])
        hT = sb("hT", [P, KD, G, L])
        arena = sb("arena", [P, 20480])
        cm = sb("cm", [P, 1280])
        base = sb("base", [P, 196])
        ident, iota, tie = base[:, 0:128], base[:, 128:192], base[:, 192:196]
        ones = sb("ones", [P, P])
        ones16, upper16 = sb("ones16", [P, P], BF16), sb("upper16", [P, P], BF16)
        zeros = sb("zeros", [P, P], BF16)
        vec = sb("vec", [P, VECS])
        mod = sb("mod", [P, LAYERS, 48, G])
        scale = sb("scale", [P, LAYERS, 2, KD, G])
        condT = sb("condT", [P, KD, 32])
        rstd = sb("rstd", [P, G, L])
        rows = sb("rows", [P, 512])
        small = sb("small", [P, 4])
        eps, one = small[:, 0:1], small[:, 1:2]
        rw = sb("rw", [P, KD, 20])
        mask = sb("mask", [P, 2, P], U8)
        over = sb("over", [1, 2], I32)
        bank = [ctx.enter_context(nc.psum_tensor(f"bank{i}", [P, 512], F32)) for i in range(8)]

        def ar(lo, *dims):
            n = int(np.prod(dims))
            v = arena[:, lo:lo + n]
            if len(dims) == 1:
                return v
            names = "abcd"[:len(dims)]
            return v.rearrange(f"p ({' '.join(names)}) -> p {' '.join(names)}",
                               **dict(zip(names, dims)))

        def vcol(name, lo, n=1):
            return vec[:, VEC[name] + lo:VEC[name] + lo + n]

        def piece(slot, *dims):
            names = "abc"[:len(dims)]
            return ring[slot][:, 0:int(np.prod(dims))].rearrange(
                f"p ({' '.join(names)}) -> p {' '.join(names)}", **dict(zip(names, dims)))

        def b_ada(i, lo, n):
            return vcol("b_ada01" if i < 2 else "b_ada23", 48 * (i % 2) + lo, n)

        def half(m):
            return bank[m // 2][:, (m % 2) * NT:(m % 2) * NT + NT]

        xin = ar(15360, G, D)
        vrows = ar(17408, 4, P)
        w3f = ar(6144, 4096)
        kfb = ar(10240, 2, HY_ORDER, D)
        win = ar(14336, D)
        spec = ar(0, 3, HY_ORDER, D)
        uT = ar(6144, 24, G, L)
        zt = ar(12288, G, D)
        prod = ar(14336, D)
        ysp = ar(15360, 2, D)
        up = ar(17408, 4, G, L + 2)
        vskip = [ar(17408, D), ar(19456, D)]
        hflat = hT[:].rearrange("p k g t -> p (k g t)")
        prods = [[prod, ar(18432, D)], [hflat[:, 0:D], hflat[:, D:2 * D]]]
        upper, mask32 = ar(19472, P), ar(19600, 2, P)
        fsmall = ar(18448, 8, P)
        htok = ar(0, G, D)
        xg = ar(2048, KD, P)
        sil = ar(3072, FF)
        hid = ar(3584, FF)
        hidT = ar(4096, 4, P)
        yv = ar(4608, D)
        sel = ar(5632, G, 2, SLOTS)
        selw = ar(5888, G, 2, SLOTS)
        selT = ar(6144, NT)
        comb = ar(6400, G, EXPERTS)
        memb = ar(6432, EXPERTS).bitcast(BF16).rearrange("p (g n) -> p g n", g=G)
        rank = ar(6464, G, EXPERTS)
        lraw = ar(6496, NT)
        lg = ar(6752, G, 20)
        rt = ar(6800, 1024)
        yb = ar(14336, 4, NT)

        fnp = ar(8192, G, 4, 512)
        fnm = ar(12288, KD, G, L)
        plr = ar(8192, G, 4, 256)
        qT, kT = ar(0, HEADS, G, L), ar(1024, HEADS, G, L)
        vrow = ar(2048, G, D)
        gT = ar(4096, KD, NT)
        gx, gt = ar(6144, 1024), ar(7168, 1024)
        e1, e2 = ar(8192, 1024), ar(9216, 1024)
        qe, ke, kdT = ar(10240, HEADS, G, L), ar(11264, HEADS, G, L), ar(12288, HEADS, G, L)
        reset = ar(11264, 1024)
        kdr = ar(13312, G, HEADS, P)
        sc = ar(14336, G, HEADS, P)
        s0 = ar(15360, 2, HEADS, DV)
        s1c, s1l, s2 = ar(17408, HEADS, DV), ar(18432, HEADS, DV), ar(19456, HEADS, DV)
        oT, osq, ors = ar(8192, KD, G, L), ar(10240, KD, NT), ar(6144, HEADS, NT)
        wg1 = cm[:, 0:256].rearrange("p (k r) -> p k r", k=KD)
        gk1 = cm[:, 0:NT]
        wg2 = cm[:, 256:1280].rearrange("p (d n) -> p d n", d=2)

        def psum_tok(b, n):
            return bank[b][:, 0:n * P].rearrange("p (a b) -> p a b", a=n)

        def rtv(lo, *dims):
            n = int(np.prod(dims))
            v = rt[:, lo:lo + n]
            if len(dims) == 1:
                return v
            names = "abcd"[:len(dims)]
            return v.rearrange(f"p ({' '.join(names)}) -> p {' '.join(names)}", **dict(zip(names, dims)))

        r_gd, r_ge = rtv(0, G, 4), rtv(8, G, 4)
        r_dd, r_de = rtv(16, G), rtv(18, G)
        r_gm, r_key, r_km, r_og = rtv(20, G), rtv(24, G, 4), rtv(32, G), rtv(40, G, 4)
        r_x4 = rtv(48, G, 4, 4)
        r_le, r_m1, r_o1, r_o2 = rtv(80, G, 4), rtv(88, G), rtv(96, G, 4), rtv(104, G, 4)
        r_le2, r_m2, r_sg, r_w1, r_w2 = rtv(112, G, 4), rtv(120, G), rtv(122, G), rtv(124, G), rtv(126, G)
        r_wt, r_mt, r_rk = rtv(128, G, 4), rtv(136, G, 4), rtv(144, G, EXPERTS)
        r_mx, r_rd = rtv(176, 1), rtv(177, 4)
        route_exp = [(r_ge, r_gd), (r_de, r_dd)]

        g_bank = lambda m: 6 if m in (3, 5) else 7

        block = ctx.enter_context(nc.Block())

        def freed(what):
            k = what[0]
            if k == "ada":
                return "ada_mm", 3 * what[1] + what[2] + 1
            if k == "w_in":
                return "win_mm", 4 * what[1] + 4
            if k in ("w_out", "wo", "fn"):
                return "res_mm", KD * {"w_out": 0, "wo": 1, "fn": 2}[k] + 4 * what[1] + 4
            if k == "pool":
                return "pool_hw", 4
            return "gla_proj", {"wq": 2, "wk": 4, "wv": 6 + 2 * what[1], "wg": 12 + 4 * what[1]}[k]

        def source(what):
            k = what[0]
            if k == "ada":
                c = 4 * what[2] + what[3]
                return a["w_ada"][what[1]][:, 512 * c:512 * c + 512].rearrange("(k p) n -> p k n", p=P), KD
            if k == "w_in":
                return a["hy_w_in"][0][:, 512 * what[1]:512 * what[1] + 512].rearrange("(k p) n -> p k n", p=P), KD
            if k == "pool":
                return a["pool_w"][0].rearrange("g (k p) e -> p (g k) e", p=P), KD
            name = {"w_out": "hy_w_out", "wo": "gla_w_o", "fn": "fn_w_out", "wq": "gla_w_q", "wk": "gla_w_k",
                    "wv": "gla_w_v", "wg": "gla_w_g"}[k]
            return a[name][0][:, 512 * what[1]:512 * what[1] + 512].rearrange("(k p) n -> p k n", p=P), KD

        expert_dram = [a["moe_w1"].rearrange("l x (k p) n -> (l x) p k n", p=P),
                       a["moe_w3"].rearrange("l x (k p) n -> (l x) p k n", p=P),
                       a["moe_w2"].rearrange("l x (k p) n -> (l x) p k n", p=P)]
        USED = ["h1_mm", "h3_mm", "y_mm"]

        def used_up(pre, kind, pairs):
            return s(pre + USED[kind]), pairs * (2 if kind == 2 else 1)

        def expert_load(sp, kind, e, i, first_expert, full):
            slot = moe_slots[i][2 * kind + e]
            dst = piece(slot, KD, FF) if kind < 2 else piece(slot, 4, D)
            src = expert_dram[kind][bass.ds(first_expert + e, 1)].rearrange("o p k n -> p (o k) n")
            sp.dma_start(dst, src).then_inc(s(f"{full}{slot if full == 'full' else 2 * kind + e}"), 16)

        def needed_rounds(eng, i):
            eng.wait_ge(s("rounds_known"), i + 1)
            return eng.value_load(over[0:1, 0:1], min_val=1, max_val=NT // SLOTS)

        def fb_count(eng, name):
            reg = eng.alloc_register(name)
            eng.reg_mov(reg, 0)
            return reg

        def further_rounds(eng, i, rounds, reg, one_round):
            with eng.If(rounds - 1):
                with eng.Fori(1, rounds) as _:
                    b = eng.snap(reg, min_val=0, max_val=8 * 3 * LAYERS)
                    one_round(b)
                    eng.reg_add(reg, reg, PAIRS)

        def vector_loads(eng, part):
            for name, t, r, n in vec_layout()[part::2]:
                dst = vrows[r:r + n, t, :]
                if name in ("b_ada01", "b_ada23"):
                    i = 0 if name == "b_ada01" else 2
                    src = a["b_ada"][i:i + 2].rearrange("l (c p) -> (l c) p", p=P)
                elif name in ("hy_f_b1", "hy_f_freq", "hy_f_b2"):
                    src, dst = a[name], vrows[r:r + 1, t, 0:HY_HID]
                elif name == "norm_g":
                    src = a[name].rearrange("l w (c p) -> (l w c) p", p=P)
                elif name in ("final_g", "c_ctx"):
                    src = a[name].rearrange("(c p) -> c p", p=P)
                elif name in ("hy_skip", "hy_conv_w", "gla_b_gk"):
                    src = a[name][0].rearrange("w (c p) -> (w c) p", p=P)
                else:
                    src = a[name].rearrange("o (c p) -> (o c) p", p=P)
                eng.dma_start(dst, src).then_inc(s("vrows_loaded"), 16)

        @block.sync
        def _(sp):
            reg = fb_count(sp, "sp_extra_pairs")
            sp.dma_start(xin[:, 0, :], a["x_prompt"][0]).then_inc(s("x_loaded"), 16)
            sp.dma_start(xin[:, 1, :], a["x_sample"][0]).then_inc(s("x_loaded"), 16)
            sp.wait_ge(s("vrows_clear"), 1)
            vector_loads(sp, 1)
            for h in range(2):
                sp.dma_start(w3f[0:HY_HID, 2048 * h:2048 * h + 2048], a["hy_f_w3"][0][:, 2048 * h:2048 * h + 2048]) \
                    .then_inc(s("w3_loaded"), 16)
            sp.dma_start(win[:], a["c_window"]).then_inc(s("window_loaded"), 16)
            sp.dma_start(cm[:, 0:1152], a["c_dft"]).then_inc(s("dft_loaded"), 16)
            last = [None] * RING
            extra = None

            def slot_free(slot):
                if last[slot]:
                    name, value = last[slot]
                    sp.wait_ge(s(name), value)
                    if name in USED:
                        sp.wait_ge(s("fb_" + name), extra * (2 if name == "y_mm" else 1))

            for what, slot, nth in stream:
                if what[0] != "moe":
                    slot_free(slot)
                    src, n = source(what)
                    sp.dma_start(piece(slot, n, 512) if what[0] != "pool" else piece(slot, n, 256), src) \
                        .then_inc(s(f"full{slot}"), 16)
                    last[slot] = freed(what)
                    continue
                i = what[1]
                for kind in range(3):
                    for e in range(2):
                        slot_free(moe_slots[i][2 * kind + e])
                        expert_load(sp, kind, e, i, EXPERTS * i, "full")
                with sp.Fori(1, PAIRS) as p:
                    for kind in range(3):
                        sem, v = used_up("", kind, 1)
                        sp.wait_ge(sem, (PAIRS * i + p) * v)
                        for e in range(2):
                            expert_load(sp, kind, e, i, EXPERTS * i + p * 2, "full")
                rounds = needed_rounds(sp, i)

                def one_round(b):
                    for kind in range(3):
                        sem, v = used_up("", kind, 1)
                        sp.wait_ge(sem, PAIRS * (i + 1) * v)
                    with sp.Fori(0, PAIRS) as p:
                        for kind in range(3):
                            sem, v = used_up("fb_", kind, 1)
                            sp.wait_ge(sem, (b + p) * v)
                            for e in range(2):
                                expert_load(sp, kind, e, i, EXPERTS * i + p * 2, "fb_full")

                further_rounds(sp, i, rounds, reg, one_round)
                for kind in range(3):
                    for e in range(2):
                        last[moe_slots[i][2 * kind + e]] = (USED[kind], PAIRS * (i + 1) * (2 if kind == 2 else 1))
                extra = sp.snap(reg, min_val=0, max_val=8 * 3 * LAYERS)
            for g, name in enumerate(("y_prompt", "y_sample")):
                sp.wait_ge(s("out_rows"), g + 1)
                sp.dma_start(a[name][0], xin[:, g, :]).then_inc(s("stored"), 16)
            if layers > 1:
                sp.wait_ge(s("state_stored"), 32)
            sp.wait_ge(s("stored"), 32)

        mm = nc.tensor.matmul
        tr = nc.tensor.transpose

        def pe_gla(pe, arrived, ada_at, norm, h_ready, project, residual):
            norm(2)
            pe.wait_ge(s("cm1_loaded"), 16 * 4)
            for k in range(KD):
                h_ready(2, k)
                last = mm(bank[4][0:32, 0:NT], wg1[:, k, :], hT[:, k].rearrange("p g t -> p (g t)"),
                          start=k == 0, stop=k == KD - 1)
            last.then_inc(s("gk1_mm"), 1)
            for w, name in enumerate(("wq", "wk")):
                slot = arrived((name, 0))
                for h in range(HEADS):
                    w8 = piece(slot, KD, 512)
                    for k in range(KD):
                        last = mm(half(4 * w + h), w8[:, k, h * P:h * P + P], hT[:, k].rearrange("p g t -> p (g t)"),
                                  start=k == 0, stop=k == KD - 1)
                    if h % 2:
                        last.then_inc(s("gla_proj"), 1)
                if w == 0:
                    gates(pe, 0)
                    ada_at("queries")
            for h in range(2):
                slot = arrived(("wv", h))
                for g in range(G):
                    b = (2 * h + g) % 4
                    pe.wait_ge(s("qk_ready"), 1 + b)
                    for k in range(KD):
                        last = mm(bank[b][:], hT[:, k, g], piece(slot, KD, 512)[:, k, :], start=k == 0, stop=k == KD - 1)
                    last.then_inc(s("gla_proj"), 1)
            gates(pe, 1)
            ada_at("values")
            pe.wait_ge(s("v_ready"), 4)
            for m in range(4):
                mm(bank[m][:], zeros[:], zeros[:, 0:1].broadcast_to([P, 512]), start=True, stop=False,
                   skip_group_check=True)

            def g_tiles(first, end, after):
                pe.wait_ge(s("mod_ready"), adas_until(after, layers))
                for m in range(first, end):
                    slot = arrived(("wg", m // 4))
                    if m == 3:
                        pe.wait_ge(s("kdr_ready"), 2)
                    if m:
                        pe.wait_ge(s("g_raw"), m - 1 if 3 <= m < 7 else m)
                    project(bank[g_bank(m)][:, 0:NT], slot, m % 4, "gla_proj")

            def k_rows(d):
                pe.wait_ge(s("kd_ready"), d + 1)
                for g in range(G):
                    if g or d:
                        pe.wait_ge(s("kdr_ready"), 2 * d + g)
                    for h in range(HEADS):
                        last = tr(bank[6][:, h * P:h * P + P], kdT[:, h, g], ident)
                    last.then_inc(s("kd_tr"), 1)

            g_tiles(0, 1, "values")
            for d in range(2):
                pe.wait_ge(s("qke_ready"), 2 * d + 2)
                pe.wait_ge(s("upd_read"), 3 * d) if d else pe.wait_ge(s("gate_x"), 2)
                for g in range(G):
                    for h in range(HEADS):
                        last = mm(bank[4 + g][:, h * P:h * P + P], ke[:, h, g], qe[:, h, g])
                    last.then_inc(s("scores_mm"), 1)
                if d == 0:
                    k_rows(0)
                    g_tiles(1, 2, "values")
                else:
                    g_tiles(7, 8, "between")
                for g in range(G):
                    pe.wait_ge(s("sc_ready"), 2 * d + g + 1)
                    for m in range(KD):
                        last = mm(half(m)[:, g * L:g * L + L], vrow[:, g, m * P:m * P + P], sc[:, g, m // 2, :],
                                  start=False, stop=False, skip_group_check=True)
                last.then_inc(s("intra_mm"), 1)
                pe.wait_ge(s("kdr_ready"), 2 * d + 2)
                pe.wait_ge(s("s0_loaded"), 32)
                steps = (((1, d), (1, d, s0[:, d])), ((0, d), (1, 1 - d, s1l)), ((0, 1 - d), (0, 1 - d, s1c)))
                for n, ((g, c), (gi, ci, st)) in enumerate(steps):
                    if n:
                        pe.wait_ge(s("upd_read"), 3 * d + n)
                    for h in range(HEADS):
                        last = mm(bank[4 + h // 2][:, (h % 2) * DV:(h % 2) * DV + DV],
                                  kdr[c * CH:c * CH + CH, g, h, :], vrow[c * CH:c * CH + CH, g, h * DV:h * DV + DV])
                    last.then_inc(s("upd_mm"), 1)
                    for m in range(KD):
                        last = mm(half(m)[:, gi * L + ci * CH:gi * L + ci * CH + CH],
                                  st[:, m // 2, (m % 2) * P:(m % 2) * P + P], qe[:, m // 2, gi, ci * CH:ci * CH + CH],
                                  start=False, stop=False, skip_group_check=True)
                last.then_inc(s("o_mm"), 1)
                if d == 0:
                    g_tiles(2, 7, "values")
                    pe.wait_ge(s("g_raw"), 6)
                    k_rows(1)
                    pe.wait_ge(s("g_raw"), 7)
                    ada_at("between")
            pe.wait_ge(s("g_raw"), 8)
            ada_at("heads")
            pe.wait_ge(s("upd_read"), 6)
            for h in range(HEADS):
                pe.wait_ge(s("osq_ready"), h + 1)
                dst = bank[4 + h // 2][:, (h % 2) * NT:(h % 2) * NT + NT]
                for t in range(2):
                    last = mm(dst, ones[:], osq[:, 2 * h + t], start=t == 0, stop=t == 1)
                if h % 2:
                    last.then_inc(s("osum_mm"), 1)
            residual(1, "wo", oT, lambda k: pe.wait_ge(s("o_ready"), k + 1))

        def gates(pe, d):
            if d == 0:
                pe.wait_ge(s("gk1_ready"), 1)
            else:
                pe.wait_ge(s("gate_x"), 1)
            for h in range(HEADS):
                last = mm(bank[4 + h // 2][:, (h % 2) * NT:(h % 2) * NT + NT], wg2[0:32, d, h * P:h * P + P],
                          gk1[0:32, :])
            last.then_inc(s("gate_mm"), 1)

        @block.tensor
        def _(pe):
            reg = fb_count(pe, "pe_extra_pairs")

            def arrived(what):
                slot, nth = where[what]
                pe.wait_ge(s(f"full{slot}"), 16 * (nth + 1))
                return slot

            def ada(i, q):
                n = 3 * i + q
                if n:
                    pe.wait_ge(s("mod_ready"), n)
                slots = [arrived(("ada", i, q, j)) for j in range(4)]
                for k in range(KD):
                    for j in range(4):
                        last = mm(bank[7][32 * j:32 * j + 32, :], condT[:, k, :], piece(slots[j], KD, 512)[:, k, :],
                                  start=k == 0, stop=k == KD - 1)
                last.then_inc(s("ada_mm"), 1)
                pe.wait_ge(s("ada_rows"), n + 1)
                for t in range(4):
                    last = tr(bank[7][:, t * P:t * P + P], rows[:, t * P:t * P + P], ident)
                last.then_inc(s("ada_tr"), 1)

            def ada_at(point):
                for n in ADA_AT[point]:
                    if n < 3 * layers:
                        ada(n // 3, n % 3)

            def sum_squares(n, k):
                pe.wait_ge(s("squares"), KD * n + k + 1)
                ins = mm(bank[6][:, 0:NT], ones[:], hT[:, k].rearrange("p g t -> p (g t)"),
                         start=k == 0, stop=k == KD - 1)
                if k == KD - 1:
                    ins.then_inc(s("square_sum"), 1)

            def norm(n):
                for k in range(KD):
                    sum_squares(n, k)

            def h_ready(n, k):
                pe.wait_ge(s("h0_ready"), KD * n + k + 1)
                pe.wait_ge(s("h1_ready"), KD * n + k + 1)

            def project(dst, slot, t, done, rhs=None, ready=None):
                w = piece(slot, KD, 512)
                for k in range(KD):
                    if ready:
                        ready(k)
                    last = mm(dst, w[:, k, t * P:t * P + P],
                              (hT[:, k] if rhs is None else rhs[:, k]).rearrange("p g t -> p (g t)"),
                              start=k == 0, stop=k == KD - 1)
                last.then_inc(s(done), 1)

            def residual(i, name, rhs, ready=None):
                for m in range(KD):
                    if m % 4 == 0:
                        slot = arrived((name, m // 4))
                    if m >= 4:
                        pe.wait_ge(s("y_biased"), KD * i + m - 3)
                    project(bank[m % 4][:, 0:NT], slot, m % 4, "res_mm", rhs, ready if m == 0 else None)
                    if m:
                        sum_squares(2 * i + 1, m - 1)
                sum_squares(2 * i + 1, KD - 1)

            def moe_round(pre, b, i):
                nbase = moe_uses[i] if pre == "" else None

                def filled(n, p):
                    slot = moe_slots[i][n]
                    if pre == "":
                        pe.wait_ge(s(f"full{slot}"), (p + (nbase[n] + 1)) * 16)
                    else:
                        pe.wait_ge(s(f"fb_full{n}"), (b + p + 1) * 16)

                def gather(p1):
                    for k in range(KD):
                        for g in range(G):
                            last = mm(bank[6 + k // 4][:, (k % 4) * P:(k % 4) * P + P], htok[:, g, k * P:k * P + P],
                                      sel[:, g].rearrange("p e n -> p (e n)"), start=g == 0, stop=g == G - 1)
                    last.then_inc(s(pre + "gathered"), 1)

                def pair(p, more):
                    n = b + p
                    pe.wait_ge(s(pre + "xg_ready"), n * 2 + 2)
                    pe.wait_ge(s(pre + "hidT_ready"), n)
                    for kind, done in ((0, "h1_mm"), (1, "h3_mm")):
                        if kind == 1:
                            pe.wait_ge(s(pre + "selT_ready"), n)
                        filled(2 * kind, p)
                        filled(2 * kind + 1, p)
                        for k in range(KD):
                            for e in range(2):
                                last = mm(bank[4 + kind][SLOTS * e:SLOTS * e + SLOTS, :],
                                          xg[:, k, SLOTS * e:SLOTS * e + SLOTS],
                                          piece(moe_slots[i][2 * kind + e], KD, FF)[:, k, :], start=k == 0, stop=k == KD - 1)
                        last.then_inc(s(pre + done), 1)
                    if more:
                        pe.wait_ge(s(pre + "sel_ready"), n + 2)
                        pe.wait_ge(s(pre + "yv_lo"), n)
                        pe.wait_ge(s(pre + "yv_hi"), n)
                        gather(None)
                    pe.wait_ge(s(pre + "hid_ready"), n + 1)
                    for f in range(4):
                        last = tr(bank[4][:, f * P:f * P + P], hid[:, f * P:f * P + P], ident)
                    last.then_inc(s(pre + "hidT_mm"), 1)
                    pe.wait_ge(s(pre + "selw_ready"), n + 1)
                    for g in range(G):
                        last = tr(bank[5][:, g * P:g * P + P], selw[:, g].rearrange("p e n -> p (e n)"), ident)
                    last.then_inc(s(pre + "selT_mm"), 1)
                    pe.wait_ge(s(pre + "hidT_ready"), n + 1)
                    if more:
                        pe.wait_ge(s(pre + "xg_ready"), n * 2 + 4)
                    filled(4, p)
                    filled(5, p)
                    for h in range(2):
                        for f in range(4):
                            for e in range(2):
                                last = mm(bank[6 + h][SLOTS * e:SLOTS * e + SLOTS, :],
                                          hidT[:, f, SLOTS * e:SLOTS * e + SLOTS],
                                          piece(moe_slots[i][4 + e], 4, D)[:, f, h * 512:h * 512 + 512], start=f == 0, stop=f == 3)
                        last.then_inc(s(pre + "y_mm"), 1)
                    pe.wait_ge(s(pre + "selT_ready"), n + 1)
                    for m in range(KD):
                        if m % 4 == 0:
                            pe.wait_ge(s(pre + ("yv_hi" if m else "yv_lo")), n + 1)
                        last = mm(half(m), yv[:, m * P:m * P + P], selT[:], start=False, stop=False,
                                  skip_group_check=True)
                        if m in (1, 3, 5) and not more:
                            last.then_inc(s(pre + "summed"), 1)
                    last.then_inc(s(pre + "scattered"), 1)

                for m in range(4):
                    mm(bank[m][:], zeros[:], zeros[:, 0:1].broadcast_to([P, 512]), start=True, stop=False, skip_group_check=True)
                pe.wait_ge(s(pre + "sel_ready"), b + 1)
                gather(None)
                with pe.Fori(0, PAIRS - 1) as p:
                    pair(p, True)
                pair(PAIRS - 1, False)

            def moe(i):
                pe.wait_ge(s("rw_loaded"), 32 * (i + 1))
                for k in range(KD):
                    h_ready(2 * i + 1, k)
                    last = mm(bank[4][0:20, 0:NT], rw[:, k, :], hT[:, k].rearrange("p g t -> p (g t)"),
                              start=k == 0, stop=k == KD - 1)
                last.then_inc(s("logits_mm"), 1)
                for g in range(G):
                    for k in range(KD):
                        last = tr(bank[2 * g + k // 4][:, (k % 4) * P:(k % 4) * P + P], hT[:, k, g], ident)
                    if g == 0:
                        last.then_inc(s("htok_tr"), 1)
                        pe.wait_ge(s("logits"), i + 1)
                        for gg in range(G):
                            lt = tr(bank[5][:, gg * 32:gg * 32 + 20], lraw[0:20, gg * P:gg * P + P], ident[0:20, 0:20])
                        lt.then_inc(s("logits_tr"), 1)
                last.then_inc(s("htok_tr"), 1)
                pe.wait_ge(s("members"), i + 1)
                mb = [memb[:, g, :] for g in range(G)]
                mm(bank[4][:, 0:16], upper16[:], mb[0], start=True, stop=True)
                mm(bank[4][:, 16:32], upper16[:], mb[1], start=True, stop=False)
                mm(bank[4][:, 16:32], ones16[:], mb[0], start=False, stop=True)
                mm(bank[4][:, 32:48], ones16[:], mb[0], start=True, stop=False)
                mm(bank[4][:, 32:48], ones16[:], mb[1], start=False, stop=True).then_inc(s("ranks_mm"), 1)
                pe.wait_ge(s("htok_ready"), 2 * (i + 1))
                moe_round("", PAIRS * i, i)
                rounds = needed_rounds(pe, i)

                def one_round(b):
                    pe.wait_ge(s("x_added"), KD * (2 * i + 2))
                    pe.wait_ge(s("fb_rounds_added"), b // PAIRS)
                    moe_round("fb_", b, i)

                further_rounds(pe, i, rounds, reg, one_round)

            pe.wait_ge(s("base_loaded"), 16)
            pe.wait_ge(s("vrows_loaded"), 16 * len(vec_layout()))
            for t in range(4):
                last = tr(bank[4][:, t * P:t * P + P], vrows[:, t, :], ident)
            last.then_inc(s("vec_tr"), 1)
            pe.wait_ge(s("x_loaded"), 32)
            for k in range(KD):
                for g in range(G):
                    last = tr(half(k)[:, g * L:g * L + L], xin[:, g, k * P:k * P + P], ident)
                if k % 2:
                    last.then_inc(s("x_tr"), 1)

            dft = [cm[:, n * P:n * P + P] for n in range(9)]
            FRE, FIM, KFI, KBR, KBI, KFD, KBD, IRE, IIM = dft
            pe.wait_ge(s("filter_loaded"), 16 * 3)
            mm(bank[5][0:HY_HID, 0:L], fsmall[0:HY_EMB, 1, 0:HY_HID], fsmall[0:HY_EMB, 0, :]).then_inc(s("f_mm"), 1)
            pe.wait_ge(s("f_sin"), 1)
            mm(bank[5][0:HY_HID, 0:L], fsmall[0:HY_HID, 2, 0:HY_HID], fsmall[0:HY_HID, 4, :]).then_inc(s("f_mm"), 1)
            pe.wait_ge(s("f_sin"), 2)
            pe.wait_ge(s("w3_loaded"), 32)
            for c in range(8):
                if c >= 2:
                    pe.wait_ge(s("kfb_ready"), c - 1)
                mm(bank[4 + c % 2][:], fsmall[0:HY_HID, 5, :], w3f[0:HY_HID, c * 512:c * 512 + 512]) \
                    .then_inc(s("f3_mm"), 1)
            pe.wait_ge(s("kfb_ready"), 8)
            pe.wait_ge(s("dft_loaded"), 16)
            pe.wait_ge(s("x_copied"), 4)
            norm(0)

            def spectra(w):
                mf, mb_ = ((FRE, KBR), (KFI, KBI), (KFD, KBD))[w]
                for o in range(HY_ORDER):
                    for h in range(2):
                        c = (w * HY_ORDER + o) * 2 + h
                        if c >= 4:
                            pe.wait_ge(s("spec_ready"), c - 3)
                        mm(bank[c % 4][:], mf, kfb[:, 0, o, h * 512:h * 512 + 512], start=True, stop=False)
                        mm(bank[c % 4][:], mb_, kfb[:, 1, o, h * 512:h * 512 + 512], start=False, stop=True) \
                            .then_inc(s("spec_mm"), 1)

            for w in range(3):
                spectra(w)
            pe.wait_ge(s("cond_ready"), 3)
            ada_at("start")
            pe.wait_ge(s("spec_ready"), 12)
            for m in range(24):
                if m % 4 == 0:
                    slot = arrived(("w_in", m // 4))
                if m >= 4:
                    pe.wait_ge(s("up_ready"), m - 3)
                project(bank[m % 4][:, 0:NT], slot, m % 4, "win_mm",
                        ready=(lambda k: h_ready(0, k)) if m == 0 else None)
                if m in (7, 15):
                    ada_at(f"w_in{m // 4}")
            pe.wait_ge(s("up_ready"), 24)

            def to_rows(n):
                if n < 2:
                    pe.wait_ge(s("conv_ready"), 8)
                if n:
                    pe.wait_ge(s("zt_ready"), 2 * n)
                if n > 1:
                    pe.wait_ge(s("z_ready"), n - 1)
                for k in range(KD):
                    last = tr(bank[4 + k // 4][:, (k % 4) * P:(k % 4) * P + P], uT[:, k, n % G], ident)
                last.then_inc(s("zt_tr"), 1)

            def forward(n):
                pe.wait_ge(s("zt_ready"), 2 * n + 2)
                if n:
                    pe.wait_ge(s("prods"), 4 * n)
                for w, f in enumerate((FRE, FIM)):
                    for h in range(2):
                        last = mm(bank[2 * w + h][:], f, zt[:, n % G, h * 512:h * 512 + 512])
                last.then_inc(s("zf_mm"), 1)

            def inverse(n):
                pe.wait_ge(s("yspec"), 2 * n + 2)
                pe.wait_ge(s("zt_ready"), min(2 * n + 4, 8))
                if n:
                    pe.wait_ge(s("z_ready"), n)
                for k in range(KD):
                    dst = bank[4 + k // 4][:, (k % 4) * P:(k % 4) * P + P]
                    mm(dst, ysp[:, 0, k * P:k * P + P], IRE, start=True, stop=False)
                    last = mm(dst, ysp[:, 1, k * P:k * P + P], IIM, start=False, stop=True)
                last.then_inc(s("zi_mm"), 1)

            to_rows(0)
            ada_at("w_in5")
            forward(0)
            to_rows(1)
            ada_at("conv0")
            forward(1)
            inverse(0)
            to_rows(2)
            forward(2)
            inverse(1)
            to_rows(3)
            ada_at("conv1")
            forward(3)
            inverse(2)
            ada_at("conv2")
            inverse(3)
            pe.wait_ge(s("z_ready"), 4)
            residual(0, "w_out", rhs=uT)
            moe(0)

            if layers > 1:
                pe_gla(pe, arrived, ada_at, norm, h_ready, project, residual)
                moe(1)

            if layers > 2:
                norm(4)
                pe.wait_ge(s("cm2_loaded"), 16)
                cg, cl, sl = cm[:, 0:1024].rearrange("p (k n) -> p k n", k=2), cm[:, 1024:1152], cm[:, 1152:1280]
                for g in range(G):
                    for r in range(4):
                        n = 4 * g + r
                        if n >= 4:
                            pe.wait_ge(s("fn_rows"), n - 3)
                        for k in range(2):
                            if g == 0:
                                h_ready(4, 2 * r + k)
                            last = mm(bank[n % 4][:], hT[:, 2 * r + k, g], cg[:, k, :], start=k == 0, stop=k == 1)
                        last.then_inc(s("fn_ch_mm"), 1)
                ada_at("fnet")
                pe.wait_ge(s("fn_rows"), 8)
                for m in range(KD):
                    for g in range(G):
                        dst = half(m)[:, g * L:g * L + L]
                        rws = fnp[:, g, m // 2]
                        mm(dst, rws[:, (m % 2) * P:(m % 2) * P + P], cl, start=True, stop=False)
                        last = mm(dst, rws[:, 256 + (m % 2) * P:256 + (m % 2) * P + P], sl, start=False, stop=True)
                    if m % 2:
                        last.then_inc(s("fn_tok_mm"), 1)
                pe.wait_ge(s("fn_mixed"), 4)
                residual(2, "fn", rhs=fnm)
                moe(2)

            if layers > 3:
                norm(6)
                slot = arrived(("pool", 0))
                pe.wait_ge(s("cm3_loaded"), 16)
                pw = piece(slot, KD, 256)
                for g in range(G):
                    for r in range(4):
                        n = 4 * g + r
                        dst = bank[n // 2][:, (n % 2) * 256:(n % 2) * 256 + 256]
                        for k in range(2):
                            if g == 0:
                                h_ready(6, 2 * r + k)
                            last = mm(dst, hT[:, 2 * r + k, g], pw[:, 2 * r + k, :], start=k == 0, stop=k == 1)
                        if r % 2:
                            last.then_inc(s("pool_hw"), 1)
                pe.wait_ge(s("pool_rows"), 4)
                for m in range(KD):
                    for g in range(G):
                        last = mm(half(m)[:, g * L:g * L + L], plr[:, g, m // 2, (m % 2) * P:(m % 2) * P + P],
                                  cm[:, (4 * g + m // 2) * P:(4 * g + m // 2) * P + P])
                    last.then_inc(s("res_mm"), 1)
                    if m:
                        sum_squares(7, m - 1)
                sum_squares(7, KD - 1)
                moe(3)

            norm(2 * layers)
            for g in range(G):
                pe.wait_ge(s("final_ready"), g + 1)
                for k in range(KD):
                    last = tr(bank[2 * g + k // 4][:, (k % 4) * P:(k % 4) * P + P], hT[:, k, g], ident)
                last.then_inc(s("out_tr"), 1)

        @block.scalar
        def _(act):
            reg = fb_count(act, "act_extra_pairs")
            act_fn = nc.scalar.activation
            chained = [0]

            def chain(ins):
                chained[0] += 1
                ins.then_inc(s("act_chain"), 1)
                act.wait_ge(s("act_chain"), chained[0])

            act.dma_start(base[:], a["c_base"]).then_inc(s("base_loaded"), 16)
            act.wait_ge(s("vrows_clear"), 1)
            vector_loads(act, 0)
            act.dma_start(upper, a["c_upper"]).then_inc(s("upper_loaded"), 16)

            def square(n, k):
                if n:
                    act.wait_ge(s("x_added"), KD * (n - 1) + k + 1)
                else:
                    act.wait_ge(s("x_copied"), k // 2 + 1)
                act_fn(hT[:, k], xT[:, k], ACT.Square).then_inc(s("squares"), 1)

            def load_table(fn):
                act_fn(small[:, 2:3], one, fn)

            def inverse_root(n):
                act.wait_ge(s("square_sum"), n + 1)
                chain(act_fn(rstd[:].rearrange("p g t -> p (g t)"), bank[6][:, 0:NT], ACT.Ln, bias=eps, scale=1.0 / D))
                act_fn(rstd[:], rstd[:], ACT.Exp, scale=-0.5).then_inc(s("rstd_ready"), 1)

            def norm(n):
                load_table(ACT.Ln)
                for k in range(KD):
                    square(n, k)
                inverse_root(n)

            def shift(n):
                i, w = n // 2, n % 2
                for k in range(KD):
                    act.wait_ge(s("normed"), KD * n + k + 1)
                    act_fn(hT[:, k, 0], hT[:, k, 0], ACT.Identity, bias=mod[:, i, 24 * w + k, 0:1],
                           scale=scale[:, i, w, k, 0:1]).then_inc(s("h0_ready"), 1)

            def residual(i, bias, src):
                for m in range(KD):
                    act.wait_ge(s("res_mm"), KD * i + m + 1 if i < 3 else KD * i + (m | 1) + 1)
                    if m >= 4:
                        act.wait_ge(s("x_added"), KD * 2 * i + m - 3)
                    ins = dict(bias=vcol(bias, m)) if bias else {}
                    act_fn(yb[:, m % 4], src(m), ACT.Identity, **ins).then_inc(s("y_biased"), 1)
                    if m == 0:
                        load_table(ACT.Ln)
                    square(2 * i + 1, m)

            quarter = lambda m: bank[m % 4][:, 0:NT]

            def evac(pre, n):
                act.wait_ge(s(pre + "gathered"), n + 1)
                for h in range(2):
                    act_fn(xg[:, 4 * h:4 * h + 4], psum_tok(6 + h, 4), ACT.Copy).then_inc(s(pre + "xg_ready"), 1)

            def moe_round(pre, b):
                def pair(p, more):
                    n = b + p
                    act.wait_ge(s(pre + "h1_mm"), n + 1)
                    act.wait_ge(s(pre + "hid_ready"), n)
                    act_fn(sil[:], bank[4][:], ACT.Silu).then_inc(s(pre + "sil_ready"), 1)
                    if more:
                        evac(pre, n + 1)
                    act.wait_ge(s(pre + "selT_mm"), n + 1)
                    act.wait_ge(s(pre + "scattered"), n)
                    act_fn(selT[:], bank[5][:, 0:NT], ACT.Copy).then_inc(s(pre + "selT_ready"), 1)
                    act.wait_ge(s(pre + "y_mm"), n * 2 + 1)
                    act_fn(yv[:, 0:512], bank[6][:], ACT.Copy).then_inc(s(pre + "yv_lo"), 1)

                evac(pre, b)
                with act.Fori(0, PAIRS - 1) as p:
                    pair(p, True)
                pair(PAIRS - 1, False)

            def moe(i):
                inverse_root(2 * i + 1)
                shift(2 * i + 1)
                act.wait_ge(s("logits_mm"), i + 1)
                act_fn(lraw[0:20, :], bank[4][0:20, 0:NT], ACT.Copy).then_inc(s("logits"), 1)
                for g in range(G):
                    act.wait_ge(s("htok_tr"), 2 * i + g + 1)
                    for h in range(2):
                        last = act_fn(htok[:, g, h * 512:h * 512 + 512], bank[2 * g + h][:], ACT.Copy)
                    last.then_inc(s("htok_ready"), 1)
                    act.wait_ge(s("route_in"), 2 * i + g + 1)
                    act_fn(*route_exp[g], ACT.Exp).then_inc(s("route_exp"), 1)
                moe_round("", PAIRS * i)
                rounds = needed_rounds(act, i)

                def one_round(b):
                    act.wait_ge(s("x_added"), KD * (2 * i + 2))
                    act.wait_ge(s("fb_rounds_added"), b // PAIRS)
                    moe_round("fb_", b)
                    act.wait_ge(s("fb_rounds_added"), b // PAIRS + 1)

                further_rounds(act, i, rounds, reg, one_round)

            act.wait_ge(s("vec_ready"), 1)
            act.wait_ge(s("cond_ready"), 1)
            for g, name in enumerate(("c_ctx", "c")):
                act_fn(condT[:, :, g], vcol(name, 0, KD), ACT.Silu).then_inc(s("cond_ready"), 1)
            for n in range(2):
                act.wait_ge(s("f_arg"), n + 1)
                act_fn(fsmall[0:HY_HID, 4 + n, :], fsmall[0:HY_HID, 3, :], ACT.Sin).then_inc(s("f_sin"), 1)

            def spectrum(c):
                act.wait_ge(s("spec_mm"), c + 1)
                act_fn(spec[:, c // 4, (c // 2) % 2, (c % 2) * 512:(c % 2) * 512 + 512], bank[c % 4][:], ACT.Copy) \
                    .then_inc(s("spec_ready"), 1)

            norm(0)
            for c in range(12):
                spectrum(c)
            shift(0)
            act.wait_ge(s("up_clear"), 1)
            for m in range(24):
                act.wait_ge(s("win_mm"), m + 1)
                if m >= 4:
                    act.wait_ge(s("conv_ready"), m - 3)
                act_fn(up[:, m % 4, :, 1:L + 1], bank[m % 4][:, 0:NT].rearrange("p (g t) -> p g t", g=G), ACT.Identity,
                       bias=vcol("hy_b_in", m)).then_inc(s("up_ready"), 1)
            for n in range(4):
                act.wait_ge(s("zt_tr"), n + 1)
                for h in range(2):
                    act_fn(zt[:, n % 2, h * 512:h * 512 + 512], bank[4 + h][:], ACT.Copy).then_inc(s("zt_ready"), 1)
            residual(0, "hy_b_out", quarter)
            moe(0)
            if layers > 1:
                norm(2)
                shift(2)
                for b in range(2):
                    act.wait_ge(s("gla_proj"), b + 1)
                    act_fn(qT[:, 2 * b:2 * b + 2], bank[b][:].rearrange("p (h g t) -> p h g t", h=2, g=G),
                           ACT.Copy, scale=DK ** -0.5).then_inc(s("qk_ready"), 1)

                def gate_logs(d):
                    act.wait_ge(s("gate_mm"), d + 1)
                    if d:
                        act.wait_ge(s("kd_ready"), 1)
                    for h in range(HEADS):
                        last = act_fn(gx[:, h * NT:h * NT + NT], bank[4 + h // 2][:, (h % 2) * NT:(h % 2) * NT + NT],
                                      ACT.Identity, bias=vcol("gla_b_gk", 4 * d + h))
                    last.then_inc(s("gate_x"), 1)
                    act.wait_ge(s("gate_x"), d + 1)
                    chain(act_fn(gt[:], gx[:], ACT.Abs))
                    chain(act_fn(gt[:], gt[:], ACT.Exp, scale=-1.0))
                    act_fn(gt[:], gt[:], ACT.Ln, bias=one).then_inc(s("gate_ln"), 1)

                def gate_k(d):
                    act.wait_ge(s("gate_cum"), 2 * d + 1)
                    act_fn(e2[:], gt[:], ACT.Exp, scale=-1.0 / 16).then_inc(s("k_exp"), 1)
                    act.wait_ge(s("gate_cum"), 2 * d + 2)
                    act_fn(gx[:], gx[:], ACT.Exp, scale=1.0 / 16).then_inc(s("k_exp"), 1)

                def gate_q(d):
                    if d:
                        act.wait_ge(s("upd_read"), 3)
                    act_fn(e1[:], gt[:], ACT.Exp, scale=1.0 / 16).then_inc(s("q_exp"), 1)

                def k_rows(d):
                    for g in range(G):
                        act.wait_ge(s("kd_tr"), 2 * d + g + 1)
                        act_fn(kdr[:, g], psum_tok(6, 4), ACT.Copy).then_inc(s("kdr_ready"), 1)

                def g_tiles(first, end):
                    for m in range(first, end):
                        act.wait_ge(s("gla_proj"), 9 + m)
                        act_fn(gT[:, m], bank[g_bank(m)][:, 0:NT], ACT.Copy).then_inc(s("g_raw"), 1)

                gate_logs(0)
                for b in range(2, 4):
                    act.wait_ge(s("gla_proj"), b + 1)
                    act_fn(kT[:, 2 * b - 4:2 * b - 2], bank[b][:].rearrange("p (h g t) -> p h g t", h=2, g=G),
                           ACT.Copy).then_inc(s("qk_ready"), 1)
                gate_k(0)
                gate_q(0)
                for n in range(4):
                    act.wait_ge(s("gla_proj"), 5 + n)
                    act_fn(vrow[:, n % 2, (n // 2) * 512:(n // 2) * 512 + 512], bank[n][:], ACT.Copy) \
                        .then_inc(s("v_ready"), 1)
                gate_logs(1)
                g_tiles(0, 1)
                k_rows(0)
                g_tiles(1, 2)
                gate_k(1)
                gate_q(1)
                g_tiles(2, 7)
                k_rows(1)
                g_tiles(7, 8)
                act.wait_ge(s("g_raw"), 8)
                act_fn(gT, gT, ACT.Silu).then_inc(s("g_ready"), 1)
                load_table(ACT.Ln)
                act.wait_ge(s("o_mm"), 2)
                for b in range(4):
                    act_fn(osq[:, 2 * b:2 * b + 2], bank[b][:].rearrange("p (h t) -> p h t", h=2), ACT.Square) \
                        .then_inc(s("osq_ready"), 1)
                for b in range(2):
                    act.wait_ge(s("osum_mm"), b + 1)
                    o_root = ors[:, 2 * b:2 * b + 2].rearrange("p h t -> p (h t)")
                    last = act_fn(o_root, bank[4 + b][:], ACT.Ln, bias=eps, scale=1.0 / DV)
                chain(last)
                for b in range(2):
                    o_root = ors[:, 2 * b:2 * b + 2].rearrange("p h t -> p (h t)")
                    act_fn(o_root, o_root, ACT.Exp, scale=-0.5).then_inc(s("ors_ready"), 1)
                residual(1, None, quarter)
                moe(1)
            if layers > 2:
                norm(4)
                shift(4)
                for n in range(8):
                    act.wait_ge(s("fn_ch_mm"), n + 1)
                    act_fn(fnp[:, n // 4, n % 4], bank[n % 4][:], ACT.Copy).then_inc(s("fn_rows"), 1)
                for b in range(4):
                    act.wait_ge(s("fn_tok_mm"), b + 1)
                    act_fn(fnm[:, 2 * b:2 * b + 2], bank[b][:].rearrange("p (h g t) -> p h g t", h=2, g=G), ACT.Copy) \
                        .then_inc(s("fn_mixed"), 1)
                residual(2, "fn_b_out", quarter)
                moe(2)
            if layers > 3:
                norm(6)
                shift(6)
                for b in range(4):
                    act.wait_ge(s("pool_hw"), b + 1)
                    act_fn(plr[:, b // 2, 2 * (b % 2):2 * (b % 2) + 2], bank[b][:].rearrange("p (r n) -> p r n", r=2),
                           ACT.Copy).then_inc(s("pool_rows"), 1)
                residual(3, "pool_b", half)
                moe(3)
            norm(2 * layers)

        @block.vector
        def _(dve):
            reg = fb_count(dve, "dve_extra_pairs")
            v = nc.vector
            tt, ts, stt = v.tensor_tensor, v.tensor_scalar, v.scalar_tensor_tensor
            chained = [0]

            def chain(ins):
                chained[0] += 1
                ins.then_inc(s("dve_chain"), 1)
                dve.wait_ge(s("dve_chain"), chained[0])

            def ada(i, q):
                n = 3 * i + q
                dve.wait_ge(s("ada_mm"), n + 1)
                v.tensor_copy(rows[:], bank[7][:]).then_inc(s("ada_rows"), 1)
                dve.wait_ge(s("ada_tr"), n + 1)
                src = bank[7][:].rearrange("p (t j r) -> p j t r", t=4, j=4)[:, :, :, 0:G]
                dst = mod[:, i, 16 * q:16 * q + 16].rearrange("p (j t) g -> p j t g", j=4)
                bia = b_ada(i, 16 * q, 16).rearrange("p (j t) -> p j t", j=4).unsqueeze(3).broadcast_to([P, 4, 4, G])
                tt(dst, src, bia, ALU.add).then_inc(s("mod_ready"), 1)
                dve.wait_ge(s("mod_ready"), n + 1)
                if q != 1:
                    w = q // 2
                    ng = vcol("norm_g", 16 * i + 8 * w, KD).unsqueeze(2).broadcast_to([P, KD, G])
                    chain(stt(scale[:, i, w], mod[:, i, 24 * w + 8:24 * w + 16], 1.0, ng, ALU.add, ALU.mult))

            def ada_at(point):
                for n in ADA_AT[point]:
                    if n < 3 * layers:
                        ada(n // 3, n % 3)

            def norm(n):
                i, w = n // 2, n % 2
                dve.wait_ge(s("rstd_ready"), n + 1)
                for k in range(KD + 1):
                    if k < KD:
                        tt(hT[:, k], xT[:, k], rstd[:], ALU.mult).then_inc(s("normed"), 1)
                    if k:
                        dve.wait_ge(s("normed"), KD * n + k)
                        ts(hT[:, k - 1, 1], hT[:, k - 1, 1], scale[:, i, w, k - 1, 1:2],
                           mod[:, i, 24 * w + k - 1, 1:2], ALU.mult, ALU.add).then_inc(s("h1_ready"), 1)

            def residual(i, gate):
                for m in range(KD):
                    dve.wait_ge(s("y_biased"), KD * i + m + 1)
                    for g in range(G):
                        last = stt(xT[:, m, g], yb[:, m % 4, g * L:g * L + L], gate(m, g), xT[:, m, g],
                                   ALU.mult, ALU.add)
                    last.then_inc(s("x_added"), 1)

            g1 = lambda i: lambda m, g: mod[:, i, 16 + m, g:g + 1]

            def build_sel(pre, n, p):
                r = rank[:, :, bass.ds(p * 2, 2)].unsqueeze(3).broadcast_to([P, G, 2, SLOTS])
                io = iota.unsqueeze(1).unsqueeze(1).broadcast_to([P, G, 2, SLOTS])
                tt(sel[:], io, r, ALU.is_equal).then_inc(s(pre + "sel_ready"), 1)

            def moe_round(pre, b, i):
                def pair(p, more):
                    n = b + p
                    dve.wait_ge(s(pre + "sel_ready"), n + 1)
                    dve.wait_ge(s(pre + "selT_mm"), n)
                    c = comb[:, :, bass.ds(p * 2, 2)].unsqueeze(3).broadcast_to([P, G, 2, SLOTS])
                    tt(selw[:], sel[:], c, ALU.mult).then_inc(s(pre + "selw_ready"), 1)
                    if more:
                        dve.wait_ge(s(pre + "gathered"), n + 1)
                        dve.wait_ge(s(pre + "selw_ready"), n + 1)
                        build_sel(pre, n + 1, p + 1)
                    dve.wait_ge(s(pre + "sil_ready"), n + 1)
                    dve.wait_ge(s(pre + "h3_mm"), n + 1)
                    dve.wait_ge(s(pre + "hidT_mm"), n)
                    tt(hid[:], sil[:], bank[5][:], ALU.mult).then_inc(s(pre + "hid_ready"), 1)
                    dve.wait_ge(s(pre + "hidT_mm"), n + 1)
                    dve.wait_ge(s(pre + "y_mm"), n * 2)
                    v.tensor_copy(hidT[:], psum_tok(4, 4)).then_inc(s(pre + "hidT_ready"), 1)
                    dve.wait_ge(s(pre + "y_mm"), n * 2 + 2)
                    dve.wait_ge(s(pre + "scattered"), n)
                    v.tensor_copy(yv[:, 512:1024], bank[7][:]).then_inc(s(pre + "yv_hi"), 1)

                if pre:
                    build_sel(pre, b, 0)
                with dve.Fori(0, PAIRS - 1) as p:
                    pair(p, True)
                pair(PAIRS - 1, False)
                for m in range(KD):
                    if m in (0, 2, 4):
                        dve.wait_ge(s(pre + "summed"), b // PAIRS * 3 + m // 2 + 1)
                    elif m == 6:
                        dve.wait_ge(s(pre + "scattered"), b + PAIRS)
                    for g in range(G):
                        last = stt(xT[:, m, g], half(m)[:, g * L:g * L + L], mod[:, i, 40 + m, g:g + 1],
                                   xT[:, m, g], ALU.mult, ALU.add)
                    if pre == "":
                        last.then_inc(s("x_added"), 1)
                if pre:
                    last.then_inc(s("fb_rounds_added"), 1)

            def first_best(out, vals, m):
                chain(tt(r_key, vals, m.unsqueeze(2).broadcast_to([P, G, 4]), ALU.is_equal))
                chain(tt(r_key, r_key, tie.unsqueeze(1).broadcast_to([P, G, 4]), ALU.mult))
                chain(v.reduce_max(r_km, r_key, AX.X))
                chain(tt(out, r_key, r_km.unsqueeze(2).broadcast_to([P, G, 4]), ALU.is_equal))

            def moe(i):
                norm(2 * i + 1)
                dve.wait_ge(s("logits_tr"), i + 1)
                chain(v.tensor_copy(lg[:], bank[5][:, 0:64].rearrange("p (g n) -> p g n", g=G)[:, :, 0:20]))
                b4 = lambda x: x.unsqueeze(2).broadcast_to([P, G, 4])
                chain(v.reduce_max(r_gm, lg[:, :, 0:4], AX.X))
                tt(r_gd, lg[:, :, 0:4], b4(r_gm), ALU.subtract).then_inc(s("route_in"), 1)
                first_best(r_og, lg[:, :, 0:4], r_gm)
                ex = lg[:, :, 4:20].rearrange("p g (q e) -> p g e q", q=4)
                chain(tt(r_x4, ex, r_og.unsqueeze(2).broadcast_to([P, G, 4, 4]), ALU.mult))
                chain(v.reduce_sum(r_le, r_x4, AX.X))
                chain(v.reduce_max(r_m1, r_le, AX.X))
                first_best(r_o1, r_le, r_m1)
                chain(stt(r_le2, r_o1, -1e30, r_le, ALU.mult, ALU.add))
                chain(v.reduce_max(r_m2, r_le2, AX.X))
                tt(r_dd, r_m2, r_m1, ALU.subtract).then_inc(s("route_in"), 1)
                first_best(r_o2, r_le2, r_m2)
                chain(tt(r_mt, r_o1, r_o2, ALU.add))
                tt(memb.rearrange("p g (q e) -> p g q e", q=4), r_og.unsqueeze(3).broadcast_to([P, G, 4, 4]),
                   r_mt.unsqueeze(2).broadcast_to([P, G, 4, 4]), ALU.mult).then_inc(s("members"), 1)
                dve.wait_ge(s("route_exp"), 2 * i + 1)
                chain(v.reduce_sum(r_sg, r_ge, AX.X))
                dve.wait_ge(s("route_exp"), 2 * i + 2)
                chain(stt(r_w2, r_de, 1.0, r_sg, ALU.add, ALU.mult))
                chain(v.reciprocal(r_w1, r_w2))
                chain(tt(r_w2, r_w1, r_de, ALU.mult))
                chain(tt(r_wt, r_o1, b4(r_w1), ALU.mult))
                chain(tt(r_key, r_o2, b4(r_w2), ALU.mult))
                chain(tt(r_wt, r_wt, r_key, ALU.add))
                chain(tt(comb.rearrange("p g (q e) -> p g q e", q=4), r_og.unsqueeze(3).broadcast_to([P, G, 4, 4]),
                         r_wt.unsqueeze(2).broadcast_to([P, G, 4, 4]), ALU.mult))
                dve.wait_ge(s("ranks_mm"), i + 1)
                v.reduce_max(r_mx, bank[4][:, 32:48], AX.X)
                chain(stt(r_rk, bank[4][:, 0:32].rearrange("p (g e) -> p g e", g=G), 1.0, memb, ALU.add, ALU.mult))
                chain(ts(rank[:], r_rk, -1.0, None, ALU.add))
                build_sel("", PAIRS * i, 0)
                for j in range(3):
                    chain(ts(r_rd[:, j:j + 1], r_mx, float(SLOTS * (j + 1)), None, ALU.is_gt))
                chain(ts(r_rd[:, 3:4], r_rd[:, 0:1], 1.0, r_rd[:, 1:2], ALU.add, ALU.add))
                tt(over[0:1, 0:1], r_rd[0:1, 3:4], r_rd[0:1, 2:3], ALU.add).then_inc(s("rounds_known"), 1)
                moe_round("", PAIRS * i, i)
                rounds = needed_rounds(dve, i)

                def one_round(b):
                    dve.wait_ge(s("x_added"), KD * (2 * i + 2))
                    dve.wait_ge(s("fb_rounds_added"), b // PAIRS)
                    ts(rank[:], rank[:], -float(SLOTS), None, ALU.add).then_inc(s("fb_rank"), 1)
                    dve.wait_ge(s("fb_rank"), b // PAIRS + 1)
                    moe_round("fb_", b, i)
                    dve.wait_ge(s("fb_rounds_added"), b // PAIRS + 1)

                further_rounds(dve, i, rounds, reg, one_round)

            v.memset(vrows[:], 0.0).then_inc(s("vrows_clear"), 1)
            v.memset(ones[:], 1.0)
            v.memset(zeros[:], 0.0)
            v.memset(ones16[:], 1.0)
            v.memset(eps, EPS)
            v.memset(one, 1.0)
            v.memset(condT[:], 0.0).then_inc(s("cond_ready"), 1)
            dve.wait_ge(s("vec_tr"), 1)
            v.tensor_copy(vec[:], bank[4][:, 0:VECS]).then_inc(s("vec_ready"), 1)
            for b in range(4):
                dve.wait_ge(s("x_tr"), b + 1)
                v.tensor_copy(xT[:, 2 * b:2 * b + 2], bank[b][:].rearrange("p (k g t) -> p k g t", k=2, g=G)) \
                    .then_inc(s("x_copied"), 1)
            dve.wait_ge(s("vec_ready"), 1)
            H = HY_HID
            big = 1.5 * 2 ** 23
            twopi = 2 * math.pi
            c1 = 6.28125
            c2 = float(np.float32(twopi - c1))
            c2 = math.floor(c2 * 2 ** 20) / 2 ** 20
            c3 = twopi - c1 - c2
            for n, bias in enumerate(("hy_f_b1", "hy_f_b2")):
                dve.wait_ge(s("f_mm"), n + 1)
                arg, turns = fsmall[0:H, 3, :], fsmall[0:H, 6, :]
                if n:
                    dve.wait_ge(s("f_sin"), 1)
                chain(ts(arg, bank[5][0:H, 0:L], vcol(bias, 0)[0:H], vcol("hy_f_freq", 0)[0:H], ALU.add, ALU.mult))
                chain(ts(turns, arg, 1.0 / twopi, big, ALU.mult, ALU.add))
                chain(ts(turns, turns, -big, None, ALU.add))
                chain(stt(arg, turns, -c1, arg, ALU.mult, ALU.add))
                chain(stt(arg, turns, -c2, arg, ALU.mult, ALU.add))
                chain(stt(arg, turns, -c3, arg, ALU.mult, ALU.add))
                pi = 3.1415925
                ts(arg, arg, pi, -pi, ALU.min, ALU.max).then_inc(s("f_arg"), 1)
            for c in range(8):
                dve.wait_ge(s("f3_mm"), c + 1)
                if c == 0:
                    dve.wait_ge(s("window_loaded"), 16)
                h = c % 2
                tt(kfb[:, c // 4, (c // 2) % 2, h * 512:h * 512 + 512], bank[4 + c % 2][:],
                   win[:, h * 512:h * 512 + 512], ALU.mult).then_inc(s("kfb_ready"), 1)
            dve.wait_ge(s("upper_loaded"), 16)
            v.tensor_copy(upper16[:], upper)
            dve.wait_ge(s("mask_loaded"), 16)
            v.tensor_copy(mask[:], mask32).then_inc(s("mask_ready"), 1)
            ada_at("start")
            norm(0)
            dve.wait_ge(s("x_tr"), 4)
            dve.wait_ge(s("vec_tr"), 1)
            v.memset(up[:, :, :, 0:1], 0.0)
            v.memset(up[:, :, :, L + 1:L + 2], 0.0).then_inc(s("up_clear"), 1)
            for m in range(24):
                dve.wait_ge(s("up_ready"), m + 1)
                if m == 0:
                    dve.wait_ge(s("spec_ready"), 12)
                u, src = uT[:, m], up[:, m % 4]
                w = lambda t: vcol("hy_conv_w", 24 * t + m)
                chain(ts(u, src[:, :, 0:L], w(0), vcol("hy_conv_b", m), ALU.mult, ALU.add))
                chain(stt(u, src[:, :, 1:L + 1], w(1), u, ALU.mult, ALU.add))
                stt(u, src[:, :, 2:L + 2], w(2), u, ALU.mult, ALU.add).then_inc(s("conv_ready"), 1)
                if m in (7, 15):
                    ada_at(f"w_in{m // 4}")

            def products(n):
                dve.wait_ge(s("zf_mm"), n + 1)
                for w, (ka, kb) in enumerate(((0, 1), (1, 2))):
                    if n:
                        dve.wait_ge(s("yspec"), 2 * n - 1 + w)
                    for dst, first, kk in ((prods[w][0], 0, ka), (prods[w][1], 2, kb)):
                        for h in range(2):
                            last = tt(dst[:, h * 512:h * 512 + 512], bank[first + h][:],
                                      spec[:, kk, n // 2, h * 512:h * 512 + 512], ALU.mult)
                        last.then_inc(s("prods"), 1)

            def gated(n):
                dve.wait_ge(s("zi_mm"), n + 1)
                dve.wait_ge(s("skip_ready"), n + 1)
                x_o = 8 * (n // 2 + 1)
                for h in range(2):
                    sk = vskip[n % 2].rearrange("p (k t) -> p k t", k=KD)[:, 4 * h:4 * h + 4]
                    chain(tt(sk, sk, psum_tok(4 + h, 4), ALU.add))
                    last = tt(uT[:, 4 * h:4 * h + 4, n % G], sk, uT[:, x_o + 4 * h:x_o + 4 * h + 4, n % G], ALU.mult)
                last.then_inc(s("z_ready"), 1)

            ada_at("w_in5")
            dve.wait_ge(s("conv_ready"), 24)
            products(0)
            ada_at("conv0")
            products(1)
            gated(0)
            products(2)
            gated(1)
            ada_at("conv1")
            products(3)
            gated(2)
            ada_at("conv2")
            gated(3)
            residual(0, g1(0))
            moe(0)
            if layers > 1:
                norm(2)
                dve.wait_ge(s("gk1_mm"), 1)
                v.tensor_copy(gk1[0:32, :], bank[4][0:32, 0:NT]).then_inc(s("gk1_ready"), 1)

                fl = lambda x: x.rearrange("p h g t -> p (h g t)")

                def cumulate(d):
                    if d:
                        dve.wait_ge(s("scores_mm"), 2)
                    v.memset(reset[:], 1.0).then_inc(s("reset"), 1)
                    dve.wait_ge(s("reset"), 2 * d + 1)
                    e = reset.rearrange("p (n t) -> p n t", t=CH)
                    v.memset(e[:, :, 0:1] if d == 0 else e[:, :, CH - 1:CH], 0.0).then_inc(s("reset"), 1)
                    dve.wait_ge(s("gate_ln"), d + 1)
                    chain(stt(gx[:], gx[:], 0.0, gt[:], ALU.min, ALU.subtract))
                    dve.wait_ge(s("reset"), 2 * d + 2)
                    if d == 0:
                        v.tensor_tensor_scan(gt[:], reset[:], gx[:], 0.0, ALU.mult, ALU.add).then_inc(s("gate_cum"), 1)
                    else:
                        v.tensor_tensor_scan(gt[:, ::-1], reset[:, ::-1], gx[:, ::-1], 0.0, ALU.mult, ALU.add) \
                            .then_inc(s("gate_cum"), 1)
                    dve.wait_ge(s("gate_cum"), 2 * d + 1)
                    b16 = gt.rearrange("p (n t) -> p n t", t=CH)
                    bl = b16[:, :, CH - 1:CH] if d == 0 else b16[:, :, 0:1]
                    tt(gx.rearrange("p (n t) -> p n t", t=CH), bl.broadcast_to([P, 16, CH]), b16, ALU.subtract) \
                        .then_inc(s("gate_cum"), 1)

                def keys(d):
                    dve.wait_ge(s("qk_ready"), 4)
                    dve.wait_ge(s("k_exp"), 2 * d + 1)
                    tt(fl(ke), fl(kT), e2[:], ALU.mult).then_inc(s("qke_ready"), 1)
                    dve.wait_ge(s("k_exp"), 2 * d + 2)
                    if d:
                        dve.wait_ge(s("kd_tr"), 2)
                    tt(fl(kdT), fl(kT), gx[:], ALU.mult).then_inc(s("kd_ready"), 1)

                def queries(d):
                    dve.wait_ge(s("q_exp"), d + 1)
                    if d:
                        dve.wait_ge(s("o_mm"), 1)
                    tt(fl(qe), fl(qT), e1[:], ALU.mult).then_inc(s("qke_ready"), 1)

                def scores(d):
                    dve.wait_ge(s("sc_clear"), 1)
                    if d:
                        dve.wait_ge(s("intra_mm"), 1)
                    dve.wait_ge(s("mask_ready"), 1)
                    for g in range(G):
                        dve.wait_ge(s("scores_mm"), 2 * d + g + 1)
                        if d:
                            v.memset(sc[:, g], 0.0).then_inc(s("sc_clear"), 1)
                            dve.wait_ge(s("sc_clear"), 2 + g)
                        v.copy_predicated(sc[:, g], mask[:, d, :].unsqueeze(1).broadcast_to([P, HEADS, P]),
                                          psum_tok(4 + g, 4)).then_inc(s("sc_ready"), 1)

                e4 = e1.rearrange("p (h g t) -> p h g t", h=HEADS, g=G)
                pu = lambda h: bank[4 + h // 2][:, (h % 2) * DV:(h % 2) * DV + DV]

                def states(d):
                    dec = lambda h, g, c: e4[:, h, g, c * CH + CH - 1:c * CH + CH] if d == 0 else \
                        e4[:, h, g, c * CH:c * CH + 1]
                    dve.wait_ge(s("s0_loaded"), 32)
                    if d == 1:
                        dve.wait_ge(s("state_stored"), 16)
                        dve.wait_ge(s("o_mm"), 1)
                    dve.wait_ge(s("upd_mm"), 3 * d + 1)
                    for h in range(HEADS):
                        last = stt(s1l[:, h], s0[:, d, h], dec(h, 1, d), pu(h), ALU.mult, ALU.add)
                    last.then_inc(s("upd_read"), 1)
                    dve.wait_ge(s("upd_mm"), 3 * d + 2)
                    for b in range(2):
                        last = v.tensor_copy(s1c[:, 2 * b:2 * b + 2], bank[4 + b][:].rearrange("p (h n) -> p h n", h=2))
                    last.then_inc(s("upd_read"), 1)
                    dve.wait_ge(s("upd_read"), 3 * d + 2)
                    dve.wait_ge(s("upd_mm"), 3 * d + 3)
                    for h in range(HEADS):
                        last = stt(s2[:, h], s1c[:, h], dec(h, 0, 1 - d), pu(h), ALU.mult, ALU.add)
                    last.then_inc(s("upd_read"), 1)

                ada_at("queries")
                cumulate(0)
                keys(0)
                queries(0)
                v.memset(sc[:], 0.0).then_inc(s("sc_clear"), 1)
                ada_at("values")
                scores(0)
                cumulate(1)
                states(0)
                keys(1)
                queries(1)
                ada_at("between")
                scores(1)
                states(1)
                dve.wait_ge(s("g_ready"), 1)
                dve.wait_ge(s("o_mm"), 2)
                dve.wait_ge(s("upd_read"), 6)
                for m in range(KD):
                    dve.wait_ge(s("osq_ready"), m // 2 + 1)
                    last = stt(oT[:, m].rearrange("p g t -> p (g t)"), half(m), vcol("gla_norm_g", m % 2), gT[:, m],
                               ALU.mult, ALU.mult)
                chain(last)
                ada_at("heads")
                for m in range(KD):
                    dve.wait_ge(s("ors_ready"), m // 4 + 1)
                    o = oT[:, m].rearrange("p g t -> p (g t)")
                    tt(o, o, ors[:, m // 2], ALU.mult).then_inc(s("o_ready"), 1)
                residual(1, g1(1))
                moe(1)
            if layers > 2:
                norm(4)
                ada_at("fnet")
                residual(2, g1(2))
                moe(2)
            if layers > 3:
                norm(6)
                gs = rtv(200, KD, G)
                chain(tt(gs, mod[:, 3, 16:24], vcol("pool_scale", 0, KD).unsqueeze(2).broadcast_to([P, KD, G]), ALU.mult))
                residual(3, lambda m, g: gs[:, m, g:g + 1])
                moe(3)
            dve.wait_ge(s("rstd_ready"), 2 * layers + 1)
            for g in range(G):
                for k in range(KD):
                    last = stt(hT[:, k, g], xT[:, k, g], vcol("final_g", k), rstd[:, g], ALU.mult, ALU.mult)
                last.then_inc(s("final_ready"), 1)
            for g in range(G):
                dve.wait_ge(s("out_tr"), g + 1)
                for h in range(2):
                    last = v.tensor_copy(xin[:, g, h * 512:h * 512 + 512], bank[2 * g + h][:])
                last.then_inc(s("out_rows"), 1)

        @block.gpsimd
        def _(pool):
            v = nc.gpsimd
            pool.dma_start(fsmall[0:HY_EMB, 0, :], a["c_pos"]).then_inc(s("filter_loaded"), 16)
            pool.dma_start(fsmall[0:HY_EMB, 1, 0:HY_HID], a["hy_f_w1"][0]).then_inc(s("filter_loaded"), 16)
            pool.dma_start(fsmall[0:HY_HID, 2, 0:HY_HID], a["hy_f_w2"][0]).then_inc(s("filter_loaded"), 16)
            pool.dma_start(mask32.rearrange("p d t -> p (d t)"), a["c_mask"]).then_inc(s("mask_loaded"), 16)

            def load_router(i):
                pool.dma_start(rw[:, :, 0:4], a["moe_w_rg"][i].rearrange("(k p) n -> p k n", p=P)) \
                    .then_inc(s("rw_loaded"), 16)
                pool.dma_start(rw[:, :, 4:20], a["moe_w_re"][i].rearrange("(k p) n -> p k n", p=P)) \
                    .then_inc(s("rw_loaded"), 16)

            load_router(0)
            pool.wait_ge(s("conv_ready"), 24)
            for n in range(4):
                if n > 1:
                    pool.wait_ge(s("z_ready"), n - 1)
                coef = vcol("hy_skip", 8 * (n // 2), KD).unsqueeze(2).broadcast_to([P, KD, L])
                v.tensor_tensor(vskip[n % 2].rearrange("p (k t) -> p k t", k=KD), uT[:, 0:KD, n % G], coef, ALU.mult) \
                    .then_inc(s("skip_ready"), 1)
                for w, op in enumerate((ALU.subtract, ALU.add)):
                    pool.wait_ge(s("prods"), 4 * n + 2 * w + 2)
                    if n:
                        pool.wait_ge(s("zi_mm"), n)
                    v.tensor_tensor(ysp[:, w], prods[w][0], prods[w][1], op).then_inc(s("yspec"), 1)
            if layers > 1:
                pool.wait_ge(s("x_added"), KD)
                v.memset(wg2[0:32], 0.0).then_inc(s("wg2_clear"), 1)
                pool.wait_ge(s("wg2_clear"), 1)
                for d in range(2):
                    pool.dma_start(wg1[:, :, 16 * d:16 * d + 16], a["gla_w_gk1"][0, d].rearrange("(k p) r -> p k r", p=P)) \
                        .then_inc(s("cm1_loaded"), 16)
                    pool.dma_start(wg2[16 * d:16 * d + 16, d, :], a["gla_w_gk2"][0, d]).then_inc(s("cm1_loaded"), 16)
                    pool.dma_start(s0[:, d], a["state_gla"][0, 0, d].rearrange("h k v -> k h v")) \
                        .then_inc(s("s0_loaded"), 16)
                pool.wait_ge(s("logits_mm"), 1)
                load_router(1)
                for d in range(2):
                    pool.wait_ge(s("upd_read"), 3 * d + 3)
                    pool.dma_start(a["new_state"][0, 0, d].rearrange("h k v -> k h v"), s2[:]) \
                        .then_inc(s("state_stored"), 16)
            if layers > 2:
                pool.wait_ge(s("x_added"), KD * 3)
                pool.dma_start(cm[:], a["c_fnet"]).then_inc(s("cm2_loaded"), 16)
                pool.wait_ge(s("logits_mm"), 2)
                load_router(2)
            if layers > 3:
                pool.wait_ge(s("x_added"), KD * 5)
                pool.dma_start(cm[:, 0:1024], a["c_pool"]).then_inc(s("cm3_loaded"), 16)
                pool.wait_ge(s("logits_mm"), 3)
                load_router(3)


INPUTS = ['x_prompt', 'x_sample', 'state_gla', 'c', 'c_ctx', 'w_ada', 'b_ada', 'norm_g',
          'hy_w_in', 'hy_b_in', 'hy_conv_w', 'hy_conv_b', 'hy_f_w1', 'hy_f_b1', 'hy_f_freq', 'hy_f_w2', 'hy_f_b2',
          'hy_f_w3', 'hy_skip', 'hy_w_out', 'hy_b_out',
          'gla_w_q', 'gla_w_k', 'gla_w_v', 'gla_w_g', 'gla_w_gk1', 'gla_w_gk2', 'gla_b_gk', 'gla_norm_g', 'gla_w_o',
          'fn_w_out', 'fn_b_out', 'pool_w', 'pool_b', 'pool_scale',
          'moe_w_rg', 'moe_w_re', 'moe_w1', 'moe_w3', 'moe_w2', 'final_g']


def declare(nc, arrays):
    aps = {n: nc.dram_tensor(f"in_{n}", x.shape, mybir.dt.from_np(x.dtype), kind="ExternalInput").ap()
           for n, x in arrays.items()}
    for n, shape in (("y_prompt", (1, L, D)), ("y_sample", (1, L, D)), ("new_state", (1, 1, 2, HEADS, DK, DV))):
        aps[n] = nc.dram_tensor(f"out_{n}", shape, F32, kind="ExternalOutput").ap()
    return aps


def kernel(**inputs):
    import concourse.bacc as bacc
    from concourse.bass_utils import run_bass_kernel_spmd

    nc = bacc.Bacc("TRN2", target_bir_lowering=False, num_devices=1)
    arrays = {n: np.ascontiguousarray(inputs[n]) for n in INPUTS}
    arrays.update({f"c_{n}": x for n, x in constants().items()})
    build(nc, declare(nc, arrays))
    r = run_bass_kernel_spmd(nc, [{f"in_{n}": x for n, x in arrays.items()}], core_ids=[0])
    got = r.results[0]
    return got["out_y_prompt"], got["out_y_sample"], got["out_new_state"]
```

```python
import math
from contextlib import ExitStack

import numpy as np
import concourse.bass as bass
from concourse import mybir

F32 = mybir.dt.float32
BF16 = mybir.dt.bfloat16
I32 = mybir.dt.int32
U8 = mybir.dt.uint8
ALU = mybir.AluOpType
ACT = mybir.ActivationFunctionType
AX = mybir.AxisListType

D = 1024
L = 128
G = 2
NT = G * L
P = 128
KD = D // P
LAYERS = 4
GRID_W = 64
EPS = 1e-6
HY_BANDS, HY_HID, HY_ORDER = 8, 64, 2
HY_EMB = 1 + 2 * HY_BANDS
HEADS, DK, DV, CH = 4, 128, 256, 64
WINDOWS = (2, 4, 8, 16)
EXPERTS, EGROUPS, FF = 16, 4, 512
SLOTS = 64
PAIRS = EXPERTS // 2
RING = 6
PIECE = 4096

VEC = {}


def vec_layout():
    tiles = [[("norm_g", 64), ("c", 8), ("c_ctx", 8), ("hy_skip", 16), ("hy_b_out", 8),
              ("fn_b_out", 8), ("pool_b", 8)],
             [("b_ada01", 96), ("hy_b_in", 24), ("pool_scale", 8)],
             [("b_ada23", 96), ("hy_conv_b", 24), ("gla_b_gk", 8)],
             [("hy_conv_w", 72), ("gla_norm_g", 2), ("hy_f_b1", 1), ("hy_f_freq", 1), ("hy_f_b2", 1)]]
    return [(name, t, sum(n for _, n in tile[:i]), n) for t, tile in enumerate(tiles)
            for i, (name, n) in enumerate(tile)]


VEC = {name: t * P + r for name, t, r, _ in vec_layout()}
VECS = max(t * P + r + n for _, t, r, n in vec_layout())


def constants():
    n = np.arange(L)
    f = np.arange(P)
    ang = 2 * np.pi * np.outer(n, f) / (2 * L)
    cos, sin = np.cos(ang), np.sin(ang)
    nyq = (-1.0) ** n
    fwd_re = cos.copy()
    fwd_im = -sin.copy()
    fwd_im[:, 0] = nyq
    k_im = -sin
    k_d = cos.copy()
    k_d[:, 0] = nyq
    inv_re = 2 * cos.T / (2 * L)
    inv_re[0] /= 2
    inv_im = -2 * sin.T / (2 * L)
    inv_im[0] = nyq / (2 * L)
    dft = np.concatenate([fwd_re, fwd_im, k_im, k_d, inv_re, inv_im], axis=1)

    bands = np.linspace(1e-4, HY_BANDS - 1, HY_BANDS)
    a = (2 * np.pi * n / L)[:, None] * bands[None]
    pos = np.concatenate([(n / L)[:, None], np.cos(a), -np.sin(a)], axis=-1).T
    deltas = np.linspace(math.log(1e-2) / 1.5, math.log(1e-2) / 0.3, D)
    window = np.exp(-np.linspace(0, 1, L)[:, None] * np.abs(deltas)[None])

    c = D // 4
    ch = 2 * np.pi * np.outer(np.arange(c), np.arange(c)) / c
    cs = np.concatenate([np.cos(ch), np.sin(ch)], axis=1).reshape(2, P, 2 * c).transpose(1, 0, 2).reshape(P, -1)
    tok = 2 * np.pi * np.outer(n, n) / L
    fnet = np.concatenate([cs, np.cos(tok) / math.sqrt(L * c), -np.sin(tok) / math.sqrt(L * c)], axis=1)

    def mean(length, k):
        m = np.zeros((length, length))
        for t in range(length):
            lo, hi = max(t - k // 2, 0), min(t + k - k // 2, length)
            m[t, lo:hi] = 1.0 / (hi - lo)
        return m

    pool = []
    for g in range(G):
        for k in WINDOWS:
            m = mean(L, k) if g == 0 else np.kron(mean(L // GRID_W, k), mean(GRID_W, k))
            pool.append((m - np.eye(L)).T)
    pool = np.concatenate(pool, axis=1)

    base = np.concatenate([np.eye(P), np.tile(np.arange(SLOTS), (P, 1)),
                           np.tile(np.arange(4, 0, -1), (P, 1))], axis=1)
    s, t = np.arange(P)[:, None] % CH, np.arange(P)[None]
    same = (np.arange(P)[:, None] // CH) == (t // CH)
    mask = np.concatenate([same & (s <= t % CH), same & (s >= t % CH)], axis=1)
    out = {"base": base, "upper": np.triu(np.ones((P, P)), 1), "dft": dft, "pos": pos, "window": window,
           "fnet": fnet, "pool": pool, "mask": mask}
    return {k: v.astype(np.float32) for k, v in out.items()}


ADA_AT = {"start": [0], "w_in1": [1], "w_in3": [2], "w_in5": [3], "conv0": [4], "conv1": [5], "conv2": [6],
          "queries": [7], "values": [8], "between": [9], "heads": [10], "fnet": [11]}


def adas_until(point, layers):
    points = list(ADA_AT)
    return sum(n < 3 * layers for at in points[:points.index(point) + 1] for n in ADA_AT[at])


def piece_stream(layers):
    ada = lambda at: [("ada", n // 3, n % 3, j) for n in ADA_AT[at] if n < 3 * layers for j in range(4)]
    halves = lambda name: [(name, 0), (name, 1)]
    lay = [ada("start") + sum([[("w_in", c), ("w_in", c + 1)] + ada(f"w_in{c + 1}") for c in (0, 2, 4)], [])
           + ada("conv0") + ada("conv1") + ada("conv2") + halves("w_out"),
           [("wq", 0)] + ada("queries") + [("wk", 0)] + halves("wv") + ada("values") + halves("wg")
           + ada("between") + ada("heads") + halves("wo"),
           ada("fnet") + halves("fn"),
           [("pool", 0)]]
    used, out, at = [0] * RING, [], 0
    for i in range(layers):
        for what in lay[i]:
            slot = at % RING
            out.append((what, slot, used[slot]))
            used[slot] += 1
            at += 1
        slots = [(at + n) % RING for n in range(RING)]
        out.append((("moe", i), slots, [used[x] for x in slots]))
        for n, x in enumerate(slots):
            used[x] += PAIRS if n < 4 else PAIRS - 1
    return out


def build(nc, a, layers=LAYERS):
    stream = piece_stream(layers)
    where = {what: (slot, nth) for what, slot, nth in stream if what[0] != "moe"}
    moe_slots = {what[1]: slots for what, slots, _ in stream if what[0] == "moe"}
    moe_uses = {what[1]: nth for what, _, nth in stream if what[0] == "moe"}

    ctx = ExitStack()
    sems = {}

    def s(name):
        if name not in sems:
            sems[name] = ctx.enter_context(nc.semaphore(name))
        return sems[name]

    def sb(name, shape, dt=F32):
        return ctx.enter_context(nc.sbuf_tensor(name, shape, dt))

    with ctx:
        ring = [sb(f"ring{i}", [P, PIECE]) for i in range(RING)]
        xT = sb("xT", [P, KD, G, L])
        hT = sb("hT", [P, KD, G, L])
        arena = sb("arena", [P, 20480])
        cm = sb("cm", [P, 1280])
        base = sb("base", [P, 196])
        ident, iota, tie = base[:, 0:128], base[:, 128:192], base[:, 192:196]
        ones = sb("ones", [P, P])
        ones16, upper16 = sb("ones16", [P, P], BF16), sb("upper16", [P, P], BF16)
        zeros = sb("zeros", [P, P], BF16)
        vec = sb("vec", [P, VECS])
        mod = sb("mod", [P, LAYERS, 48, G])
        scale = sb("scale", [P, LAYERS, 2, KD, G])
        condT = sb("condT", [P, KD, 32])
        rstd = sb("rstd", [P, G, L])
        rows = sb("rows", [P, 512])
        small = sb("small", [P, 5])
        eps, one, rstd_col = small[:, 0:1], small[:, 1:2], small[:, 2:4]
        rw = sb("rw", [P, KD, 20])
        mask = sb("mask", [P, 2, P], U8)
        over = sb("over", [1, 2], I32)
        bank = [ctx.enter_context(nc.psum_tensor(f"bank{i}", [P, 512], F32)) for i in range(8)]

        def ar(lo, *dims):
            n = int(np.prod(dims))
            v = arena[:, lo:lo + n]
            if len(dims) == 1:
                return v
            names = "abcd"[:len(dims)]
            return v.rearrange(f"p ({' '.join(names)}) -> p {' '.join(names)}",
                               **dict(zip(names, dims)))

        def vcol(name, lo, n=1):
            return vec[:, VEC[name] + lo:VEC[name] + lo + n]

        def piece(slot, *dims):
            names = "abc"[:len(dims)]
            return ring[slot][:, 0:int(np.prod(dims))].rearrange(
                f"p ({' '.join(names)}) -> p {' '.join(names)}", **dict(zip(names, dims)))

        def b_ada(i, lo, n):
            return vcol("b_ada01" if i < 2 else "b_ada23", 48 * (i % 2) + lo, n)

        def half(m):
            return bank[m // 2][:, (m % 2) * NT:(m % 2) * NT + NT]

        xin = ar(15360, G, D)
        vrows = ar(17408, 4, P)
        w3f = ar(6144, 4096)
        kfb = ar(10240, 2, HY_ORDER, D)
        k_even, k_odd = ar(15360, HY_ORDER, D), kfb[:, 1]
        win = ar(14336, D)
        spec = ar(0, 3, HY_ORDER, D)
        uT = ar(6144, 24, G, L)
        zt = ar(12288, G, D)
        prod = ar(14336, D)
        ysp = ar(15360, 2, D)
        up = ar(17408, 4, G, L + 2)
        vskip = [ar(17408, D), ar(19456, D)]
        hflat = hT[:].rearrange("p k g t -> p (k g t)")
        prods = [[prod, ar(18432, D)], [hflat[:, 0:D], hflat[:, D:2 * D]]]
        upper, mask32 = ar(19472, P), ar(19600, 2, P)
        fsmall = ar(18448, 8, P)
        htok = ar(0, G, D)
        xg = ar(2048, KD, P)
        sil = ar(3072, FF)
        hid = ar(3584, FF)
        hidT = ar(4096, 4, P)
        yv = ar(4608, D)
        sel = ar(5632, G, 2, SLOTS)
        selw = ar(5888, G, 2, SLOTS)
        selT = ar(6144, NT)
        comb = ar(6400, G, EXPERTS)
        memb = ar(6432, EXPERTS).bitcast(BF16).rearrange("p (g n) -> p g n", g=G)
        rank = ar(6464, G, EXPERTS)
        lraw = ar(6496, NT)
        lg = ar(6752, G, 20)
        rt = ar(6800, 1024)
        final_g = ar(14336, D)
        xout = ar(15360, G, D)
        first_w2 = [[ar(16384, 4, D), ar(8192 if i in (0, 2) else 10240, 4, D)] for i in range(LAYERS)]
        yb = ar(14336, 4, NT)

        fnp = ar(8192, G, 4, 512)
        fnm = ar(12288, KD, G, L)
        plr = ar(8192, G, 4, 256)
        qT, kT = ar(0, HEADS, G, L), ar(1024, HEADS, G, L)
        vrow = ar(2048, G, D)
        gT = ar(4096, KD, NT)
        gx, gt = ar(6144, 1024), ar(7168, 1024)
        e1, e2 = ar(8192, 1024), ar(9216, 1024)
        qe, ke, kdT = ar(10240, HEADS, G, L), ar(11264, HEADS, G, L), ar(12288, HEADS, G, L)
        reset = ar(11264, 1024)
        kdr = ar(13312, G, HEADS, P)
        sc = ar(14336, G, HEADS, P)
        s0 = ar(15360, 2, HEADS, DV)
        s1c, s1l, s2 = ar(17408, HEADS, DV), ar(18432, HEADS, DV), ar(19456, HEADS, DV)
        oT, osq, ors = ar(8192, KD, G, L), ar(10240, KD, NT), ar(6144, HEADS, NT)
        wg1 = cm[:, 0:256].rearrange("p (k r) -> p k r", k=KD)
        gk1 = cm[:, 0:NT]
        wg2 = cm[:, 256:1280].rearrange("p (d n) -> p d n", d=2)

        def psum_tok(b, n):
            return bank[b][:, 0:n * P].rearrange("p (a b) -> p a b", a=n)

        def rtv(lo, *dims):
            n = int(np.prod(dims))
            v = rt[:, lo:lo + n]
            if len(dims) == 1:
                return v
            names = "abcd"[:len(dims)]
            return v.rearrange(f"p ({' '.join(names)}) -> p {' '.join(names)}", **dict(zip(names, dims)))

        r_gd, r_ge = rtv(0, G, 4), rtv(8, G, 4)
        r_dd, r_de = rtv(16, G), rtv(18, G)
        r_gm, r_key, r_km, r_og = rtv(20, G), rtv(24, G, 4), rtv(32, G), rtv(40, G, 4)
        r_x4 = rtv(48, G, 4, 4)
        r_le, r_m1, r_o1, r_o2 = rtv(80, G, 4), rtv(88, G), rtv(96, G, 4), rtv(104, G, 4)
        r_le2, r_m2, r_sg, r_w1, r_w2 = rtv(112, G, 4), rtv(120, G), rtv(122, G), rtv(124, G), rtv(126, G)
        r_wt, r_mt, r_rk = rtv(128, G, 4), rtv(136, G, 4), rtv(144, G, EXPERTS)
        r_mx, r_rd = rtv(176, 1), rtv(177, 4)
        route_exp = [(r_ge, r_gd), (r_de, r_dd)]

        g_bank = lambda m: 6 if m in (3, 5) else 7

        block = ctx.enter_context(nc.Block())

        def freed(what):
            k = what[0]
            if k == "ada":
                return "ada_mm", 3 * what[1] + what[2] + 1
            if k == "w_in":
                return "win_mm", 4 * what[1] + 4
            if k in ("w_out", "wo", "fn"):
                return "res_mm", KD * {"w_out": 0, "wo": 1, "fn": 2}[k] + 4 * what[1] + 4
            if k == "pool":
                return "pool_hw", 4
            return "gla_proj", {"wq": 2, "wk": 4, "wv": 6 + 2 * what[1], "wg": 12 + 4 * what[1]}[k]

        def source(what):
            k = what[0]
            if k == "ada":
                c = 4 * what[2] + what[3]
                return a["w_ada"][what[1]][:, 512 * c:512 * c + 512].rearrange("(k p) n -> p k n", p=P), KD
            if k == "w_in":
                return a["hy_w_in"][0][:, 512 * what[1]:512 * what[1] + 512].rearrange("(k p) n -> p k n", p=P), KD
            if k == "pool":
                return a["pool_w"][0].rearrange("g (k p) e -> p (g k) e", p=P), KD
            name = {"w_out": "hy_w_out", "wo": "gla_w_o", "fn": "fn_w_out", "wq": "gla_w_q", "wk": "gla_w_k",
                    "wv": "gla_w_v", "wg": "gla_w_g"}[k]
            return a[name][0][:, 512 * what[1]:512 * what[1] + 512].rearrange("(k p) n -> p k n", p=P), KD

        expert_dram = [a["moe_w1"].rearrange("l x (k p) n -> (l x) p k n", p=P),
                       a["moe_w3"].rearrange("l x (k p) n -> (l x) p k n", p=P),
                       a["moe_w2"].rearrange("l x (k p) n -> (l x) p k n", p=P)]
        USED = ["h1_mm", "h3_mm", "y_mm"]

        def prime(eng, *names):
            for pre in ("", "fb_"):
                for name in names:
                    eng.sem_inc(s(pre + name), 1)

        def primed(count):
            return count + 1

        def used_up(pre, kind, pairs):
            return s(pre + USED[kind]), pairs * (2 if kind == 2 else 1)

        def expert_load(sp, kind, e, i, first_expert, full):
            slot = moe_slots[i][2 * kind + e]
            dst = piece(slot, KD, FF) if kind < 2 else piece(slot, 4, D)
            src = expert_dram[kind][bass.ds(first_expert + e, 1)].rearrange("o p k n -> p (o k) n")
            sp.dma_start(dst, src).then_inc(s(f"{full}{slot if full == 'full' else 2 * kind + e}"), 16)

        def needed_rounds(eng, i):
            eng.wait_ge(s("rounds_known"), i + 1)
            return eng.value_load(over[0:1, 0:1], min_val=1, max_val=NT // SLOTS)

        def fb_count(eng, name):
            reg = eng.alloc_register(name)
            eng.reg_mov(reg, 0)
            return reg

        def further_rounds(eng, i, rounds, reg, one_round):
            with eng.If(rounds - 1):
                with eng.Fori(1, rounds) as _:
                    b = eng.snap(reg, min_val=0, max_val=8 * 3 * LAYERS)
                    one_round(b)
                    eng.reg_add(reg, reg, PAIRS)

        def vector_loads(eng, part):
            for name, t, r, n in vec_layout()[::-1][part::2]:
                dst = vrows[r:r + n, t, :]
                if name in ("b_ada01", "b_ada23"):
                    i = 0 if name == "b_ada01" else 2
                    src = a["b_ada"][i:i + 2].rearrange("l (c p) -> (l c) p", p=P)
                elif name in ("hy_f_b1", "hy_f_freq", "hy_f_b2"):
                    src, dst = a[name], vrows[r:r + 1, t, 0:HY_HID]
                elif name == "norm_g":
                    src = a[name].rearrange("l w (c p) -> (l w c) p", p=P)
                elif name == "c_ctx":
                    src = a[name].rearrange("(c p) -> c p", p=P)
                elif name in ("hy_skip", "hy_conv_w", "gla_b_gk"):
                    src = a[name][0].rearrange("w (c p) -> (w c) p", p=P)
                else:
                    src = a[name].rearrange("o (c p) -> (o c) p", p=P)
                eng.dma_start(dst, src).then_inc(s("filter_rows_loaded" if t == 3 else "vrows_loaded"), 16)

        @block.sync
        def _(sp):
            reg = fb_count(sp, "sp_extra_pairs")
            sp.wait_ge(s("vrows_clear"), 1)
            vector_loads(sp, 1)
            sp.dma_start(xin[:, 0, :], a["x_prompt"][0]).then_inc(s("x_loaded"), 16)
            sp.dma_start(xin[:, 1, :], a["x_sample"][0]).then_inc(s("x_loaded"), 16)
            for h in range(2):
                sp.dma_start(w3f[0:HY_HID, 2048 * h:2048 * h + 2048], a["hy_f_w3"][0][:, 2048 * h:2048 * h + 2048]) \
                    .then_inc(s("w3_loaded"), 16)
            sp.dma_start(win[:], a["c_window"]).then_inc(s("window_loaded"), 16)
            sp.dma_start(cm[:, 0:6 * P], a["c_dft"]).then_inc(s("dft_loaded"), 16)
            last = [None] * RING
            extra = None

            def slot_free(slot):
                if last[slot]:
                    name, value = last[slot]
                    sp.wait_ge(s(name), value)
                    if name in USED:
                        sp.wait_ge(s("fb_" + name), primed(extra * (2 if name == "y_mm" else 1)))

            for what, slot, nth in stream:
                if what[0] != "moe":
                    slot_free(slot)
                    src, n = source(what)
                    sp.dma_start(piece(slot, n, 512) if what[0] != "pool" else piece(slot, n, 256), src) \
                        .then_inc(s(f"full{slot}"), 16)
                    last[slot] = freed(what)
                    continue
                i = what[1]
                for kind in range(2):
                    for e in range(2):
                        slot_free(moe_slots[i][2 * kind + e])
                        expert_load(sp, kind, e, i, EXPERTS * i, "full")
                if i == 0:
                    sp.wait_ge(s("z_ready"), 4)
                elif i == 1:
                    sp.wait_ge(s("osum_mm"), 2)
                    sp.wait_ge(s("state_stored"), 32)
                elif i == 2:
                    sp.wait_ge(s("fn_tok_mm"), 4)
                for e in range(2):
                    sp.dma_start(first_w2[i][e], a["moe_w2"][i, e].rearrange("(k p) n -> p k n", p=P)) \
                        .then_inc(s("first_w2_loaded"), 16)
                for e in range(2):
                    slot_free(moe_slots[i][4 + e])
                    expert_load(sp, 2, e, i, EXPERTS * i + 2, "full")
                for kind in range(2):
                    sem, v = used_up("", kind, 1)
                    sp.wait_ge(sem, primed((PAIRS * i + 1) * v))
                    for e in range(2):
                        expert_load(sp, kind, e, i, EXPERTS * i + 2, "full")
                with sp.Fori(2, PAIRS) as p:
                    for kind in range(3):
                        sem, v = used_up("", kind, 1)
                        sp.wait_ge(sem, primed((PAIRS * i + p) * v))
                        for e in range(2):
                            expert_load(sp, kind, e, i, EXPERTS * i + p * 2, "full")
                rounds = needed_rounds(sp, i)

                def one_round(b):
                    for kind in range(3):
                        sem, v = used_up("", kind, 1)
                        sp.wait_ge(sem, primed(PAIRS * (i + 1) * v))
                    with sp.Fori(0, PAIRS) as p:
                        for kind in range(3):
                            sem, v = used_up("fb_", kind, 1)
                            sp.wait_ge(sem, primed((b + p) * v))
                            for e in range(2):
                                expert_load(sp, kind, e, i, EXPERTS * i + p * 2, "fb_full")

                further_rounds(sp, i, rounds, reg, one_round)
                for kind in range(3):
                    for e in range(2):
                        last[moe_slots[i][2 * kind + e]] = (USED[kind],
                                                              primed(PAIRS * (i + 1) * (2 if kind == 2 else 1)))
                extra = sp.snap(reg, min_val=0, max_val=8 * 3 * LAYERS)
            for g, name in enumerate(("y_prompt", "y_sample")):
                sp.wait_ge(s("out_rows"), 2 * g + 1)
                sp.dma_start(a[name][0][:, 0:512], xout[:, g, 0:512]).then_inc(s("stored"), 16)
            if layers > 1:
                sp.wait_ge(s("state_stored"), 32)
            sp.wait_ge(s("stored"), 16 * 4)

        mm = nc.tensor.matmul
        tr = nc.tensor.transpose

        def pe_gla(pe, arrived, ada_at, norm, h_ready, project, residual):
            norm(2)
            pe.wait_ge(s("cm_loaded"), 16 * 4)
            for k in range(KD):
                h_ready(2, k)
                last = mm(bank[4][0:32, 0:NT], wg1[:, k, :], hT[:, k].rearrange("p g t -> p (g t)"),
                          start=k == 0, stop=k == KD - 1)
            last.then_inc(s("gk1_mm"), 1)
            for w, name in enumerate(("wq", "wk")):
                slot = arrived((name, 0))
                for h in range(HEADS):
                    w8 = piece(slot, KD, 512)
                    for k in range(KD):
                        last = mm(half(4 * w + h), w8[:, k, h * P:h * P + P], hT[:, k].rearrange("p g t -> p (g t)"),
                                  start=k == 0, stop=k == KD - 1)
                    if h % 2:
                        last.then_inc(s("gla_proj"), 1)
                if w == 0:
                    gates(pe, 0)
                    ada_at("queries")
            for h in range(2):
                slot = arrived(("wv", h))
                for g in range(G):
                    b = (2 * h + g) % 4
                    pe.wait_ge(s("qk_ready"), 1 + b)
                    for k in range(KD):
                        last = mm(bank[b][:], hT[:, k, g], piece(slot, KD, 512)[:, k, :], start=k == 0, stop=k == KD - 1)
                    last.then_inc(s("gla_proj"), 1)
            gates(pe, 1)
            ada_at("values")
            pe.wait_ge(s("v_ready"), 4)
            for m in range(4):
                mm(bank[m][:], zeros[:], zeros[:, 0:1].broadcast_to([P, 512]), start=True, stop=False,
                   skip_group_check=True)

            def g_tiles(first, end, after):
                pe.wait_ge(s("mod_ready"), adas_until(after, layers))
                for m in range(first, end):
                    slot = arrived(("wg", m // 4))
                    if m == 3:
                        pe.wait_ge(s("kdr_ready"), 2)
                    if m:
                        pe.wait_ge(s("g_raw"), m - 1 if 3 <= m < 7 else m)
                    project(bank[g_bank(m)][:, 0:NT], slot, m % 4, "gla_proj")

            def k_rows(d):
                pe.wait_ge(s("kd_ready"), d + 1)
                for g in range(G):
                    if g or d:
                        pe.wait_ge(s("kdr_ready"), 2 * d + g)
                    for h in range(HEADS):
                        last = tr(bank[6][:, h * P:h * P + P], kdT[:, h, g], ident)
                    last.then_inc(s("kd_tr"), 1)

            g_tiles(0, 1, "values")
            for d in range(2):
                pe.wait_ge(s("qke_ready"), 2 * d + 2)
                pe.wait_ge(s("upd_read"), 3 * d) if d else pe.wait_ge(s("gate_x"), 2)
                for g in range(G):
                    for h in range(HEADS):
                        last = mm(bank[4 + g][:, h * P:h * P + P], ke[:, h, g], qe[:, h, g])
                    last.then_inc(s("scores_mm"), 1)
                if d == 0:
                    k_rows(0)
                    g_tiles(1, 2, "values")
                else:
                    g_tiles(7, 8, "between")
                for g in range(G):
                    pe.wait_ge(s("sc_ready"), 2 * d + g + 1)
                    for m in range(KD):
                        last = mm(half(m)[:, g * L:g * L + L], vrow[:, g, m * P:m * P + P], sc[:, g, m // 2, :],
                                  start=False, stop=False, skip_group_check=True)
                last.then_inc(s("intra_mm"), 1)
                pe.wait_ge(s("kdr_ready"), 2 * d + 2)
                pe.wait_ge(s("s0_loaded"), 32)
                steps = (((1, d), (1, d, s0[:, d])), ((0, d), (1, 1 - d, s1l)), ((0, 1 - d), (0, 1 - d, s1c)))
                for n, ((g, c), (gi, ci, st)) in enumerate(steps):
                    if n:
                        pe.wait_ge(s("upd_read"), 3 * d + n)
                    for h in range(HEADS):
                        last = mm(bank[4 + h // 2][:, (h % 2) * DV:(h % 2) * DV + DV],
                                  kdr[c * CH:c * CH + CH, g, h, :], vrow[c * CH:c * CH + CH, g, h * DV:h * DV + DV])
                    last.then_inc(s("upd_mm"), 1)
                    for m in range(KD):
                        last = mm(half(m)[:, gi * L + ci * CH:gi * L + ci * CH + CH],
                                  st[:, m // 2, (m % 2) * P:(m % 2) * P + P], qe[:, m // 2, gi, ci * CH:ci * CH + CH],
                                  start=False, stop=False, skip_group_check=True)
                last.then_inc(s("o_mm"), 1)
                if d == 0:
                    g_tiles(2, 7, "values")
                    pe.wait_ge(s("g_raw"), 6)
                    k_rows(1)
                    pe.wait_ge(s("g_raw"), 7)
                    ada_at("between")
            pe.wait_ge(s("g_raw"), 8)
            ada_at("heads")
            pe.wait_ge(s("upd_read"), 6)
            for h in range(HEADS):
                pe.wait_ge(s("osq_ready"), h + 1)
                dst = bank[4 + h // 2][:, (h % 2) * NT:(h % 2) * NT + NT]
                for t in range(2):
                    last = mm(dst, ones[:], osq[:, 2 * h + t], start=t == 0, stop=t == 1)
                if h % 2:
                    last.then_inc(s("osum_mm"), 1)
            residual(1, "wo", oT, lambda k: pe.wait_ge(s("o_ready"), k + 1))

        def gates(pe, d):
            if d == 0:
                pe.wait_ge(s("gk1_ready"), 1)
            else:
                pe.wait_ge(s("gate_x"), 1)
            for h in range(HEADS):
                last = mm(bank[4 + h // 2][:, (h % 2) * NT:(h % 2) * NT + NT], wg2[0:32, d, h * P:h * P + P],
                          gk1[0:32, :])
            last.then_inc(s("gate_mm"), 1)

        @block.tensor
        def _(pe):
            reg = fb_count(pe, "pe_extra_pairs")
            prime(pe, "h1_mm", "h3_mm", "hidT_mm", "selT_mm", "y_mm", "scattered")

            def arrived(what):
                slot, nth = where[what]
                pe.wait_ge(s(f"full{slot}"), 16 * (nth + 1))
                return slot

            def ada(i, q):
                n = 3 * i + q
                if n:
                    pe.wait_ge(s("mod_ready"), n)
                slots = [arrived(("ada", i, q, j)) for j in range(4)]
                for k in range(KD):
                    for j in range(4):
                        last = mm(bank[7][32 * j:32 * j + 32, :], condT[:, k, :], piece(slots[j], KD, 512)[:, k, :],
                                  start=k == 0, stop=k == KD - 1)
                last.then_inc(s("ada_mm"), 1)
                pe.wait_ge(s("ada_rows"), n + 1)
                for t in range(4):
                    last = tr(bank[7][:, t * P:t * P + P], rows[:, t * P:t * P + P], ident)
                last.then_inc(s("ada_tr"), 1)

            def ada_at(point):
                for n in ADA_AT[point]:
                    if n < 3 * layers:
                        ada(n // 3, n % 3)

            def sum_squares(n, k):
                pe.wait_ge(s("squares"), KD * n + k + 1)
                ins = mm(bank[6][:, 0:NT], ones[:], hT[:, k].rearrange("p g t -> p (g t)"),
                         start=k == 0, stop=k == KD - 1)
                if k == KD - 1:
                    ins.then_inc(s("square_sum"), 1)

            def norm(n):
                if n:
                    pe.wait_ge(s("squares_added"), (KD - 2) * n)
                for k in (0, KD - 1) if n else range(KD):
                    sum_squares(n, k)

            def h_ready(n, k):
                pe.wait_ge(s("h0_ready"), KD * n + k + 1)
                pe.wait_ge(s("h1_ready"), KD * n + k + 1)

            def project(dst, slot, t, done, rhs=None, ready=None):
                w = piece(slot, KD, 512)
                for k in range(KD):
                    if ready:
                        ready(k)
                    last = mm(dst, w[:, k, t * P:t * P + P],
                              (hT[:, k] if rhs is None else rhs[:, k]).rearrange("p g t -> p (g t)"),
                              start=k == 0, stop=k == KD - 1)
                last.then_inc(s(done), 1)

            def residual(i, name, rhs, ready=None):
                for m in range(KD):
                    if m % 4 == 0:
                        slot = arrived((name, m // 4))
                    if m >= 4:
                        pe.wait_ge(s("y_biased"), KD * i + m - 3)
                    project(bank[m % 4][:, 0:NT], slot, m % 4, "res_mm", rhs, ready if m == 0 else None)
                norm(2 * i + 1)

            def moe_round(pre, b, i):
                nbase = moe_uses[i] if pre == "" else None

                def filled(n, p):
                    slot = moe_slots[i][n]
                    if pre == "" and n >= 4:
                        pe.wait_ge(s(f"full{slot}"), (p + nbase[n]) * 16)
                    elif pre == "":
                        pe.wait_ge(s(f"full{slot}"), (p + (nbase[n] + 1)) * 16)
                    else:
                        pe.wait_ge(s(f"fb_full{n}"), (b + p + 1) * 16)

                def gather(h):
                    for k in range(4 * h, 4 * h + 4):
                        for g in range(G):
                            last = mm(bank[6 + h][:, (k % 4) * P:(k % 4) * P + P], htok[:, g, k * P:k * P + P],
                                      sel[:, g].rearrange("p e n -> p (e n)"), start=g == 0, stop=g == G - 1)
                    last.then_inc(s(pre + "gathered"), 1)

                def pair(p, more, first=False):
                    n = b + p
                    pe.wait_ge(s(pre + "xg_ready"), n * 2 + 2)
                    pe.wait_ge(s(pre + "hidT_ready"), primed(n))
                    for kind, done in ((0, "h1_mm"), (1, "h3_mm")):
                        if kind == 1:
                            pe.wait_ge(s(pre + "selT_ready"), primed(n))
                        filled(2 * kind, p)
                        filled(2 * kind + 1, p)
                        for k in range(KD):
                            for e in range(2):
                                last = mm(bank[4 + kind][SLOTS * e:SLOTS * e + SLOTS, :],
                                          xg[:, k, SLOTS * e:SLOTS * e + SLOTS],
                                          piece(moe_slots[i][2 * kind + e], KD, FF)[:, k, :], start=k == 0, stop=k == KD - 1)
                        last.then_inc(s(pre + done), 1)
                    if more:
                        pe.wait_ge(s(pre + "sel_ready"), n + 2)
                        pe.wait_ge(s(pre + "yv_lo"), primed(n))
                        gather(0)
                    pe.wait_ge(s(pre + "hid_ready"), primed(n + 1))
                    for f in range(4):
                        last = tr(bank[4][:, f * P:f * P + P], hid[:, f * P:f * P + P], ident)
                    last.then_inc(s(pre + "hidT_mm"), 1)
                    if more:
                        pe.wait_ge(s(pre + "yv_hi"), primed(n))
                        gather(1)
                    pe.wait_ge(s(pre + "selw_ready"), n + 1)
                    for g in range(G):
                        last = tr(bank[5][:, g * P:g * P + P], selw[:, g].rearrange("p e n -> p (e n)"), ident)
                    last.then_inc(s(pre + "selT_mm"), 1)
                    pe.wait_ge(s(pre + "hidT_ready"), primed(n + 1))
                    if first:
                        w2 = first_w2[i]
                        pe.wait_ge(s("first_w2_loaded"), 32 * (i + 1))
                    else:
                        w2 = [piece(moe_slots[i][4 + e], 4, D) for e in range(2)]
                        filled(4, p)
                        filled(5, p)
                    for h in range(2):
                        if more:
                            pe.wait_ge(s(pre + "xg_ready"), n * 2 + 3 + h)
                        for f in range(4):
                            for e in range(2):
                                last = mm(bank[6 + h][SLOTS * e:SLOTS * e + SLOTS, :],
                                          hidT[:, f, SLOTS * e:SLOTS * e + SLOTS],
                                          w2[e][:, f, h * 512:h * 512 + 512], start=f == 0, stop=f == 3)
                        last.then_inc(s(pre + "y_mm"), 1)
                    pe.wait_ge(s(pre + "selT_ready"), primed(n + 1))
                    for m in range(KD):
                        if m % 4 == 0:
                            pe.wait_ge(s(pre + ("yv_hi" if m else "yv_lo")), primed(n + 1))
                        last = mm(half(m), yv[:, m * P:m * P + P], selT[:], start=False, stop=False,
                                  skip_group_check=True)
                        if m in (1, 3, 5) and not more:
                            last.then_inc(s(pre + "summed"), 1)
                    last.then_inc(s(pre + "scattered"), 1)

                for m in range(4):
                    mm(bank[m][:], zeros[:], zeros[:, 0:1].broadcast_to([P, 512]), start=True, stop=False, skip_group_check=True)
                pe.wait_ge(s(pre + "sel_ready"), b + 1)
                gather(0)
                gather(1)
                if pre == "":
                    pair(0, True, first=True)
                with pe.Fori(0 if pre else 1, PAIRS - 1) as p:
                    pair(p, True)
                pair(PAIRS - 1, False)

            def moe(i):
                pe.wait_ge(s("rw_loaded"), 32 * (i + 1))
                for k in range(KD):
                    h_ready(2 * i + 1, k)
                    last = mm(bank[4][0:20, 0:NT], rw[:, k, :], hT[:, k].rearrange("p g t -> p (g t)"),
                              start=k == 0, stop=k == KD - 1)
                last.then_inc(s("logits_mm"), 1)
                for g in range(G):
                    for k in range(KD):
                        last = tr(bank[2 * g + k // 4][:, (k % 4) * P:(k % 4) * P + P], hT[:, k, g], ident)
                    if g == 0:
                        last.then_inc(s("htok_tr"), 1)
                        pe.wait_ge(s("logits"), i + 1)
                        for gg in range(G):
                            lt = tr(bank[5][:, gg * 32:gg * 32 + 20], lraw[0:20, gg * P:gg * P + P], ident[0:20, 0:20])
                        lt.then_inc(s("logits_tr"), 1)
                last.then_inc(s("htok_tr"), 1)
                pe.wait_ge(s("members"), i + 1)
                mb = [memb[:, g, :] for g in range(G)]
                mm(bank[4][:, 0:16], upper16[:], mb[0], start=True, stop=True)
                mm(bank[4][:, 16:32], upper16[:], mb[1], start=True, stop=False)
                mm(bank[4][:, 16:32], ones16[:], mb[0], start=False, stop=True)
                mm(bank[4][:, 32:48], ones16[:], mb[0], start=True, stop=False)
                mm(bank[4][:, 32:48], ones16[:], mb[1], start=False, stop=True).then_inc(s("ranks_mm"), 1)
                pe.wait_ge(s("htok_ready"), 2 * (i + 1))
                moe_round("", PAIRS * i, i)
                rounds = needed_rounds(pe, i)

                def one_round(b):
                    pe.wait_ge(s("x_added"), KD * (2 * i + 2))
                    pe.wait_ge(s("fb_rounds_added"), primed(b // PAIRS))
                    moe_round("fb_", b, i)

                further_rounds(pe, i, rounds, reg, one_round)

            pe.wait_ge(s("base_loaded"), 16)
            filter_rows = sum(t == 3 for _, t, _, _ in vec_layout())
            pe.wait_ge(s("filter_rows_loaded"), 16 * filter_rows)
            tr(bank[6][:, 0:P], vrows[:, 3, :], ident).then_inc(s("vec_tr"), 1)
            pe.wait_ge(s("filter_loaded"), 16 * 3)
            mm(bank[5][0:HY_HID, 0:L], fsmall[0:HY_EMB, 1, 0:HY_HID], fsmall[0:HY_EMB, 0, :]).then_inc(s("f_mm"), 1)
            pe.wait_ge(s("vrows_loaded"), 16 * (len(vec_layout()) - filter_rows))
            for t in range(3):
                last = tr(bank[7][:, t * P:t * P + P], vrows[:, t, :], ident)
            last.then_inc(s("vec_tr"), 1)
            pe.wait_ge(s("f_sin"), 1)
            mm(bank[5][0:HY_HID, 0:L], fsmall[0:HY_HID, 2, 0:HY_HID], fsmall[0:HY_HID, 4, :]).then_inc(s("f_mm"), 1)
            pe.wait_ge(s("x_loaded"), 32)
            for k in range(KD):
                for g in range(G):
                    last = tr(half(k)[:, g * L:g * L + L], xin[:, g, k * P:k * P + P], ident)
                if k % 2:
                    last.then_inc(s("x_tr"), 1)

            FRE, FIM, KIM, KD_, IRE, IIM = [cm[:, n * P:n * P + P] for n in range(6)]
            pe.wait_ge(s("f_sin"), 2)
            pe.wait_ge(s("w3_loaded"), 32)
            for c in range(8):
                if c >= 2:
                    pe.wait_ge(s("kfb_ready"), c - 1)
                if c == 4:
                    pe.wait_ge(s("f_backward"), 1)
                mm(bank[4 + c % 2][:], fsmall[0:HY_HID, 5 + 2 * (c // 4), :], w3f[0:HY_HID, c * 512:c * 512 + 512]) \
                    .then_inc(s("f3_mm"), 1)
            pe.wait_ge(s("dft_loaded"), 16)
            pe.wait_ge(s("x_copied"), 4)
            norm(0)
            for c in range(12):
                w, o, h = c // 4, (c // 2) % 2, c % 2
                if c < 4:
                    pe.wait_ge(s("k_even"), c + 1)
                elif w == 1:
                    pe.wait_ge(s("k_odd"), c - 3)
                if c >= 4:
                    pe.wait_ge(s("spec_ready"), c - 3)
                mm(bank[c % 4][:], (FRE, KIM, KD_)[w], (k_odd if w == 1 else k_even)[:, o, h * 512:h * 512 + 512]) \
                    .then_inc(s("spec_mm"), 1)
            pe.wait_ge(s("cond_ready"), 3)
            ada_at("start")
            pe.wait_ge(s("spec_ready"), 12)
            for m in range(24):
                if m % 4 == 0:
                    slot = arrived(("w_in", m // 4))
                if m >= 4:
                    pe.wait_ge(s("up_ready"), m - 3)
                project(bank[m % 4][:, 0:NT], slot, m % 4, "win_mm",
                        ready=(lambda k: h_ready(0, k)) if m == 0 else None)
                if m in (7, 15):
                    ada_at(f"w_in{m // 4}")
            pe.wait_ge(s("up_ready"), 24)

            def to_rows(n):
                if n < 2:
                    pe.wait_ge(s("conv_ready"), 8)
                if n:
                    pe.wait_ge(s("zt_ready"), 2 * n)
                if n > 1:
                    pe.wait_ge(s("z_ready"), n - 1)
                for k in range(KD):
                    last = tr(bank[4 + k // 4][:, (k % 4) * P:(k % 4) * P + P], uT[:, k, n % G], ident)
                last.then_inc(s("zt_tr"), 1)

            def forward(n):
                pe.wait_ge(s("zt_ready"), 2 * n + 2)
                if n:
                    pe.wait_ge(s("prods"), 4 * n)
                for w, f in enumerate((FRE, FIM)):
                    for h in range(2):
                        last = mm(bank[2 * w + h][:], f, zt[:, n % G, h * 512:h * 512 + 512])
                last.then_inc(s("zf_mm"), 1)

            def inverse(n):
                pe.wait_ge(s("yspec"), 2 * n + 2)
                pe.wait_ge(s("zt_ready"), min(2 * n + 4, 8))
                if n:
                    pe.wait_ge(s("z_ready"), n)
                for k in range(KD):
                    dst = bank[4 + k // 4][:, (k % 4) * P:(k % 4) * P + P]
                    mm(dst, ysp[:, 0, k * P:k * P + P], IRE, start=True, stop=False)
                    last = mm(dst, ysp[:, 1, k * P:k * P + P], IIM, start=False, stop=True)
                last.then_inc(s("zi_mm"), 1)

            to_rows(0)
            ada_at("w_in5")
            forward(0)
            to_rows(1)
            ada_at("conv0")
            forward(1)
            inverse(0)
            to_rows(2)
            forward(2)
            inverse(1)
            to_rows(3)
            ada_at("conv1")
            forward(3)
            inverse(2)
            ada_at("conv2")
            inverse(3)
            pe.wait_ge(s("z_ready"), 4)
            residual(0, "w_out", rhs=uT)
            moe(0)

            if layers > 1:
                pe_gla(pe, arrived, ada_at, norm, h_ready, project, residual)
                moe(1)

            if layers > 2:
                norm(4)
                pe.wait_ge(s("cm_loaded"), 16 * 5)
                cg, cl, sl = cm[:, 0:1024].rearrange("p (k n) -> p k n", k=2), cm[:, 1024:1152], cm[:, 1152:1280]
                for g in range(G):
                    for r in range(4):
                        n = 4 * g + r
                        if n >= 4:
                            pe.wait_ge(s("fn_rows"), n - 3)
                        for k in range(2):
                            if g == 0:
                                h_ready(4, 2 * r + k)
                            last = mm(bank[n % 4][:], hT[:, 2 * r + k, g], cg[:, k, :], start=k == 0, stop=k == 1)
                        last.then_inc(s("fn_ch_mm"), 1)
                ada_at("fnet")
                pe.wait_ge(s("fn_rows"), 8)
                for m in range(KD):
                    for g in range(G):
                        dst = half(m)[:, g * L:g * L + L]
                        rws = fnp[:, g, m // 2]
                        mm(dst, rws[:, (m % 2) * P:(m % 2) * P + P], cl, start=True, stop=False)
                        last = mm(dst, rws[:, 256 + (m % 2) * P:256 + (m % 2) * P + P], sl, start=False, stop=True)
                    if m % 2:
                        last.then_inc(s("fn_tok_mm"), 1)
                pe.wait_ge(s("fn_mixed"), 4)
                residual(2, "fn", rhs=fnm)
                moe(2)

            if layers > 3:
                norm(6)
                slot = arrived(("pool", 0))
                pe.wait_ge(s("cm_loaded"), 16 * 6)
                pw = piece(slot, KD, 256)
                for g in range(G):
                    for r in range(4):
                        n = 4 * g + r
                        dst = bank[n // 2][:, (n % 2) * 256:(n % 2) * 256 + 256]
                        for k in range(2):
                            if g == 0:
                                h_ready(6, 2 * r + k)
                            last = mm(dst, hT[:, 2 * r + k, g], pw[:, 2 * r + k, :], start=k == 0, stop=k == 1)
                        if r % 2:
                            last.then_inc(s("pool_hw"), 1)
                pe.wait_ge(s("pool_rows"), 4)
                for m in range(KD):
                    for g in range(G):
                        last = mm(half(m)[:, g * L:g * L + L], plr[:, g, m // 2, (m % 2) * P:(m % 2) * P + P],
                                  cm[:, (4 * g + m // 2) * P:(4 * g + m // 2) * P + P])
                    last.then_inc(s("res_mm"), 1)
                norm(7)
                moe(3)

            for g in range(G):
                for k in range(KD):
                    if g == 0:
                        pe.wait_ge(s("squares"), KD * 2 * layers + k + 1)
                    last = tr(bank[4 * (1 - g) + k // 4][:, (k % 4) * P:(k % 4) * P + P], xT[:, k, g], ident)
                    if k % 4 == 3:
                        last.then_inc(s("out_tr"), 1)
                if g == 0:
                    norm(2 * layers)
            pe.wait_ge(s("rstd_ready"), 2 * layers + 1)
            for g in range(G):
                last = tr(bank[7][:, g * P:g * P + P], rstd[:, g], ident)
            last.then_inc(s("rstd_tr"), 1)

        @block.scalar
        def _(act):
            reg = fb_count(act, "act_extra_pairs")
            prime(act, "selT_ready", "yv_lo")
            act_fn = nc.scalar.activation
            chained = [0]

            def chain(ins):
                chained[0] += 1
                ins.then_inc(s("act_chain"), 1)
                act.wait_ge(s("act_chain"), chained[0])

            act.dma_start(base[:], a["c_base"]).then_inc(s("base_loaded"), 16)
            act.wait_ge(s("vrows_clear"), 1)
            vector_loads(act, 0)

            def square(n, k):
                if n:
                    act.wait_ge(s("x_added"), KD * (n - 1) + k + 1)
                else:
                    act.wait_ge(s("x_copied"), k // 2 + 1)
                act_fn(hT[:, k], xT[:, k], ACT.Square).then_inc(s("squares"), 1)

            def load_table(fn):
                act_fn(small[:, 4:5], one, fn)

            def inverse_root(n):
                act.wait_ge(s("square_sum"), n + 1)
                chain(act_fn(rstd[:].rearrange("p g t -> p (g t)"), bank[6][:, 0:NT], ACT.Ln, bias=eps, scale=1.0 / D))
                act_fn(rstd[:], rstd[:], ACT.Exp, scale=-0.5).then_inc(s("rstd_ready"), 1)

            def norm(n):
                load_table(ACT.Ln)
                for k in range(KD):
                    square(n, k)
                inverse_root(n)

            def shift(n):
                i, w = n // 2, n % 2
                for k in range(KD):
                    act.wait_ge(s("normed"), KD * n + k + 1)
                    act_fn(hT[:, k, 0], hT[:, k, 0], ACT.Identity, bias=mod[:, i, 24 * w + k, 0:1],
                           scale=scale[:, i, w, k, 0:1]).then_inc(s("h0_ready"), 1)

            def residual(i, bias, src):
                for m in range(KD):
                    act.wait_ge(s("res_mm"), KD * i + m + 1 if i < 3 else KD * i + (m | 1) + 1)
                    if m >= 4:
                        act.wait_ge(s("x_added"), KD * 2 * i + m - 3)
                    ins = dict(bias=vcol(bias, m)) if bias else {}
                    act_fn(yb[:, m % 4], src(m), ACT.Identity, **ins).then_inc(s("y_biased"), 1)
                    if m == 0:
                        load_table(ACT.Ln)
                    square(2 * i + 1, m)

            quarter = lambda m: bank[m % 4][:, 0:NT]

            def evac(pre, n):
                for h in range(2):
                    act.wait_ge(s(pre + "gathered"), n * 2 + h + 1)
                    act_fn(xg[:, 4 * h:4 * h + 4], psum_tok(6 + h, 4), ACT.Copy).then_inc(s(pre + "xg_ready"), 1)

            def moe_round(pre, b):
                def pair(p, more):
                    n = b + p
                    act.wait_ge(s(pre + "h1_mm"), primed(n + 1))
                    act.wait_ge(s(pre + "hid_ready"), primed(n))
                    act_fn(sil[:], bank[4][:], ACT.Silu).then_inc(s(pre + "sil_ready"), 1)
                    if more:
                        evac(pre, n + 1)
                    act.wait_ge(s(pre + "selT_mm"), primed(n + 1))
                    act.wait_ge(s(pre + "scattered"), primed(n))
                    act_fn(selT[:], bank[5][:, 0:NT], ACT.Copy).then_inc(s(pre + "selT_ready"), 1)
                    act.wait_ge(s(pre + "y_mm"), primed(n * 2 + 1))
                    act_fn(yv[:, 0:512], bank[6][:], ACT.Copy).then_inc(s(pre + "yv_lo"), 1)

                evac(pre, b)
                with act.Fori(0, PAIRS - 1) as p:
                    pair(p, True)
                pair(PAIRS - 1, False)

            def moe(i):
                inverse_root(2 * i + 1)
                shift(2 * i + 1)
                act.wait_ge(s("logits_mm"), i + 1)
                act_fn(lraw[0:20, :], bank[4][0:20, 0:NT], ACT.Copy).then_inc(s("logits"), 1)
                for g in range(G):
                    act.wait_ge(s("htok_tr"), 2 * i + g + 1)
                    for h in range(2):
                        last = act_fn(htok[:, g, h * 512:h * 512 + 512], bank[2 * g + h][:], ACT.Copy)
                    last.then_inc(s("htok_ready"), 1)
                    act.wait_ge(s("route_in"), 2 * i + g + 1)
                    act_fn(*route_exp[g], ACT.Exp).then_inc(s("route_exp"), 1)
                moe_round("", PAIRS * i)
                rounds = needed_rounds(act, i)

                def one_round(b):
                    act.wait_ge(s("x_added"), KD * (2 * i + 2))
                    act.wait_ge(s("fb_rounds_added"), primed(b // PAIRS))
                    moe_round("fb_", b)
                    act.wait_ge(s("fb_rounds_added"), primed(b // PAIRS + 1))

                further_rounds(act, i, rounds, reg, one_round)

            for n in range(2):
                act.wait_ge(s("f_arg"), n + 1)
                act_fn(fsmall[0:HY_HID, 4 + n, :], fsmall[0:HY_HID, 3, :], ACT.Sin).then_inc(s("f_sin"), 1)

            act.wait_ge(s("vec_ready"), 2)
            act.wait_ge(s("cond_ready"), 1)
            for g, name in enumerate(("c_ctx", "c")):
                act_fn(condT[:, :, g], vcol(name, 0, KD), ACT.Silu).then_inc(s("cond_ready"), 1)

            def spectrum(c):
                act.wait_ge(s("spec_mm"), c + 1)
                act_fn(spec[:, c // 4, (c // 2) % 2, (c % 2) * 512:(c % 2) * 512 + 512], bank[c % 4][:], ACT.Copy) \
                    .then_inc(s("spec_ready"), 1)

            norm(0)
            for c in range(12):
                spectrum(c)
            shift(0)
            act.wait_ge(s("up_clear"), 1)
            for m in range(24):
                act.wait_ge(s("win_mm"), m + 1)
                if m >= 4:
                    act.wait_ge(s("conv_ready"), m - 3)
                act_fn(up[:, m % 4, :, 1:L + 1], bank[m % 4][:, 0:NT].rearrange("p (g t) -> p g t", g=G), ACT.Identity,
                       bias=vcol("hy_b_in", m)).then_inc(s("up_ready"), 1)
            for n in range(4):
                act.wait_ge(s("zt_tr"), n + 1)
                for h in range(2):
                    act_fn(zt[:, n % 2, h * 512:h * 512 + 512], bank[4 + h][:], ACT.Copy).then_inc(s("zt_ready"), 1)
            residual(0, "hy_b_out", quarter)
            moe(0)
            if layers > 1:
                norm(2)
                shift(2)
                for b in range(2):
                    act.wait_ge(s("gla_proj"), b + 1)
                    act_fn(qT[:, 2 * b:2 * b + 2], bank[b][:].rearrange("p (h g t) -> p h g t", h=2, g=G),
                           ACT.Copy, scale=DK ** -0.5).then_inc(s("qk_ready"), 1)

                def gate_logs(d):
                    act.wait_ge(s("gate_mm"), d + 1)
                    if d:
                        act.wait_ge(s("kd_ready"), 1)
                    for h in range(HEADS):
                        last = act_fn(gx[:, h * NT:h * NT + NT], bank[4 + h // 2][:, (h % 2) * NT:(h % 2) * NT + NT],
                                      ACT.Identity, bias=vcol("gla_b_gk", 4 * d + h))
                    last.then_inc(s("gate_x"), 1)
                    act.wait_ge(s("gate_x"), d + 1)
                    chain(act_fn(gt[:], gx[:], ACT.Abs))
                    chain(act_fn(gt[:], gt[:], ACT.Exp, scale=-1.0))
                    act_fn(gt[:], gt[:], ACT.Ln, bias=one).then_inc(s("gate_ln"), 1)

                def gate_k(d):
                    act.wait_ge(s("gate_cum"), 2 * d + 1)
                    act_fn(e2[:], gt[:], ACT.Exp, scale=-1.0 / 16).then_inc(s("k_exp"), 1)
                    act.wait_ge(s("gate_cum"), 2 * d + 2)
                    act_fn(gx[:], gx[:], ACT.Exp, scale=1.0 / 16).then_inc(s("k_exp"), 1)

                def gate_q(d):
                    if d:
                        act.wait_ge(s("upd_read"), 3)
                    act_fn(e1[:], gt[:], ACT.Exp, scale=1.0 / 16).then_inc(s("q_exp"), 1)

                def k_rows(d):
                    for g in range(G):
                        act.wait_ge(s("kd_tr"), 2 * d + g + 1)
                        act_fn(kdr[:, g], psum_tok(6, 4), ACT.Copy).then_inc(s("kdr_ready"), 1)

                def g_tiles(first, end):
                    for m in range(first, end):
                        act.wait_ge(s("gla_proj"), 9 + m)
                        act_fn(gT[:, m], bank[g_bank(m)][:, 0:NT], ACT.Copy).then_inc(s("g_raw"), 1)

                gate_logs(0)
                for b in range(2, 4):
                    act.wait_ge(s("gla_proj"), b + 1)
                    act_fn(kT[:, 2 * b - 4:2 * b - 2], bank[b][:].rearrange("p (h g t) -> p h g t", h=2, g=G),
                           ACT.Copy).then_inc(s("qk_ready"), 1)
                gate_k(0)
                gate_q(0)
                for n in range(4):
                    act.wait_ge(s("gla_proj"), 5 + n)
                    act_fn(vrow[:, n % 2, (n // 2) * 512:(n // 2) * 512 + 512], bank[n][:], ACT.Copy) \
                        .then_inc(s("v_ready"), 1)
                gate_logs(1)
                g_tiles(0, 1)
                k_rows(0)
                g_tiles(1, 2)
                gate_k(1)
                gate_q(1)
                g_tiles(2, 7)
                k_rows(1)
                g_tiles(7, 8)
                act.wait_ge(s("g_raw"), 8)
                act_fn(gT, gT, ACT.Silu).then_inc(s("g_ready"), 1)
                load_table(ACT.Ln)
                act.wait_ge(s("o_mm"), 2)
                for b in range(4):
                    act_fn(osq[:, 2 * b:2 * b + 2], bank[b][:].rearrange("p (h t) -> p h t", h=2), ACT.Square) \
                        .then_inc(s("osq_ready"), 1)
                for b in range(2):
                    act.wait_ge(s("osum_mm"), b + 1)
                    o_root = ors[:, 2 * b:2 * b + 2].rearrange("p h t -> p (h t)")
                    last = act_fn(o_root, bank[4 + b][:], ACT.Ln, bias=eps, scale=1.0 / DV)
                chain(last)
                for b in range(2):
                    o_root = ors[:, 2 * b:2 * b + 2].rearrange("p h t -> p (h t)")
                    act_fn(o_root, o_root, ACT.Exp, scale=-0.5).then_inc(s("ors_ready"), 1)
                residual(1, None, quarter)
                moe(1)
            if layers > 2:
                norm(4)
                shift(4)
                for n in range(8):
                    act.wait_ge(s("fn_ch_mm"), n + 1)
                    act_fn(fnp[:, n // 4, n % 4], bank[n % 4][:], ACT.Copy).then_inc(s("fn_rows"), 1)
                for b in range(4):
                    act.wait_ge(s("fn_tok_mm"), b + 1)
                    act_fn(fnm[:, 2 * b:2 * b + 2], bank[b][:].rearrange("p (h g t) -> p h g t", h=2, g=G), ACT.Copy) \
                        .then_inc(s("fn_mixed"), 1)
                residual(2, "fn_b_out", quarter)
                moe(2)
            if layers > 3:
                norm(6)
                shift(6)
                for b in range(4):
                    act.wait_ge(s("pool_hw"), b + 1)
                    act_fn(plr[:, b // 2, 2 * (b % 2):2 * (b % 2) + 2], bank[b][:].rearrange("p (r n) -> p r n", r=2),
                           ACT.Copy).then_inc(s("pool_rows"), 1)
                residual(3, "pool_b", half)
                moe(3)
            norm(2 * layers)
            for g, name in enumerate(("y_prompt", "y_sample")):
                act.wait_ge(s("out_rows"), 2 * g + 2)
                act.dma_start(a[name][0][:, 512:D], xout[:, g, 512:D]).then_inc(s("stored"), 16)

        @block.vector
        def _(dve):
            reg = fb_count(dve, "dve_extra_pairs")
            prime(dve, "hid_ready", "hidT_ready", "yv_hi")
            dve.sem_inc(s("fb_rounds_added"), 1)
            v = nc.vector
            tt, ts, stt = v.tensor_tensor, v.tensor_scalar, v.scalar_tensor_tensor
            chained = [0]

            def chain(ins):
                chained[0] += 1
                ins.then_inc(s("dve_chain"), 1)
                dve.wait_ge(s("dve_chain"), chained[0])

            def ada(i, q):
                n = 3 * i + q
                dve.wait_ge(s("ada_mm"), n + 1)
                v.tensor_copy(rows[:], bank[7][:]).then_inc(s("ada_rows"), 1)
                dve.wait_ge(s("ada_tr"), n + 1)
                src = bank[7][:].rearrange("p (t j r) -> p j t r", t=4, j=4)[:, :, :, 0:G]
                dst = mod[:, i, 16 * q:16 * q + 16].rearrange("p (j t) g -> p j t g", j=4)
                bia = b_ada(i, 16 * q, 16).rearrange("p (j t) -> p j t", j=4).unsqueeze(3).broadcast_to([P, 4, 4, G])
                tt(dst, src, bia, ALU.add).then_inc(s("mod_ready"), 1)
                dve.wait_ge(s("mod_ready"), n + 1)
                if q != 1:
                    w = q // 2
                    ng = vcol("norm_g", 16 * i + 8 * w, KD).unsqueeze(2).broadcast_to([P, KD, G])
                    chain(stt(scale[:, i, w], mod[:, i, 24 * w + 8:24 * w + 16], 1.0, ng, ALU.add, ALU.mult))

            def ada_at(point):
                for n in ADA_AT[point]:
                    if n < 3 * layers:
                        ada(n // 3, n % 3)

            def norm(n):
                i, w = n // 2, n % 2
                dve.wait_ge(s("rstd_ready"), n + 1)
                for k in range(KD + 1):
                    if k < KD:
                        tt(hT[:, k], xT[:, k], rstd[:], ALU.mult).then_inc(s("normed"), 1)
                    if k:
                        dve.wait_ge(s("normed"), KD * n + k)
                        ts(hT[:, k - 1, 1], hT[:, k - 1, 1], scale[:, i, w, k - 1, 1:2],
                           mod[:, i, 24 * w + k - 1, 1:2], ALU.mult, ALU.add).then_inc(s("h1_ready"), 1)

            def residual(i, gate):
                for m in range(KD):
                    dve.wait_ge(s("y_biased"), KD * i + m + 1)
                    for g in range(G):
                        last = stt(xT[:, m, g], yb[:, m % 4, g * L:g * L + L], gate(m, g), xT[:, m, g],
                                   ALU.mult, ALU.add)
                    last.then_inc(s("x_added"), 1)

            g1 = lambda i: lambda m, g: mod[:, i, 16 + m, g:g + 1]

            def build_sel(pre, n, p):
                r = rank[:, :, bass.ds(p * 2, 2)].unsqueeze(3).broadcast_to([P, G, 2, SLOTS])
                io = iota.unsqueeze(1).unsqueeze(1).broadcast_to([P, G, 2, SLOTS])
                tt(sel[:], io, r, ALU.is_equal).then_inc(s(pre + "sel_ready"), 1)

            def moe_round(pre, b, i):
                def pair(p, more):
                    n = b + p
                    dve.wait_ge(s(pre + "sel_ready"), n + 1)
                    dve.wait_ge(s(pre + "selT_mm"), primed(n))
                    c = comb[:, :, bass.ds(p * 2, 2)].unsqueeze(3).broadcast_to([P, G, 2, SLOTS])
                    tt(selw[:], sel[:], c, ALU.mult).then_inc(s(pre + "selw_ready"), 1)
                    if more:
                        dve.wait_ge(s(pre + "gathered"), n * 2 + 2)
                        dve.wait_ge(s(pre + "selw_ready"), n + 1)
                        build_sel(pre, n + 1, p + 1)
                    dve.wait_ge(s(pre + "sil_ready"), n + 1)
                    dve.wait_ge(s(pre + "h3_mm"), primed(n + 1))
                    dve.wait_ge(s(pre + "hidT_mm"), primed(n))
                    tt(hid[:], sil[:], bank[5][:], ALU.mult).then_inc(s(pre + "hid_ready"), 1)
                    dve.wait_ge(s(pre + "hidT_mm"), primed(n + 1))
                    dve.wait_ge(s(pre + "y_mm"), primed(n * 2))
                    v.tensor_copy(hidT[:], psum_tok(4, 4)).then_inc(s(pre + "hidT_ready"), 1)
                    dve.wait_ge(s(pre + "y_mm"), primed(n * 2 + 2))
                    dve.wait_ge(s(pre + "scattered"), primed(n))
                    v.tensor_copy(yv[:, 512:1024], bank[7][:]).then_inc(s(pre + "yv_hi"), 1)

                if pre:
                    build_sel(pre, b, 0)
                with dve.Fori(0, PAIRS - 1) as p:
                    pair(p, True)
                pair(PAIRS - 1, False)
                for m in range(KD):
                    if m in (0, 2, 4):
                        dve.wait_ge(s(pre + "summed"), b // PAIRS * 3 + m // 2 + 1)
                    elif m == 6:
                        dve.wait_ge(s(pre + "scattered"), primed(b + PAIRS))
                    for g in range(G):
                        last = stt(xT[:, m, g], half(m)[:, g * L:g * L + L], mod[:, i, 40 + m, g:g + 1],
                                   xT[:, m, g], ALU.mult, ALU.add)
                    if pre == "":
                        last.then_inc(s("x_added"), 1)
                if pre:
                    last.then_inc(s("fb_rounds_added"), 1)

            def first_best(out, vals, m):
                chain(tt(r_key, vals, m.unsqueeze(2).broadcast_to([P, G, 4]), ALU.is_equal))
                chain(tt(r_key, r_key, tie.unsqueeze(1).broadcast_to([P, G, 4]), ALU.mult))
                chain(v.reduce_max(r_km, r_key, AX.X))
                chain(tt(out, r_key, r_km.unsqueeze(2).broadcast_to([P, G, 4]), ALU.is_equal))

            def moe(i):
                norm(2 * i + 1)
                dve.wait_ge(s("logits_tr"), i + 1)
                chain(v.tensor_copy(lg[:], bank[5][:, 0:64].rearrange("p (g n) -> p g n", g=G)[:, :, 0:20]))
                b4 = lambda x: x.unsqueeze(2).broadcast_to([P, G, 4])
                chain(v.reduce_max(r_gm, lg[:, :, 0:4], AX.X))
                tt(r_gd, lg[:, :, 0:4], b4(r_gm), ALU.subtract).then_inc(s("route_in"), 1)
                first_best(r_og, lg[:, :, 0:4], r_gm)
                ex = lg[:, :, 4:20].rearrange("p g (q e) -> p g e q", q=4)
                chain(tt(r_x4, ex, r_og.unsqueeze(2).broadcast_to([P, G, 4, 4]), ALU.mult))
                chain(v.reduce_sum(r_le, r_x4, AX.X))
                chain(v.reduce_max(r_m1, r_le, AX.X))
                first_best(r_o1, r_le, r_m1)
                chain(stt(r_le2, r_o1, -1e30, r_le, ALU.mult, ALU.add))
                chain(v.reduce_max(r_m2, r_le2, AX.X))
                tt(r_dd, r_m2, r_m1, ALU.subtract).then_inc(s("route_in"), 1)
                first_best(r_o2, r_le2, r_m2)
                chain(tt(r_mt, r_o1, r_o2, ALU.add))
                tt(memb.rearrange("p g (q e) -> p g q e", q=4), r_og.unsqueeze(3).broadcast_to([P, G, 4, 4]),
                   r_mt.unsqueeze(2).broadcast_to([P, G, 4, 4]), ALU.mult).then_inc(s("members"), 1)
                dve.wait_ge(s("route_exp"), 2 * i + 1)
                chain(v.reduce_sum(r_sg, r_ge, AX.X))
                dve.wait_ge(s("route_exp"), 2 * i + 2)
                chain(stt(r_w2, r_de, 1.0, r_sg, ALU.add, ALU.mult))
                chain(v.reciprocal(r_w1, r_w2))
                chain(tt(r_w2, r_w1, r_de, ALU.mult))
                chain(tt(r_wt, r_o1, b4(r_w1), ALU.mult))
                chain(tt(r_key, r_o2, b4(r_w2), ALU.mult))
                chain(tt(r_wt, r_wt, r_key, ALU.add))
                chain(tt(comb.rearrange("p g (q e) -> p g q e", q=4), r_og.unsqueeze(3).broadcast_to([P, G, 4, 4]),
                         r_wt.unsqueeze(2).broadcast_to([P, G, 4, 4]), ALU.mult))
                dve.wait_ge(s("ranks_mm"), i + 1)
                v.reduce_max(r_mx, bank[4][:, 32:48], AX.X)
                chain(stt(r_rk, bank[4][:, 0:32].rearrange("p (g e) -> p g e", g=G), 1.0, memb, ALU.add, ALU.mult))
                chain(ts(rank[:], r_rk, -1.0, None, ALU.add))
                build_sel("", PAIRS * i, 0)
                for j in range(3):
                    chain(ts(r_rd[:, j:j + 1], r_mx, float(SLOTS * (j + 1)), None, ALU.is_gt))
                chain(ts(r_rd[:, 3:4], r_rd[:, 0:1], 1.0, r_rd[:, 1:2], ALU.add, ALU.add))
                tt(over[0:1, 0:1], r_rd[0:1, 3:4], r_rd[0:1, 2:3], ALU.add).then_inc(s("rounds_known"), 1)
                moe_round("", PAIRS * i, i)
                rounds = needed_rounds(dve, i)

                def one_round(b):
                    dve.wait_ge(s("x_added"), KD * (2 * i + 2))
                    dve.wait_ge(s("fb_rounds_added"), primed(b // PAIRS))
                    ts(rank[:], rank[:], -float(SLOTS), None, ALU.add).then_inc(s("fb_rank"), 1)
                    dve.wait_ge(s("fb_rank"), b // PAIRS + 1)
                    moe_round("fb_", b, i)
                    dve.wait_ge(s("fb_rounds_added"), primed(b // PAIRS + 1))

                further_rounds(dve, i, rounds, reg, one_round)

            v.memset(vrows[:], 0.0).then_inc(s("vrows_clear"), 1)
            v.memset(ones[:], 1.0)
            v.memset(zeros[:], 0.0)
            v.memset(ones16[:], 1.0)
            v.memset(eps, EPS)
            v.memset(one, 1.0)
            v.memset(condT[:], 0.0).then_inc(s("cond_ready"), 1)
            dve.wait_ge(s("vec_tr"), 1)
            v.tensor_copy(vec[:, 3 * P:VECS], bank[6][:, 0:VECS - 3 * P]).then_inc(s("vec_ready"), 1)
            dve.wait_ge(s("vec_ready"), 1)
            H = HY_HID
            big = 1.5 * 2 ** 23
            twopi = 2 * math.pi
            c1 = 6.28125
            c2 = float(np.float32(twopi - c1))
            c2 = math.floor(c2 * 2 ** 20) / 2 ** 20
            c3 = twopi - c1 - c2
            for n, bias in enumerate(("hy_f_b1", "hy_f_b2")):
                dve.wait_ge(s("f_mm"), n + 1)
                arg, turns = fsmall[0:H, 3, :], fsmall[0:H, 6, :]
                if n:
                    dve.wait_ge(s("f_sin"), 1)
                chain(ts(arg, bank[5][0:H, 0:L], vcol(bias, 0)[0:H], vcol("hy_f_freq", 0)[0:H], ALU.add, ALU.mult))
                chain(ts(turns, arg, 1.0 / twopi, big, ALU.mult, ALU.add))
                chain(ts(turns, turns, -big, None, ALU.add))
                chain(stt(arg, turns, -c1, arg, ALU.mult, ALU.add))
                chain(stt(arg, turns, -c2, arg, ALU.mult, ALU.add))
                chain(stt(arg, turns, -c3, arg, ALU.mult, ALU.add))
                pi = 3.1415925
                ts(arg, arg, pi, -pi, ALU.min, ALU.max).then_inc(s("f_arg"), 1)
                if n == 0:
                    dve.wait_ge(s("vec_tr"), 2)
                    v.tensor_copy(vec[:, 0:3 * P], bank[7][:, 0:3 * P]).then_inc(s("vec_ready"), 1)
            for b in range(4):
                dve.wait_ge(s("x_tr"), b + 1)
                v.tensor_copy(xT[:, 2 * b:2 * b + 2], bank[b][:].rearrange("p (k g t) -> p k g t", k=2, g=G)) \
                    .then_inc(s("x_copied"), 1)
            dve.wait_ge(s("f_sin"), 2)
            chain(v.memset(fsmall[0:H, 7, 0:1], 0.0))
            v.tensor_copy(fsmall[0:H, 7, 1:L], fsmall[0:H, 5, 1:L]).then_inc(s("f_backward"), 1)
            for c in range(8):
                dve.wait_ge(s("f3_mm"), c + 1)
                if c == 0:
                    dve.wait_ge(s("window_loaded"), 16)
                o, cols = (c // 2) % 2, slice((c % 2) * 512, (c % 2) * 512 + 512)
                filt = kfb[:, c // 4, o, cols]
                tt(filt, bank[4 + c % 2][:], win[:, cols], ALU.mult).then_inc(s("kfb_ready"), 1)
                if c >= 4:
                    dve.wait_ge(s("kfb_ready"), c + 1)
                    if c == 4:
                        dve.wait_ge(s("x_copied"), 4)
                    tt(k_even[:, o, cols], kfb[:, 0, o, cols], filt, ALU.add).then_inc(s("k_even"), 1)
                    dve.wait_ge(s("k_even"), c - 3)
                    tt(k_odd[:, o, cols], kfb[:, 0, o, cols], filt, ALU.subtract).then_inc(s("k_odd"), 1)
            dve.wait_ge(s("masks_loaded"), 32)
            v.tensor_copy(upper16[:], upper)
            v.tensor_copy(mask[:], mask32).then_inc(s("mask_ready"), 1)
            ada_at("start")
            norm(0)
            dve.wait_ge(s("x_tr"), 4)
            dve.wait_ge(s("vec_tr"), 2)
            v.memset(up[:, :, :, 0:1], 0.0)
            v.memset(up[:, :, :, L + 1:L + 2], 0.0).then_inc(s("up_clear"), 1)
            for m in range(24):
                dve.wait_ge(s("up_ready"), m + 1)
                if m == 0:
                    dve.wait_ge(s("spec_ready"), 12)
                u, src = uT[:, m], up[:, m % 4]
                w = lambda t: vcol("hy_conv_w", 24 * t + m)
                chain(ts(u, src[:, :, 0:L], w(0), vcol("hy_conv_b", m), ALU.mult, ALU.add))
                chain(stt(u, src[:, :, 1:L + 1], w(1), u, ALU.mult, ALU.add))
                stt(u, src[:, :, 2:L + 2], w(2), u, ALU.mult, ALU.add).then_inc(s("conv_ready"), 1)
                if m in (7, 15):
                    ada_at(f"w_in{m // 4}")

            def products(n):
                dve.wait_ge(s("zf_mm"), n + 1)
                for w, (ka, kb) in enumerate(((0, 1), (1, 2))):
                    if n:
                        dve.wait_ge(s("yspec"), 2 * n - 1 + w)
                    for dst, first, kk in ((prods[w][0], 0, ka), (prods[w][1], 2, kb)):
                        for h in range(2):
                            last = tt(dst[:, h * 512:h * 512 + 512], bank[first + h][:],
                                      spec[:, kk, n // 2, h * 512:h * 512 + 512], ALU.mult)
                        last.then_inc(s("prods"), 1)

            def gated(n):
                dve.wait_ge(s("zi_mm"), n + 1)
                dve.wait_ge(s("skip_ready"), n + 1)
                x_o = 8 * (n // 2 + 1)
                for h in range(2):
                    sk = vskip[n % 2].rearrange("p (k t) -> p k t", k=KD)[:, 4 * h:4 * h + 4]
                    chain(tt(sk, sk, psum_tok(4 + h, 4), ALU.add))
                    last = tt(uT[:, 4 * h:4 * h + 4, n % G], sk, uT[:, x_o + 4 * h:x_o + 4 * h + 4, n % G], ALU.mult)
                last.then_inc(s("z_ready"), 1)

            ada_at("w_in5")
            dve.wait_ge(s("conv_ready"), 24)
            products(0)
            ada_at("conv0")
            products(1)
            gated(0)
            products(2)
            gated(1)
            ada_at("conv1")
            products(3)
            gated(2)
            ada_at("conv2")
            gated(3)
            residual(0, g1(0))
            moe(0)
            if layers > 1:
                norm(2)
                dve.wait_ge(s("gk1_mm"), 1)
                v.tensor_copy(gk1[0:32, :], bank[4][0:32, 0:NT]).then_inc(s("gk1_ready"), 1)

                fl = lambda x: x.rearrange("p h g t -> p (h g t)")

                def cumulate(d):
                    if d:
                        dve.wait_ge(s("scores_mm"), 2)
                    v.memset(reset[:], 1.0).then_inc(s("reset"), 1)
                    dve.wait_ge(s("reset"), 2 * d + 1)
                    e = reset.rearrange("p (n t) -> p n t", t=CH)
                    v.memset(e[:, :, 0:1] if d == 0 else e[:, :, CH - 1:CH], 0.0).then_inc(s("reset"), 1)
                    dve.wait_ge(s("gate_ln"), d + 1)
                    chain(stt(gx[:], gx[:], 0.0, gt[:], ALU.min, ALU.subtract))
                    dve.wait_ge(s("reset"), 2 * d + 2)
                    if d == 0:
                        v.tensor_tensor_scan(gt[:], reset[:], gx[:], 0.0, ALU.mult, ALU.add).then_inc(s("gate_cum"), 1)
                    else:
                        v.tensor_tensor_scan(gt[:, ::-1], reset[:, ::-1], gx[:, ::-1], 0.0, ALU.mult, ALU.add) \
                            .then_inc(s("gate_cum"), 1)
                    dve.wait_ge(s("gate_cum"), 2 * d + 1)
                    b16 = gt.rearrange("p (n t) -> p n t", t=CH)
                    bl = b16[:, :, CH - 1:CH] if d == 0 else b16[:, :, 0:1]
                    tt(gx.rearrange("p (n t) -> p n t", t=CH), bl.broadcast_to([P, 16, CH]), b16, ALU.subtract) \
                        .then_inc(s("gate_cum"), 1)

                def keys(d):
                    dve.wait_ge(s("qk_ready"), 4)
                    dve.wait_ge(s("k_exp"), 2 * d + 1)
                    tt(fl(ke), fl(kT), e2[:], ALU.mult).then_inc(s("qke_ready"), 1)
                    dve.wait_ge(s("k_exp"), 2 * d + 2)
                    if d:
                        dve.wait_ge(s("kd_tr"), 2)
                    tt(fl(kdT), fl(kT), gx[:], ALU.mult).then_inc(s("kd_ready"), 1)

                def queries(d):
                    dve.wait_ge(s("q_exp"), d + 1)
                    if d:
                        dve.wait_ge(s("o_mm"), 1)
                    tt(fl(qe), fl(qT), e1[:], ALU.mult).then_inc(s("qke_ready"), 1)

                def scores(d):
                    dve.wait_ge(s("sc_clear"), 1)
                    if d:
                        dve.wait_ge(s("intra_mm"), 1)
                    dve.wait_ge(s("mask_ready"), 1)
                    for g in range(G):
                        dve.wait_ge(s("scores_mm"), 2 * d + g + 1)
                        if d:
                            v.memset(sc[:, g], 0.0).then_inc(s("sc_clear"), 1)
                            dve.wait_ge(s("sc_clear"), 2 + g)
                        v.copy_predicated(sc[:, g], mask[:, d, :].unsqueeze(1).broadcast_to([P, HEADS, P]),
                                          psum_tok(4 + g, 4)).then_inc(s("sc_ready"), 1)

                e4 = e1.rearrange("p (h g t) -> p h g t", h=HEADS, g=G)
                pu = lambda h: bank[4 + h // 2][:, (h % 2) * DV:(h % 2) * DV + DV]

                def states(d):
                    dec = lambda h, g, c: e4[:, h, g, c * CH + CH - 1:c * CH + CH] if d == 0 else \
                        e4[:, h, g, c * CH:c * CH + 1]
                    dve.wait_ge(s("s0_loaded"), 32)
                    if d == 1:
                        dve.wait_ge(s("state_stored"), 16)
                        dve.wait_ge(s("o_mm"), 1)
                    dve.wait_ge(s("upd_mm"), 3 * d + 1)
                    for h in range(HEADS):
                        last = stt(s1l[:, h], s0[:, d, h], dec(h, 1, d), pu(h), ALU.mult, ALU.add)
                    last.then_inc(s("upd_read"), 1)
                    dve.wait_ge(s("upd_mm"), 3 * d + 2)
                    for b in range(2):
                        last = v.tensor_copy(s1c[:, 2 * b:2 * b + 2], bank[4 + b][:].rearrange("p (h n) -> p h n", h=2))
                    last.then_inc(s("upd_read"), 1)
                    dve.wait_ge(s("upd_read"), 3 * d + 2)
                    dve.wait_ge(s("upd_mm"), 3 * d + 3)
                    for h in range(HEADS):
                        last = stt(s2[:, h], s1c[:, h], dec(h, 0, 1 - d), pu(h), ALU.mult, ALU.add)
                    last.then_inc(s("upd_read"), 1)

                ada_at("queries")
                cumulate(0)
                keys(0)
                queries(0)
                v.memset(sc[:], 0.0).then_inc(s("sc_clear"), 1)
                ada_at("values")
                scores(0)
                cumulate(1)
                states(0)
                keys(1)
                queries(1)
                ada_at("between")
                scores(1)
                states(1)
                dve.wait_ge(s("g_ready"), 1)
                dve.wait_ge(s("o_mm"), 2)
                dve.wait_ge(s("upd_read"), 6)
                for m in range(KD):
                    dve.wait_ge(s("osq_ready"), m // 2 + 1)
                    last = stt(oT[:, m].rearrange("p g t -> p (g t)"), half(m), vcol("gla_norm_g", m % 2), gT[:, m],
                               ALU.mult, ALU.mult)
                chain(last)
                ada_at("heads")
                for m in range(KD):
                    dve.wait_ge(s("ors_ready"), m // 4 + 1)
                    o = oT[:, m].rearrange("p g t -> p (g t)")
                    tt(o, o, ors[:, m // 2], ALU.mult).then_inc(s("o_ready"), 1)
                residual(1, g1(1))
                moe(1)
            if layers > 2:
                norm(4)
                ada_at("fnet")
                residual(2, g1(2))
                moe(2)
            if layers > 3:
                norm(6)
                gs = rtv(200, KD, G)
                chain(tt(gs, mod[:, 3, 16:24], vcol("pool_scale", 0, KD).unsqueeze(2).broadcast_to([P, KD, G]), ALU.mult))
                residual(3, lambda m, g: gs[:, m, g:g + 1])
                moe(3)
            dve.wait_ge(s("rstd_tr"), 1)
            chain(v.tensor_copy(rstd_col[:], bank[7][:, 0:NT].rearrange("p (g t) -> p g t", g=G)[:, :, 0]))
            dve.wait_ge(s("cm_loaded"), 16 * 7)
            for g in range(G):
                for h in range(2):
                    dve.wait_ge(s("out_tr"), 2 * g + h + 1)
                    stt(xout[:, g, h * 512:h * 512 + 512], bank[4 * (1 - g) + h][:], rstd_col[:, g:g + 1],
                        final_g[:, h * 512:h * 512 + 512], ALU.mult, ALU.mult).then_inc(s("out_rows"), 1)

        @block.gpsimd
        def _(pool):
            v = nc.gpsimd
            pool.dma_start(fsmall[0:HY_EMB, 0, :], a["c_pos"]).then_inc(s("filter_loaded"), 16)
            pool.dma_start(fsmall[0:HY_EMB, 1, 0:HY_HID], a["hy_f_w1"][0]).then_inc(s("filter_loaded"), 16)
            pool.dma_start(fsmall[0:HY_HID, 2, 0:HY_HID], a["hy_f_w2"][0]).then_inc(s("filter_loaded"), 16)
            pool.dma_start(upper, a["c_upper"]).then_inc(s("masks_loaded"), 16)
            pool.dma_start(mask32.rearrange("p d t -> p (d t)"), a["c_mask"]).then_inc(s("masks_loaded"), 16)

            def load_router(i):
                pool.dma_start(rw[:, :, 0:4], a["moe_w_rg"][i].rearrange("(k p) n -> p k n", p=P)) \
                    .then_inc(s("rw_loaded"), 16)
                pool.dma_start(rw[:, :, 4:20], a["moe_w_re"][i].rearrange("(k p) n -> p k n", p=P)) \
                    .then_inc(s("rw_loaded"), 16)

            def add_squares(n):
                for k in range(1, KD - 1):
                    pool.wait_ge(s("squares"), KD * n + k + 1)
                    if k > 1:
                        pool.wait_ge(s("squares_added"), (KD - 2) * (n - 1) + k - 1)
                    v.tensor_tensor(hT[:, 0], hT[:, 0], hT[:, k], ALU.add).then_inc(s("squares_added"), 1)

            load_router(0)
            pool.wait_ge(s("conv_ready"), 24)
            for n in range(4):
                if n > 1:
                    pool.wait_ge(s("z_ready"), n - 1)
                coef = vcol("hy_skip", 8 * (n // 2), KD).unsqueeze(2).broadcast_to([P, KD, L])
                v.tensor_tensor(vskip[n % 2].rearrange("p (k t) -> p k t", k=KD), uT[:, 0:KD, n % G], coef, ALU.mult) \
                    .then_inc(s("skip_ready"), 1)
                for w, op in enumerate((ALU.subtract, ALU.add)):
                    pool.wait_ge(s("prods"), 4 * n + 2 * w + 2)
                    if n:
                        pool.wait_ge(s("zi_mm"), n)
                    v.tensor_tensor(ysp[:, w], prods[w][0], prods[w][1], op).then_inc(s("yspec"), 1)
            add_squares(1)
            if layers > 1:
                pool.wait_ge(s("x_added"), KD)
                pool.wait_ge(s("y_mm"), primed(2))
                v.memset(wg2[0:32], 0.0).then_inc(s("wg2_clear"), 1)
                pool.wait_ge(s("wg2_clear"), 1)
                for d in range(2):
                    pool.dma_start(wg1[:, :, 16 * d:16 * d + 16], a["gla_w_gk1"][0, d].rearrange("(k p) r -> p k r", p=P)) \
                        .then_inc(s("cm_loaded"), 16)
                    pool.dma_start(wg2[16 * d:16 * d + 16, d, :], a["gla_w_gk2"][0, d]).then_inc(s("cm_loaded"), 16)
                    pool.dma_start(s0[:, d], a["state_gla"][0, 0, d].rearrange("h k v -> k h v")) \
                        .then_inc(s("s0_loaded"), 16)
                pool.wait_ge(s("logits_mm"), 1)
                load_router(1)
                add_squares(2)
                for d in range(2):
                    pool.wait_ge(s("upd_read"), 3 * d + 3)
                    pool.dma_start(a["new_state"][0, 0, d].rearrange("h k v -> k h v"), s2[:]) \
                        .then_inc(s("state_stored"), 16)
                add_squares(3)
            if layers > 2:
                pool.wait_ge(s("x_added"), KD * 3)
                pool.dma_start(cm[:], a["c_fnet"]).then_inc(s("cm_loaded"), 16)
                pool.wait_ge(s("logits_mm"), 2)
                load_router(2)
                add_squares(4)
                add_squares(5)
            if layers > 3:
                pool.wait_ge(s("x_added"), KD * 5)
                pool.dma_start(cm[:, 0:1024], a["c_pool"]).then_inc(s("cm_loaded"), 16)
                pool.wait_ge(s("logits_mm"), 3)
                load_router(3)
                add_squares(6)
                add_squares(7)
            pool.wait_ge(s("x_added"), KD * (2 * layers - 1))
            pool.dma_start(final_g, a["final_g"].unsqueeze(0).broadcast_to([P, D])).then_inc(s("cm_loaded"), 16)
            add_squares(2 * layers)


INPUTS = ['x_prompt', 'x_sample', 'state_gla', 'c', 'c_ctx', 'w_ada', 'b_ada', 'norm_g',
          'hy_w_in', 'hy_b_in', 'hy_conv_w', 'hy_conv_b', 'hy_f_w1', 'hy_f_b1', 'hy_f_freq', 'hy_f_w2', 'hy_f_b2',
          'hy_f_w3', 'hy_skip', 'hy_w_out', 'hy_b_out',
          'gla_w_q', 'gla_w_k', 'gla_w_v', 'gla_w_g', 'gla_w_gk1', 'gla_w_gk2', 'gla_b_gk', 'gla_norm_g', 'gla_w_o',
          'fn_w_out', 'fn_b_out', 'pool_w', 'pool_b', 'pool_scale',
          'moe_w_rg', 'moe_w_re', 'moe_w1', 'moe_w3', 'moe_w2', 'final_g']


def declare(nc, arrays):
    aps = {n: nc.dram_tensor(f"in_{n}", x.shape, mybir.dt.from_np(x.dtype), kind="ExternalInput").ap()
           for n, x in arrays.items()}
    for n, shape in (("y_prompt", (1, L, D)), ("y_sample", (1, L, D)), ("new_state", (1, 1, 2, HEADS, DK, DV))):
        aps[n] = nc.dram_tensor(f"out_{n}", shape, F32, kind="ExternalOutput").ap()
    return aps


def kernel(**inputs):
    import concourse.bacc as bacc
    from concourse.bass_utils import run_bass_kernel_spmd

    nc = bacc.Bacc("TRN2", target_bir_lowering=False, num_devices=1)
    arrays = {n: np.ascontiguousarray(inputs[n]) for n in INPUTS}
    arrays.update({f"c_{n}": x for n, x in constants().items()})
    build(nc, declare(nc, arrays))
    r = run_bass_kernel_spmd(nc, [{f"in_{n}": x for n, x in arrays.items()}], core_ids=[0])
    got = r.results[0]
    return got["out_y_prompt"], got["out_y_sample"], got["out_new_state"]
```
